# Optimizing a Trainium2 kernel written in Bass

```python
import math, functools
import jax, jax.numpy as jnp
from jax import lax
import numpy as np

D_MODEL = 1024
BATCH = 1
SEQ = 256
DEPTH = 1
DEC_BATCH = 1
DEC_SEQ = 1024
PAST_LEN = 256

GRID_W = 64
D_MIX = D_MODEL
D_ATTN = D_MIX // 2
D_HYENA = D_MIX - D_ATTN
HEAD_DIM = 64
N_HEADS = D_ATTN // HEAD_DIM
WIN_ROWS = 8
WIN_COLS = 16
Q_COLS = 16
K_COLS = Q_COLS + WIN_COLS
Q_BLOCK = 128
HYENA_ORDER = 2
SHORT_CONV = 3
FILTER_EMB = 33
FILTER_BANDS = (FILTER_EMB - 1) // 2
FILTER_HIDDEN = 64
DECAY_TARGET = 1e-2
SHORT_DECAY_PCT = 0.3
LONG_DECAY_PCT = 1.5
MOD_SHIFT = 0.05
N_EXPERTS = 16
EC_FACTOR = 2
EXPERT_FF = 2816
N_MOD = 6
EPS = 1e-6
NEG_INF = -1e30

kernel_name = 'hybrid_natten_hyena_ec_diffusion_step'

def rmsnorm(x, g):
    xf = x.astype(jnp.float32)
    y = xf * lax.rsqrt(jnp.mean(xf * xf, axis=-1, keepdims=True) + EPS)
    return y.astype(x.dtype) * g

def ada_mod(cond, w_ada, b_ada):
    m = jax.nn.silu(cond) @ w_ada + b_ada
    return jnp.split(m, N_MOD, axis=-1)

def to_heads(a):
    b, t, _ = a.shape
    return a.reshape(b, t, N_HEADS, HEAD_DIM).transpose(0, 2, 1, 3)

def context_attention(q, k, v):
    b, h, t, dh = q.shape
    nb = t // Q_BLOCK
    qb = q.reshape(b, h, nb, Q_BLOCK, dh).transpose(2, 0, 1, 3, 4)

    def block(q_i):
        s = jnp.einsum('bhqd,bhtd->bhqt', q_i, k).astype(jnp.float32)
        p = jax.nn.softmax(s, axis=-1).astype(v.dtype)
        return jnp.einsum('bhqt,bhtd->bhqd', p, v)

    o = lax.map(block, qb)
    return o.transpose(1, 2, 0, 3, 4).reshape(b, h, t, dh)

def latent_neighbourhood_attention(q, k, v, k_ctx, v_ctx, rpb):
    b, h, l, dh = q.shape
    rows = l // GRID_W
    wr = min(WIN_ROWS, rows)
    ncb = GRID_W // Q_COLS
    n_win = wr * K_COLS
    row_start = jnp.clip(jnp.arange(rows) - wr // 2, 0, rows - wr)
    q_col = jnp.arange(GRID_W).reshape(ncb, Q_COLS)
    win_start = jnp.clip(q_col - WIN_COLS // 2, 0, GRID_W - WIN_COLS)
    blk_start = jnp.clip(jnp.arange(ncb) * Q_COLS - WIN_COLS // 2, 0, GRID_W - K_COLS)
    key_col = blk_start[:, None] + jnp.arange(K_COLS)[None, :]
    kc = key_col[:, None, :]
    col_ok = (kc >= win_start[..., None]) & (kc < win_start[..., None] + WIN_COLS)
    dcol = jnp.clip(kc - q_col[..., None], -(WIN_COLS - 1), WIN_COLS - 1) + (WIN_COLS - 1)
    qg = q.reshape(b, h, rows, ncb, Q_COLS, dh)
    kg = k.reshape(b, h, rows, GRID_W, dh)
    vg = v.reshape(b, h, rows, GRID_W, dh)

    def one_row(r):
        rs = row_start[r]
        q_r = lax.dynamic_index_in_dim(qg, r, axis=2, keepdims=False)
        k_r = jnp.take(lax.dynamic_slice_in_dim(kg, rs, wr, axis=2), key_col, axis=3)
        v_r = jnp.take(lax.dynamic_slice_in_dim(vg, rs, wr, axis=2), key_col, axis=3)
        drow = rs + jnp.arange(wr) - r + (WIN_ROWS - 1)
        bias = rpb[:, drow[None, None, :, None], dcol[:, :, None, :]]
        s_win = jnp.einsum('bhjqd,bhijkd->bhjqik', q_r, k_r).astype(jnp.float32) + bias.astype(jnp.float32)
        s_win = jnp.where(col_ok[:, :, None, :], s_win, NEG_INF).reshape(b, h, ncb, Q_COLS, n_win)
        s_ctx = jnp.einsum('bhjqd,bhtd->bhjqt', q_r, k_ctx).astype(jnp.float32)
        p = jax.nn.softmax(jnp.concatenate([s_win, s_ctx], axis=-1), axis=-1).astype(v.dtype)
        p_win = p[..., :n_win].reshape(b, h, ncb, Q_COLS, wr, K_COLS)
        return (jnp.einsum('bhjqik,bhijkd->bhjqd', p_win, v_r)
                + jnp.einsum('bhjqt,bhtd->bhjqd', p[..., n_win:], v_ctx))

    o = lax.map(one_row, jnp.arange(rows))
    return o.transpose(1, 2, 0, 3, 4, 5).reshape(b, h, l, dh)

def implicit_filter_fft(length, w1, b1, w2, b2, w3, freq):
    f32 = jnp.float32
    t = jnp.linspace(0.0, 1.0, length, dtype=f32)[:, None]
    w = (2.0 * math.pi / length) * jnp.arange(length, dtype=f32)[:, None]
    bands = jnp.linspace(1e-4, FILTER_BANDS - 1, FILTER_BANDS, dtype=f32)[None, :]
    z = jnp.concatenate([t, jnp.cos(bands * w), -jnp.sin(bands * w)], axis=-1)
    fr = freq.astype(f32)
    hid = jnp.sin(fr * (z @ w1.astype(f32) + b1.astype(f32)))
    hid = jnp.sin(fr * (hid @ w2.astype(f32) + b2.astype(f32)))
    filt = (hid @ w3.astype(f32)).reshape(length, 2, HYENA_ORDER, D_HYENA)
    deltas = jnp.abs(jnp.linspace(math.log(DECAY_TARGET) / LONG_DECAY_PCT,
                                  math.log(DECAY_TARGET) / SHORT_DECAY_PCT, D_HYENA, dtype=f32))
    window = jnp.exp(-t * deltas) + MOD_SHIFT
    filt = filt * window[:, None, None, :]
    fwd, bwd = filt[:, 0], filt[:, 1]
    two_sided = jnp.concatenate([fwd, jnp.zeros((1, HYENA_ORDER, D_HYENA), f32), bwd[1:][::-1]], axis=0)
    two_sided = two_sided / jnp.sum(jnp.abs(two_sided), axis=0, keepdims=True)
    return jnp.fft.rfft(two_sided, axis=0)

def short_conv(u, w, b):
    up = jnp.pad(u, ((0, 0), (1, 1), (0, 0)))
    return up[:, :-2] * w[0] + up[:, 1:-1] * w[1] + up[:, 2:] * w[2] + b

def long_conv(u, k_f, bias):
    length = u.shape[1]
    uf = u.astype(jnp.float32)
    y = jnp.fft.irfft(jnp.fft.rfft(uf, n=2 * length, axis=1) * k_f[None], n=2 * length, axis=1)[:, :length]
    return y + uf * bias.astype(jnp.float32)

def hyena_mixer(u, conv_w, conv_b, k_f, hy_bias):
    uc = short_conv(u, conv_w, conv_b)
    v, x1, x2 = jnp.split(uc, 3, axis=-1)
    z = x1.astype(jnp.float32) * long_conv(v, k_f[:, 0], hy_bias[0])
    y = x2.astype(jnp.float32) * long_conv(z, k_f[:, 1], hy_bias[1])
    return y.astype(u.dtype)

def expert_choice_ffn(x, w_router, w1, w3, w2):
    b, t, d = x.shape
    xf = x.reshape(b * t, d)
    n = b * t
    cap = EC_FACTOR * n // N_EXPERTS
    aff = jax.nn.softmax((xf @ w_router).astype(jnp.float32), axis=-1)
    top_aff, top_idx = lax.top_k(aff.T, cap)
    xe = xf[top_idx]
    hid = jax.nn.silu(jnp.einsum('ecd,edf->ecf', xe, w1)) * jnp.einsum('ecd,edf->ecf', xe, w3)
    ye = jnp.einsum('ecf,efd->ecd', hid, w2) * top_aff[..., None].astype(xf.dtype)
    out = jnp.zeros_like(xf).at[top_idx.reshape(-1)].add(ye.reshape(-1, d))
    return out.reshape(b, t, d)

def trunk_layer(x, cond, attend, k_f, norm1_g, norm2_g, w_ada, b_ada, w_in, w_out, out_g_attn, out_g_hyena,
                conv_w, conv_b, hy_bias, w_router, w1, w3, w2):
    b, t, _ = x.shape
    sh1, sc1, g1, sh2, sc2, g2 = ada_mod(cond, w_ada, b_ada)
    h = rmsnorm(x, norm1_g) * (1.0 + sc1) + sh1
    proj = h @ w_in
    q, k, v, hy = jnp.split(proj, [D_ATTN, 2 * D_ATTN, 3 * D_ATTN], axis=-1)
    k = to_heads(k)
    v = to_heads(v)
    a = attend(to_heads(q) * (HEAD_DIM ** -0.5), k, v)
    a = a.transpose(0, 2, 1, 3).reshape(b, t, D_ATTN)
    y_h = hyena_mixer(hy, conv_w, conv_b, k_f, hy_bias)
    mix = jnp.concatenate([rmsnorm(a, out_g_attn), rmsnorm(y_h, out_g_hyena)], axis=-1) @ w_out
    x = x + g1 * mix
    h2 = rmsnorm(x, norm2_g) * (1.0 + sc2) + sh2
    x = x + g2 * expert_choice_ffn(h2, w_router, w1, w3, w2)
    return x, k, v

def setup_inputs(seed: int = 0) -> dict:
    key = jax.random.key(seed)
    ks = jax.random.split(key, 32)
    d = D_MODEL
    c3 = 3 * D_HYENA

    def nrm(k, shape, scale):
        return scale * jax.random.normal(k, shape, jnp.float32)

    return {
        'x_prompt': nrm(ks[0], (BATCH, SEQ, d), 1.0),
        'x_sample': nrm(ks[1], (DEC_BATCH, DEC_SEQ, d), 1.0),
        'cache_k': nrm(ks[2], (DEC_BATCH, DEPTH, N_HEADS, PAST_LEN, HEAD_DIM), 1.0),
        'cache_v': nrm(ks[3], (DEC_BATCH, DEPTH, N_HEADS, PAST_LEN, HEAD_DIM), 1.0),
        'c': nrm(ks[4], (DEC_BATCH, d), 1.0),
        'c_ctx': nrm(ks[5], (d,), 1.0),
        'norm1_g': 1.0 + nrm(ks[6], (DEPTH, d), 0.01),
        'norm2_g': 1.0 + nrm(ks[7], (DEPTH, d), 0.01),
        'w_ada': nrm(ks[8], (DEPTH, d, N_MOD * d), 0.5 * d ** -0.5),
        'b_ada': nrm(ks[9], (DEPTH, N_MOD * d), 0.02),
        'w_in': nrm(ks[10], (DEPTH, d, 3 * D_ATTN + c3), d ** -0.5),
        'w_out': nrm(ks[11], (DEPTH, D_MIX, d), D_MIX ** -0.5),
        'out_g_attn': 1.0 + nrm(ks[12], (DEPTH, D_ATTN), 0.01),
        'out_g_hyena': 1.0 + nrm(ks[13], (DEPTH, D_HYENA), 0.01),
        'rpb': nrm(ks[14], (DEPTH, N_HEADS, 2 * WIN_ROWS - 1, 2 * WIN_COLS - 1), 0.5),
        'conv_w': nrm(ks[15], (DEPTH, SHORT_CONV, c3), SHORT_CONV ** -0.5),
        'conv_b': nrm(ks[16], (DEPTH, c3), 0.02),
        'filt_w1': nrm(ks[17], (DEPTH, FILTER_EMB, FILTER_HIDDEN), FILTER_EMB ** -0.5),
        'filt_b1': nrm(ks[18], (DEPTH, FILTER_HIDDEN), 0.5),
        'filt_w2': nrm(ks[19], (DEPTH, FILTER_HIDDEN, FILTER_HIDDEN), FILTER_HIDDEN ** -0.5),
        'filt_b2': nrm(ks[20], (DEPTH, FILTER_HIDDEN), 0.5),
        'filt_w3': nrm(ks[21], (DEPTH, FILTER_HIDDEN, 2 * HYENA_ORDER * D_HYENA), FILTER_HIDDEN ** -0.5),
        'filt_freq': 1.0 + nrm(ks[22], (DEPTH, FILTER_HIDDEN), 0.01),
        'hyena_bias': nrm(ks[23], (DEPTH, HYENA_ORDER, D_HYENA), 0.5),
        'w_router': nrm(ks[24], (DEPTH, d, N_EXPERTS), d ** -0.5),
        'w1': nrm(ks[25], (DEPTH, N_EXPERTS, d, EXPERT_FF), d ** -0.5),
        'w3': nrm(ks[26], (DEPTH, N_EXPERTS, d, EXPERT_FF), d ** -0.5),
        'w2': nrm(ks[27], (DEPTH, N_EXPERTS, EXPERT_FF, d), EXPERT_FF ** -0.5),
        'final_g': 1.0 + nrm(ks[28], (d,), 0.01),
    }

def reference(x_prompt, x_sample, cache_k, cache_v, c, c_ctx, norm1_g, norm2_g, w_ada, b_ada, w_in, w_out,
              out_g_attn, out_g_hyena, rpb, conv_w, conv_b, filt_w1, filt_b1, filt_w2, filt_b2, filt_w3,
              filt_freq, hyena_bias, w_router, w1, w3, w2, final_g):
    cond_ctx = c_ctx[None, None, :]
    cond_lat = c[:, None, :]
    xp, xs = x_prompt, x_sample
    keys, vals = [], []
    for l in range(DEPTH):
        shared = (norm1_g[l], norm2_g[l], w_ada[l], b_ada[l], w_in[l], w_out[l], out_g_attn[l], out_g_hyena[l],
                  conv_w[l], conv_b[l], hyena_bias[l], w_router[l], w1[l], w3[l], w2[l])
        filt = (filt_w1[l], filt_b1[l], filt_w2[l], filt_b2[l], filt_w3[l], filt_freq[l])
        kf_ctx = implicit_filter_fft(xp.shape[1], *filt)
        kf_lat = implicit_filter_fft(xs.shape[1], *filt)
        xp, k_ctx, v_ctx = trunk_layer(xp, cond_ctx, context_attention, kf_ctx, *shared)
        keys.append(k_ctx)
        vals.append(v_ctx)
        attend = functools.partial(latent_neighbourhood_attention, k_ctx=cache_k[:, l], v_ctx=cache_v[:, l],
                                   rpb=rpb[l])
        xs, _, _ = trunk_layer(xs, cond_lat, attend, kf_lat, *shared)
    y_prompt = rmsnorm(xp, final_g)
    y_sample = rmsnorm(xs, final_g)
    state_k = jnp.stack(keys, axis=1)
    state_v = jnp.stack(vals, axis=1)
    return (y_prompt, y_sample, state_k, state_v)


_drawn_inputs = setup_inputs


def setup_inputs(seed=0):
    import zlib

    import numpy as np

    out = dict(_drawn_inputs(seed))
    spreads = {}
    factors = {'norm1_g': 5.763,
     'norm2_g': 8.0,
     'out_g_attn': 8.0,
     'out_g_hyena': 8.0,
     'conv_b': 5.477,
     'filt_freq': 8.0,
     'final_g': 5.471}
    for name, (base, spread) in spreads.items():
        noise = np.random.default_rng([zlib.crc32(name.encode()), seed]).standard_normal(out[name].shape)
        drawn = base * np.exp(spread * noise) if base else spread * noise
        out[name] = __import__('jax').numpy.asarray(drawn.astype(out[name].dtype))
    for name, factor in factors.items():
        out[name] = (out[name] * factor).astype(out[name].dtype)
    return out
```

```python
from contextlib import ExitStack

import numpy as np
import concourse.bass as bass
from concourse import mybir

F32 = mybir.dt.float32
F32R = mybir.dt.float32r
U32 = mybir.dt.uint32
ALU = mybir.AluOpType
ACT = mybir.ActivationFunctionType
AX = mybir.AxisListType

D = 1024
KT = D // 128
TP, TS = 256, 1024
T = TP + TS
NTT = T // 128
DA = DH = 512
NH, HD = 8, 64
GW, WR, WC = 64, 8, 16
QC, KC = 16, 32
KR = 12
NWIN = KR * KC
NCTX = 256
NE, FF = 16, 2816
FT = FF // 128
CAP_S, CAP_P = 2 * TS // NE, 2 * TP // NE
CAP = CAP_S + CAP_P
EPS = 1e-6
NEG = -1e30
CH = 1024
NF = 20


class Phase:

    def __init__(self, nc, name):
        self.nc, self.name, self.stack, self.sems = nc, name, ExitStack(), []

    def __enter__(self):
        return self

    def __exit__(self, *exc):
        self.stack.__exit__(*exc)
        self.nc.clear_and_free_semaphores(self.sems)
        self.nc.all_engine_barrier()

    def sb(self, name, shape, dt=F32):
        return self.stack.enter_context(self.nc.sbuf_tensor(f"{self.name}_{name}", shape, dt))

    def ps(self, name, shape, dt=F32):
        return self.stack.enter_context(self.nc.psum_tensor(f"{self.name}_{name}", shape, dt))

    def sem(self, name):
        self.sems.append(self.nc.alloc_semaphore(f"{self.name}_{name}"))
        return self.sems[-1]

    def block(self):
        return self.stack.enter_context(self.nc.Block())


class Chain:

    def __init__(self, eng, sem, base=0):
        self.eng, self.sem, self.n, self.base = eng, sem, 0, base

    def __call__(self, ins):
        ins.then_inc(self.sem, 1)
        self.n += 1
        self.eng.wait_ge(self.sem, self.base + self.n)


class Stream:

    def __init__(self, ph, nr, ns, used, per=1):
        self.nr, self.ns, self.used, self.per = nr, ns, used, per
        self.raw = ph.sb("raw", [128, nr, CH])
        self.hi = ph.sb("hi", [128, ns, CH], F32R)
        self.lo = ph.sb("lo", [128, ns, CH], F32R)
        self.landed = [ph.sem(f"raw_landed{i}") for i in range(nr)]
        self.hi_done = ph.sem("hi_done")
        self.lo_done = ph.sem("lo_done")

    def start_pe(self, pe):
        pe.sem_inc(self.used, self.ns * self.per)

    def start_dve(self, dve):
        dve.sem_inc(self.lo_done, self.nr)

    def load(self, sp, laps, base, c, src):
        sp.wait_ge(self.lo_done, base + c + 1)
        sp.dma_start(self.raw[:, c % self.nr, :], src).then_inc(self.landed[c % self.nr], 16)

    def split_hi(self, act, laps, base, c):
        act.wait_ge(self.landed[c % self.nr], (laps + c // self.nr) * 16 + 16)
        act.wait_ge(self.used, (base + c + 1) * self.per)
        act.activation(self.hi[:, c % self.ns, :], self.raw[:, c % self.nr, :], ACT.Copy).then_inc(self.hi_done, 1)

    def split_lo(self, dve, base, c):
        dve.wait_ge(self.hi_done, base + c + 1)
        dve.tensor_tensor(self.lo[:, c % self.ns, :], self.raw[:, c % self.nr, :],
                          self.hi[:, c % self.ns, :].bitcast(F32), ALU.subtract).then_inc(self.lo_done, 1)

    def ready(self, pe, base, c):
        pe.wait_ge(self.lo_done, base + c + 1 + self.nr)

    def tile(self, part, c, j, n=128):
        return part[:, c % self.ns, j * n:(j + 1) * n]


def modulation(nc, a, g):
    NBLK = 12
    with Phase(nc, "ada") as ph:
        w = ph.sb("w", [128, 2, KT, 512])
        cond = ph.sb("cond", [128, KT, 2])
        sc = ph.sb("sc", [128, KT, 2])
        bada = ph.sb("bada", [128, 48])
        modr = ph.sb("modr", [48, 2, 128])
        gmodr = ph.sb("gmodr", [16, 2, 128])
        acc = ph.ps("acc", [128, 48, 2])
        accr = ph.ps("accr", [48, 2, 128])
        accg = ph.ps("accg", [16, 2, 128])
        s_w = [ph.sem(f"w_landed{i}") for i in range(2)]
        s_small = ph.sem("small_landed")
        s_silu, s_mm, s_mod = ph.sem("silu"), ph.sem("mm"), ph.sem("mod")
        s_tr, s_modr, s_out = ph.sem("tr"), ph.sem("modr"), ph.sem("out")
        block = ph.block()

        @block.sync
        def _(sp):
            sp.dma_start(cond[:], a["cond"]).then_inc(s_small, 16)
            sp.dma_start(bada[:], a["bada"]).then_inc(s_small, 16)
            sp.dma_start(g["gains"][:], a["gains"]).then_inc(s_small, 16)
            sp.dma_start(g["ident"][:], a["ident"]).then_inc(s_small, 16)
            for n in range(NBLK):
                if n >= 2:
                    sp.wait_ge(s_mm, n - 1)
                sp.dma_start(w[:, n % 2], a["w_ada"][:, :, n * 512:(n + 1) * 512]).then_inc(s_w[n % 2], 16)
            sp.wait_ge(s_modr, 1)
            for c in range(2):
                sp.dma_start(g["MODR"][c].rearrange("(f p) -> f p", p=128), modr[:, c, :]).then_inc(s_out, 16)
                sp.dma_start(g["GMODR"][c].rearrange("(f p) -> f p", p=128), gmodr[:, c, :]).then_inc(s_out, 16)
            sp.wait_ge(s_out, 64)

        @block.scalar
        def _(act):
            act.wait_ge(s_small, 64)
            act.activation(sc[:], cond[:], ACT.Silu).then_inc(s_silu, 1)

        @block.tensor
        def _(pe):
            pe.wait_ge(s_silu, 1)
            for n in range(NBLK):
                pe.wait_ge(s_w[n % 2], 16 * (n // 2 + 1))
                for f in range(4):
                    for k in range(KT):
                        mm = pe.matmul(acc[:, 4 * n + f, :], w[:, n % 2, k, f * 128:(f + 1) * 128], sc[:, k, :],
                                       start=(k == 0), stop=(k == KT - 1))
                mm.then_inc(s_mm, 1)
            pe.wait_ge(s_mod, 2)
            for c in range(2):
                pe.transpose(accr[:, c, :], g["mod"][:, :, c], g["ident"][:])
                tr = pe.transpose(accg[:, c, :], g["gmod"][:, c, :], g["ident"][:])
            tr.then_inc(s_tr, 1)

        @block.vector
        def _(dve):
            mod = g["mod"]
            dve.memset(g["ones"][:], 1.0)
            dve.wait_ge(s_mm, NBLK)
            for c in range(2):
                ins = dve.tensor_tensor(mod[:, :, c], acc[:, :, c], bada[:], ALU.add)
            ins.then_inc(s_mod, 1)
            dve.wait_ge(s_mod, 1)
            for c in range(2):
                for j, (sc0, gn) in enumerate(((8, 0), (32, 8))):
                    ins = dve.scalar_tensor_tensor(g["gmod"][:, c, j * 8:(j + 1) * 8], mod[:, sc0:sc0 + 8, c], 1.0,
                                                   g["gains"][:, gn:gn + 8], ALU.add, ALU.mult)
            ins.then_inc(s_mod, 1)
            dve.wait_ge(s_tr, 1)
            dve.tensor_copy(modr[:], accr[:])
            dve.tensor_copy(gmodr[:], accg[:]).then_inc(s_modr, 1)


def projection(nc, a, g):
    NS = 5
    GRP = [(0, 2), (2, 4), (6, 4)]
    BLK = [(0, 512), (512, 512), (1024, 256)]
    with Phase(nc, "proj") as ph:
        s_mm = ph.sem("mm")
        st = Stream(ph, NS, NS, s_mm, 3)
        M0 = 3 * NS
        xr = ph.sb("xr", [128, NTT, D])
        hh = ph.sb("hh", [128, KT, T], F32R)
        hl = ph.sb("hl", [128, KT, T], F32R)
        junk = ph.sb("junk", [128, D])
        ss = ph.sb("ss", [128, NTT])
        rr = ph.sb("rr", [128, NTT])
        r2 = ph.sb("r2", [128, NTT])
        stats_sq = ph.sb("stats_sq", [128, NTT])
        bank = [ph.ps(f"bank{i}", [128, 512]) for i in range(8)]
        s_x = [ph.sem(f"x_landed{i}") for i in range(NTT)]
        s_ss, s_sq, s_r, s_xs = ph.sem("ss"), ph.sem("sqrt"), ph.sem("rstd"), ph.sem("xs")
        s_tr, s_h, s_hh, s_hl = ph.sem("tr"), ph.sem("h"), ph.sem("hh"), ph.sem("hl")
        s_evd, s_eva = ph.sem("ev_dve"), ph.sem("ev_act")
        s_st = [ph.sem(f"stored{i}") for i in range(2)]
        s_vmm, s_vev = ph.sem("vmm"), ph.sem("vev")
        s_vst = [ph.sem(f"vstored{i}") for i in range(2)]
        s_fin = ph.sem("fin")
        block = ph.block()
        tmp = [junk[:, 0:512], junk[:, 512:1024]]
        stage = [xr[:, 2:4, :].rearrange("p a b -> p (a b)")[:, 0:T], xr[:, 4:6, :].rearrange("p a b -> p (a b)")[:, 0:T]]
        vstage = [xr[:, 6, 0:512], xr[:, 7, 0:512]]
        NIT = 2
        CPI = NF // NIT

        @block.sync
        def _(sp):
            for t in range(NTT):
                sp.dma_start(xr[:, t, :], a["x"][t * 128:(t + 1) * 128, :]).then_inc(s_x[t], 16)
            for s in s_st:
                sp.sem_inc(s, 16)
            for c in range(4):
                st.load(sp, 0, 0, c, a["w_in"][c])
            with sp.Fori(0, NIT) as i:
                for c in range(CPI):
                    n = i * CPI + c
                    st.load(sp, 0, i * CPI, c + 4, a["w_in"][bass.ds(n + 4, 1)].rearrange("a p f -> p (a f)"))
                    sp.wait_ge(s_evd, n + 3)
                    sp.wait_ge(s_eva, n * 2 + 6)
                    sp.dma_start(g["QKH"][bass.ds(n * 128, 128), :], stage[c % 2]).then_inc(s_st[c % 2], 16)
            for b in range(2):
                sp.wait_ge(s_st[b], 16 * (NF // 2 + 1))

        @block.gpsimd
        def _(pool):
            for t in range(NTT):
                pool.wait_ge(s_vev, t + 1)
                pool.dma_start(g["V"][t * 128:(t + 1) * 128, :], vstage[t % 2]).then_inc(s_vst[t % 2], 16)
            for b in range(2):
                pool.wait_ge(s_st[b], 16 * (NF // 2 + 1))
                pool.wait_ge(s_vst[b], 16 * (NTT // 2))
            pool.dma_start(a["state_kT"], g["QKH"][512:1024, 0:TP]).then_inc(s_fin, 16)
            pool.dma_start(a["state_v"], g["V"][0:TP, :]).then_inc(s_fin, 16)
            pool.wait_ge(s_fin, 32)

        @block.scalar
        def _(act):
            for t in range(NTT):
                act.wait_ge(s_x[t], 16)
                if t:
                    act.wait_ge(s_ss, t)
                act.activation(junk[:], xr[:, t, :], ACT.Square, accum_out=ss[:, t:t + 1]).then_inc(s_ss, 1)
            act.wait_ge(s_r, 1)
            act.activation(stats_sq[:], r2[:], ACT.Sqrt).then_inc(s_sq, 1)
            for q, (t0, nt) in enumerate(GRP):
                c = 1 if q == 0 else 0
                for k in range(KT):
                    n = q * KT + k
                    act.wait_ge(s_tr, n + 1)
                    if n >= 2:
                        act.wait_ge(s_hl, n - 1)
                    act.activation(tmp[n % 2][:, 0:nt * 128], bank[n % 8][:, 0:nt * 128], ACT.Identity,
                                   bias=g["mod"][:, k, c:c + 1], scale=g["gmod"][:, c, k:k + 1]).then_inc(s_h, 1)
                    act.wait_ge(s_h, n + 1)
                    act.activation(hh[:, k, t0 * 128:(t0 + nt) * 128], tmp[n % 2][:, 0:nt * 128], ACT.Copy).then_inc(s_hh, 1)
            act.sem_inc(s_eva, 4)
            for c in range(2):
                st.split_hi(act, 0, 0, c)
            with act.Fori(0, NIT) as i:
                for c in range(CPI):
                    n = i * CPI + c
                    st.split_hi(act, i * (CPI // NS), i * CPI, c + 2)
                    act.wait_ge(s_st[c % 2], (i * (CPI // 2) + c // 2 + 1) * 16)
                    for b in (1, 2):
                        c0, w = BLK[b]
                        act.wait_ge(s_mm, n * 3 + b + 1 + M0)
                        act.activation(stage[c % 2][:, c0:c0 + w], bank[(c % 2) * 3 + b][:, 0:w], ACT.Copy).then_inc(s_eva, 1)
            for c in range(2, 4):
                st.split_hi(act, NF // NS, NF, c)

        @block.vector
        def _(dve):
            st.start_dve(dve)
            dve.wait_ge(s_ss, NTT)
            dve.tensor_scalar(rr[:], ss[:], 1.0 / D, EPS, ALU.mult, ALU.add).then_inc(s_xs, 1)
            dve.wait_ge(s_xs, 1)
            dve.reciprocal(r2[:], rr[:]).then_inc(s_r, 1)
            dve.wait_ge(s_sq, 1)
            dve.tensor_tensor(r2[:], stats_sq[:], stats_sq[:], ALU.mult).then_inc(s_xs, 1)
            dve.wait_ge(s_xs, 2)
            dve.tensor_tensor(r2[:], r2[:], rr[:], ALU.mult).then_inc(s_xs, 1)
            dve.wait_ge(s_xs, 3)
            dve.tensor_scalar(r2[:], r2[:], -0.5, 1.5, ALU.mult, ALU.add).then_inc(s_xs, 1)
            dve.wait_ge(s_xs, 4)
            dve.tensor_tensor(rr[:], stats_sq[:], r2[:], ALU.mult).then_inc(s_xs, 1)
            dve.wait_ge(s_xs, 5)
            for t in range(NTT):
                dve.tensor_scalar(xr[:, t, :], xr[:, t, :], rr[:, t:t + 1], None, ALU.mult).then_inc(s_xs, 1)
            for q, (t0, nt) in enumerate(GRP):
                for k in range(KT):
                    n = q * KT + k
                    dve.wait_ge(s_hh, n + 1)
                    dve.tensor_tensor(hl[:, k, t0 * 128:(t0 + nt) * 128], tmp[n % 2][:, 0:nt * 128],
                                      hh[:, k, t0 * 128:(t0 + nt) * 128].bitcast(F32), ALU.subtract).then_inc(s_hl, 1)
            dve.sem_inc(s_evd, 2)
            for c in range(2):
                st.split_lo(dve, 0, c)
            with dve.Fori(0, NIT) as i:
                for c in range(CPI):
                    n = i * CPI + c
                    st.split_lo(dve, i * CPI, c + 2)
                    dve.wait_ge(s_st[c % 2], (i * (CPI // 2) + c // 2 + 1) * 16)
                    dve.wait_ge(s_mm, n * 3 + 1 + M0)
                    dve.tensor_copy(stage[c % 2][:, 0:512], bank[(c % 2) * 3][:, :]).then_inc(s_evd, 1)
            for c in range(2, 4):
                st.split_lo(dve, NF, c)
            for t in range(NTT):
                if t >= 2:
                    dve.wait_ge(s_vst[t % 2], 16 * (t // 2))
                dve.wait_ge(s_vmm, t + 1)
                dve.tensor_copy(vstage[t % 2], bank[6 + t % 2][:, :]).then_inc(s_vev, 1)

        @block.tensor
        def _(pe):
            st.start_pe(pe)
            for q, (t0, nt) in enumerate(GRP):
                for k in range(KT):
                    n = q * KT + k
                    if k == 0:
                        pe.wait_ge(s_xs, 5 + t0 + nt)
                    if n >= 8:
                        pe.wait_ge(s_h, n - 7)
                    for j in range(nt):
                        tr = pe.transpose(bank[n % 8][:, j * 128:(j + 1) * 128], xr[:, t0 + j, k * 128:(k + 1) * 128],
                                          g["ident"][:])
                    tr.then_inc(s_tr, 1)
            pe.wait_ge(s_hl, 3 * KT)
            pe.wait_ge(s_h, 3 * KT)
            with pe.Fori(0, NIT) as i:
                for c in range(CPI):
                    n = i * CPI + c
                    st.ready(pe, i * CPI, c)
                    for b, (c0, w) in enumerate(BLK):
                        pe.wait_ge(s_evd if b == 0 else s_eva, n + 1 if b == 0 else n * 2 + b)
                        out = bank[(c % 2) * 3 + b][:, 0:w]
                        for k in range(KT):
                            whi, wlo = st.tile(st.hi, c, k), st.tile(st.lo, c, k)
                            pe.matmul(out, whi, hh[:, k, c0:c0 + w], start=(k == 0), stop=False)
                            pe.matmul(out, whi, hl[:, k, c0:c0 + w], start=False, stop=False)
                            mm = pe.matmul(out, wlo, hh[:, k, c0:c0 + w], start=False, stop=(k == KT - 1))
                        mm.then_inc(s_mm, 1)
            st.ready(pe, NF, 3)
            for t in range(NTT):
                if t >= 2:
                    pe.wait_ge(s_vev, t - 1)
                out = bank[6 + t % 2][:, :]
                for k in range(KT):
                    xh, xl = hh[:, k, t * 128:(t + 1) * 128], hl[:, k, t * 128:(t + 1) * 128]
                    whi, wlo = st.tile(st.hi, k // 2, k % 2, 512), st.tile(st.lo, k // 2, k % 2, 512)
                    pe.matmul(out, xh, whi, start=(k == 0), stop=False)
                    pe.matmul(out, xh, wlo, start=False, stop=False)
                    mm = pe.matmul(out, xl, whi, start=False, stop=(k == KT - 1))
                mm.then_inc(s_vmm, 1)




def rstd_vector(dve, chain, s_root, root, ss, out, tmp, n):
    chain(dve.tensor_scalar(out, ss, 1.0 / n, EPS, ALU.mult, ALU.add))
    dve.reciprocal(tmp, out).then_inc(s_root, 1)
    dve.wait_ge(s_root, 2)
    chain(dve.tensor_tensor(tmp, root, root, ALU.mult))
    chain(dve.tensor_tensor(tmp, tmp, out, ALU.mult))
    chain(dve.tensor_scalar(tmp, tmp, -0.5, 1.5, ALU.mult, ALU.add))
    chain(dve.tensor_tensor(out, root, tmp, ALU.mult))


def rstd_scalar(act, s_root, root, tmp):
    act.wait_ge(s_root, 1)
    act.activation(root, tmp, ACT.Sqrt).then_inc(s_root, 1)


BLK_START = [min(max(j * QC - WC // 2, 0), GW - KC) for j in range(GW // QC)]


def attention(nc, a, g):
    NT = 2 * NTT
    with Phase(nc, "attn") as ph:
        q = ph.sb("q", [64, 2, T])
        qs = ph.sb("qs", [64, 2, T])
        k = ph.sb("k", [64, 2, T])
        ck = ph.sb("ck", [64, 2, NCTX])
        bias = ph.sb("bias", [128, 2, 8, NWIN])
        vw = ph.sb("vw", [128, 4, 4, DA])
        vc = ph.sb("vc", [128, 2, DA])
        vp = ph.sb("vp", [128, 2, DA])
        sw = ph.sb("sw", [128, 2, NWIN])
        p = ph.sb("p", [128, 2, NWIN + NCTX])
        pt = ph.sb("pt", [128, 2, NWIN + NCTX])
        mx = ph.sb("mx", [128, 2, 2])
        nm = ph.sb("nm", [128, 2])
        neg1 = ph.sb("neg1", [128, 1])
        l = ph.sb("l", [128, 4, 2])
        ls = ph.sb("ls", [128, 1])
        li = ph.sb("li", [128, 1])
        ar = ph.sb("ar", [128, NTT, DA])
        at = ph.sb("at", [128, 4, T])
        ss, rr, r2, root = (ph.sb(x, [128, NTT]) for x in ("ss", "rr", "r2", "root"))
        psw = [ph.ps(f"psw{b}", [128, 512]) for b in range(2)]
        psc = [ph.ps(f"psc{b}", [128, 512]) for b in range(2)]
        ptw = ph.ps("ptw", [128, 512])
        ptc = ph.ps("ptc", [128, 512])
        po = [ph.ps(f"po{b}", [128, 512]) for b in range(2)]
        s_v = ph.sem("v_landed")
        s_head = [ph.sem(f"head_landed{u}") for u in range(2)]
        s_q, s_s, s_am, s_exp = ph.sem("q_scaled"), ph.sem("scores"), ph.sem("max"), ph.sem("exp")
        s_t, s_ptw, s_ptc = ph.sem("transposed"), ph.sem("win_copied"), ph.sem("ctx_copied")
        s_pv, s_norm, s_dve = ph.sem("pv"), ph.sem("normed"), ph.sem("dve_steps")
        s_ss, s_root, s_rows, s_at = ph.sem("ss"), ph.sem("root"), ph.sem("rows"), ph.sem("at_ready")
        s_tr, s_atd, s_ata, s_out = ph.sem("tr"), ph.sem("at_dve"), ph.sem("at_act"), ph.sem("out")
        s_neg = ph.sem("neg1")
        block = ph.block()

        def tiles():
            return [(u * NTT + t, u, t) for u in range(2) for t in range(NTT)]

        def keys(t):
            if t < 2:
                return [(NWIN + 128 * c, ("p", c)) for c in range(2)]
            half, j = divmod(t - 2, 4)
            return [(128 * c, ("w", half + c, j)) for c in range(3)] + [(NWIN + 128 * c, ("c", c)) for c in range(2)]

        @block.sync
        def _(sp):
            vs = g["V"][TP:T, :].rearrange("(rg r c) f -> r c rg f", r=4, c=GW)
            for r in range(4):
                for j in range(4):
                    sp.dma_start(vw[32 * r:32 * r + 32, :, j, :], vs[r, BLK_START[j]:BLK_START[j] + KC]).then_inc(s_v, 16)
            sp.dma_start(vc[:], a["cache_v"]).then_inc(s_v, 16)
            sp.dma_start(vp[:], g["V"][0:TP, :].rearrange("(c p) f -> p c f", p=128)).then_inc(s_v, 16)
            with sp.Fori(0, NH // 2) as i:
                for u in range(2):
                    sp.wait_ge(s_pv, i * NT + u * NTT + NTT)
                    row = i * 128 + u * 64
                    sp.dma_start(q[:, u, :], g["QKH"][bass.ds(row, 64), :]).then_inc(s_head[u], 16)
                    sp.dma_start(k[:, u, :], g["QKH"][bass.ds(row + DA, 64), :]).then_inc(s_head[u], 16)
                    sp.dma_start(ck[:, u, :], a["cache_kT"][bass.ds(row, 64), :]).then_inc(s_head[u], 16)
                    sp.dma_start(bias[:, u, :, :].rearrange("p a b -> p (a b)"),
                                 a["bias"][bass.ds(i * 256 + u * 128, 128), :]).then_inc(s_head[u], 16)
            sp.wait_ge(s_atd, 2 * NTT)
            sp.wait_ge(s_ata, 2 * NTT)
            for f in range(4):
                sp.dma_start(g["MIXT"][f * 128:(f + 1) * 128, :], at[:, f, :]).then_inc(s_out, 16)
            sp.wait_ge(s_out, 64)

        @block.tensor
        def _(pe):
            pe.sem_inc(s_pv, NT)

            def scores(i, n, u, t):
                if t == 0:
                    pe.wait_ge(s_q, i * 2 + u + 1)
                if t < 2:
                    pe.matmul(psc[n % 2][:, 0:NCTX], qs[:, u, t * 128:(t + 1) * 128], k[:, u, 0:TP],
                              start=True, stop=True).then_inc(s_s, 1)
                    return
                half, j = divmod(t - 2, 4)
                qv = qs[:, u, t * 128:(t + 1) * 128]
                kv = k[:, u, TP:T].rearrange("d (r c) -> d r c", c=GW)[:, half * 4:half * 4 + KR,
                                                                      BLK_START[j]:BLK_START[j] + KC]
                pe.matmul(psw[n % 2][:, 0:NWIN], qv, kv, start=True, stop=True)
                pe.matmul(psc[n % 2][:, 0:NCTX], qv, ck[:, u, :], start=True, stop=True).then_inc(s_s, 1)

            def transposes(i, n, t):
                pe.wait_ge(s_exp, i * NT + n + 1)
                for col, _ in keys(t):
                    out = ptw[:, col:col + 128] if col < NWIN else ptc[:, col - NWIN:col - NWIN + 128]
                    tr = pe.transpose(out, p[:, n % 2, col:col + 128], g["ident"][:])
                tr.then_inc(s_t, 1)

            def values(i, n, u, t):
                if t >= 2:
                    pe.wait_ge(s_ptw, i * 16 + u * 8 + t - 1)
                pe.wait_ge(s_ptc, i * NT + n + 1)
                pe.wait_ge(s_norm, i * NT + n + 1)
                ks = keys(t)
                for x, (col, v) in enumerate(ks):
                    vt = {"p": vp[:, v[1], :], "c": vc[:, v[1], :]}[v[0]] if v[0] != "w" else vw[:, v[1], v[2], :]
                    mm = pe.matmul(po[n % 2][:, 0:HD], pt[:, n % 2, col:col + 128],
                                   vt[:, bass.ds(i * 128 + u * 64, HD)], start=(x == 0), stop=(x == len(ks) - 1))
                mm.then_inc(s_pv, 1)

            pe.wait_ge(s_v, 16 * 18)
            with pe.Fori(0, NH // 2) as i:
                ts = tiles()
                scores(i, *ts[0])
                for n, u, t in ts:
                    if n + 1 < NT:
                        scores(i, *ts[n + 1])
                    if n:
                        values(i, *ts[n - 1])
                    transposes(i, n, t)
                values(i, *ts[-1])
            for t in range(NTT):
                pe.wait_ge(s_rows, t + 1)
                if t >= 2:
                    pe.wait_ge(s_atd, 2 * (t - 1))
                    pe.wait_ge(s_ata, 2 * (t - 1))
                for f in range(4):
                    out = (psw if f < 2 else psc)[t % 2][:, f % 2 * 128:f % 2 * 128 + 128]
                    tr = pe.transpose(out, ar[:, t, f * 128:(f + 1) * 128], g["ident"][:])
                tr.then_inc(s_tr, 1)

        def at_out(f, t):
            if t < 2:
                return at[:, f, t * 128:(t + 1) * 128]
            half, j = divmod(t - 2, 4)
            return at[:, f, TP:T].rearrange("p (r c) -> p r c", c=GW)[:, half * 8:half * 8 + 8, j * QC:(j + 1) * QC]

        def at_in(f, t):
            x = (psw if f < 2 else psc)[t % 2][:, f % 2 * 128:f % 2 * 128 + 128]
            return x if t < 2 else x.rearrange("p (r c) -> p r c", c=QC)

        @block.vector
        def _(dve):
            dve.sem_inc(s_norm, 2)
            dve.memset(neg1[:], -1.0).then_inc(s_neg, 1)
            dve.wait_ge(s_neg, 1)
            with dve.Fori(0, NH // 2) as i:
                PER = 2 * (2 * 2 + 8 * 3)
                chain = Chain(dve, s_dve, i * PER)

                def add_max(n, u, t):
                    if t == 0:
                        dve.wait_ge(s_head[u], i * 64 + 64)
                        dve.tensor_scalar(qs[:, u, 0:TP], q[:, u, 0:TP], HD ** -0.5, None, ALU.mult)
                        for h in range(2):
                            c0 = TP + h * 512
                            ins = dve.tensor_scalar(qs[:, u, c0:c0 + 512].rearrange("d (j r c) -> d j r c", r=8, c=QC),
                                                    q[:, u, c0:c0 + 512].rearrange("d (r j c) -> d j r c", r=8, c=QC),
                                                    HD ** -0.5, None, ALU.mult)
                        ins.then_inc(s_q, 1)
                    dve.wait_ge(s_s, i * NT + n + 1)
                    if t < 2:
                        chain(dve.tensor_reduce(mx[:, n % 2, 0:1], psc[n % 2][:, 0:NCTX], AX.X, ALU.max))
                        dve.tensor_scalar(nm[:, n % 2:n % 2 + 1], mx[:, n % 2, 0:1], -1.0, None, ALU.mult).then_inc(s_am, 1)
                        return
                    dve.tensor_reduce(mx[:, n % 2, 1:2], psc[n % 2][:, 0:NCTX], AX.X, ALU.max)
                    chain(dve.tensor_tensor_reduce(sw[:, n % 2, :], psw[n % 2][:, 0:NWIN], bias[:, u, t - 2, :], 1.0,
                                                   3 * NEG, ALU.add, ALU.max, mx[:, n % 2, 0:1]))
                    dve.scalar_tensor_tensor(nm[:, n % 2:n % 2 + 1], mx[:, n % 2, 0:1], mx[:, n % 2, 1:2], neg1[:],
                                             ALU.max, ALU.mult).then_inc(s_am, 1)

                def copy_win(n, u, t):
                    if t >= 2:
                        dve.wait_ge(s_t, i * NT + n + 1)
                        dve.tensor_copy(pt[:, n % 2, 0:NWIN], ptw[:, 0:NWIN]).then_inc(s_ptw, 1)

                def norm(n, u, t):
                    dve.wait_ge(s_pv, i * NT + n + 1 + NT)
                    if t < 2:
                        chain(dve.reciprocal(li[:], l[:, n % 4, 1:2]))
                    else:
                        chain(dve.tensor_tensor(ls[:], l[:, n % 4, 0:1], l[:, n % 4, 1:2], ALU.add))
                        chain(dve.reciprocal(li[:], ls[:]))
                    dve.tensor_scalar(ar[:, t, bass.ds(i * 128 + u * 64, HD)], po[n % 2][:, 0:HD], li[:], None,
                                      ALU.mult).then_inc(s_norm, 1)

                ts = tiles()
                add_max(*ts[0])
                for n, u, t in ts:
                    if n + 1 < NT:
                        add_max(*ts[n + 1])
                    copy_win(n, u, t)
                    if n:
                        norm(*ts[n - 1])
                norm(*ts[-1])
                assert chain.n == PER
            dve.wait_ge(s_ss, NTT)
            rchain = Chain(dve, s_neg, 1)
            rstd_vector(dve, rchain, s_root, root[:], ss[:], rr[:], r2[:], DA)
            for t in range(NTT):
                dve.tensor_scalar(ar[:, t, :], ar[:, t, :], rr[:, t:t + 1], None, ALU.mult).then_inc(s_rows, 1)
            for t in range(NTT):
                dve.wait_ge(s_tr, t + 1)
                for f in range(2):
                    dve.tensor_scalar(at_out(f, t), at_in(f, t), g["gains"][:, 16 + f:17 + f], None, ALU.mult).then_inc(s_atd, 1)

        @block.scalar
        def _(act):
            with act.Fori(0, NH // 2) as i:
                def exps(n, u, t):
                    act.wait_ge(s_am, i * NT + n + 1)
                    nb = nm[:, n % 2:n % 2 + 1]
                    if t >= 2:
                        act.activation(p[:, n % 2, 0:NWIN], sw[:, n % 2, :], ACT.Exp, bias=nb, accum_out=l[:, n % 4, 0:1])
                    act.activation(p[:, n % 2, NWIN:], psc[n % 2][:, 0:NCTX], ACT.Exp, bias=nb,
                                   accum_out=l[:, n % 4, 1:2]).then_inc(s_exp, 1)

                def copy_ctx(n, u, t):
                    act.wait_ge(s_t, i * NT + n + 1)
                    act.activation(pt[:, n % 2, NWIN:], ptc[:, 0:NCTX], ACT.Copy).then_inc(s_ptc, 1)

                ts = tiles()
                exps(*ts[0])
                for n, u, t in ts:
                    if n + 1 < NT:
                        exps(*ts[n + 1])
                    copy_ctx(n, u, t)
            act.wait_ge(s_norm, NH * NTT + 2)
            for t in range(NTT):
                act.wait_ge(s_ss, t) if t else None
                act.activation(p[:, 0, 0:DA], ar[:, t, :], ACT.Square, accum_out=ss[:, t:t + 1]).then_inc(s_ss, 1)
            rstd_scalar(act, s_root, root[:], r2[:])
            for t in range(NTT):
                act.wait_ge(s_tr, t + 1)
                for f in range(2, 4):
                    act.activation(at_out(f, t), at_in(f, t), ACT.Copy, scale=g["gains"][:, 16 + f:17 + f]).then_inc(s_ata, 1)


TWO_PI_HI = 6.28125
TWO_PI_MID = 0.0019353071693331003
TWO_PI_LO = 1.0253131677018246e-11
MAGIC = 12582912.0


def filter_jobs(MT):
    jobs = []
    for par in range(2):
        for f in range(MT):
            jobs += [("cos", par, f), ("sin", par, f)]
    return jobs + [("cosx", 0, 0)]


def filters(nc, a, g, s, L):
    M = L // 2
    MT = M // 128
    NZ = 2 * M + 2
    JOBS = filter_jobs(MT)
    NCK = (len(JOBS) * MT * 128 + CH - 1) // CH
    PC = 8 // MT if MT > 1 else 8
    TB = [(c, min(512, NZ - c)) for c in range(0, NZ, 512)]
    NB = len(TB)
    with Phase(nc, f"filt{s}") as ph:
        st = Stream(ph, 3, 3, ph.sem("chunk_used"))
        z = ph.sb("z", [33, NZ])
        w1 = ph.sb("w1", [33, 64])
        w2 = ph.sb("w2", [64, 64])
        w3 = ph.sb("w3", [64, 4 * DH])
        fb = ph.sb("fb", [64, 3])
        y = ph.sb("y", [64, NZ])
        kk = ph.sb("kk", [64, NZ])
        hid = ph.sb("hid", [64, NZ])
        win = ph.sb("win", [128, 2, 2, DH])
        wmid = ph.sb("wmid", [1, DH])
        sgn = ph.sb("sgn", [1, 128])
        rowf = ph.sb("rowf", [128, 3])
        F = ph.sb("F", [128, 4, DH])
        AB = ph.sb("AB", [128, 4, DH])
        ABm = ph.sb("ABm", [128, 4, DH])
        absacc = ph.sb("absacc", [128, DH])
        AA = ph.sb("AA", [128, DH])
        opnd_h = ph.sb("opnd_h", [128, MT, 4, DH], F32R)
        opnd_l = ph.sb("opnd_l", [128, MT, 4, DH], F32R)
        mid = ph.sb("mid", [1, 4, DH])
        rn = ph.sb("rn", [128, DH])
        skip = ph.sb("skip", [128, 2, DH])
        spec = ph.sb("spec", [128, 2, DH])
        pf = [ph.ps(f"pf{b}", [128, 512]) for b in range(4)]
        pk = [ph.ps(f"pk{b}", [128, 512]) for b in range(2)]
        pn = ph.ps("pn", [128, 512])
        pm = ph.ps("pm", [128, 512])
        s_in, s_h, s_dve, s_sin = ph.sem("in_landed"), ph.sem("hidden_mm"), ph.sem("dve_steps"), ph.sem("sin")
        s_y = ph.sem("y_ready")
        s_win = [ph.sem(f"win_landed{b}") for b in range(2)]
        s_f, s_F, s_pool, s_ab = ph.sem("filt_mm"), ph.sem("windowed"), ph.sem("pool_steps"), ph.sem("abs")
        s_oh, s_ol, s_n, s_rn = ph.sem("opnd_hi"), ph.sem("opnd_lo"), ph.sem("norm_mm"), ph.sem("rnorm")
        s_mid, s_midv = ph.sem("mid_mm"), ph.sem("mid_ready")
        s_k = ph.sem("spec_mm")
        s_ev = ph.sem("spec_ready")
        s_st = [ph.sem(f"stored{b}") for b in range(2)]
        block = ph.block()
        NJ = len(JOBS)

        @block.sync
        def _(sp):
            for dst, src in ((z, "z"), (w1, None), (w2, None), (w3, None), (fb, None), (wmid, "wmid"), (sgn, None), (rowf, "rowf")):
                name = {id(w1): "filt_w1", id(w2): "filt_w2", id(w3): "filt_w3", id(fb): "filt_b", id(sgn): "sgn"}.get(id(dst))
                sp.dma_start(dst[:], a[name or f"{src}_{s}"]).then_inc(s_in, 16)
            for o in range(2):
                sp.dma_start(skip[:, o, :], a["hyena_bias"][o:o + 1, :].to_broadcast([128, DH])).then_inc(s_in, 16)
            for o in range(2):
                for c in range(min(3, NCK)):
                    st.load(sp, 0, 0, o * NCK + c, a[f"kbasis_{s}"][c])
                for t in range(MT):
                    n = o * MT + t
                    if n >= 2:
                        sp.wait_ge(s_F, (n - 1))
                    sp.dma_start(win[:, n % 2], a[f"win_{s}"][t]).then_inc(s_win[n % 2], 16)
                for ji, (kind, par, f) in enumerate(JOBS):
                    if ji % PC == 0 and ji // PC + 3 < NCK:
                        st.load(sp, 0, 0, o * NCK + ji // PC + 3, a[f"kbasis_{s}"][ji // PC + 3])
                    job = o * NJ + ji
                    sp.wait_ge(s_ev, job + 1)
                    slot = {"cos": 0, "sin": 1, "cosx": 2}[kind]
                    sp.dma_start(g[f"K{s}"][o, par * MT + f, slot], spec[:, job % 2, :]).then_inc(s_st[job % 2], 16)
            for b in range(2):
                sp.wait_ge(s_st[b], 16 * NJ)

        @block.tensor
        def _(pe):
            st.start_pe(pe)
            pe.wait_ge(s_in, 16 * 10)
            for layer in range(2):
                for b, (c0, w) in enumerate(TB):
                    if layer:
                        pe.wait_ge(s_sin, 1)
                    pe.matmul(pf[b][0:64, 0:w], (w2 if layer else w1)[:], (hid if layer else z)[:, c0:c0 + w],
                              start=True, stop=True).then_inc(s_h, 1)
            pe.wait_ge(s_sin, 2)
            job = 0
            for o in range(2):
                for t in range(MT):
                    n = o * MT + t
                    if n:
                        pe.wait_ge(s_F, n)
                    for x in range(4):
                        d, m = x % 2, x // 2
                        mm = pe.matmul(pf[x][:], hid[:, m * M + t * 128:m * M + t * 128 + 128],
                                       w3[:, (d * 2 + o) * DH:(d * 2 + o + 1) * DH], start=True, stop=True)
                    mm.then_inc(s_f, 1)
                for d in range(2):
                    if d or o:
                        pe.wait_ge(s_mid, 2 * o + d)
                    pe.matmul(pm[0:1, :], hid[:, 2 * M:2 * M + 1], w3[:, (d * 2 + o) * DH:(d * 2 + o + 1) * DH],
                              start=True, stop=True).then_inc(s_midv, 1)
                pe.wait_ge(s_ab, o + 1)
                pe.matmul(pn[:], g["ones"][:], absacc[:], start=True, stop=True).then_inc(s_n, 1)
                pe.wait_ge(s_ol, (o + 1) * MT)
                for ji, (kind, par, f) in enumerate(JOBS):
                    c = o * NCK + ji // PC
                    if ji % PC == 0:
                        st.ready(pe, 0, c)
                    if job >= 2:
                        pe.wait_ge(s_ev, job - 1)
                    x = {"cos": par, "cosx": 0, "sin": 2 + par}[kind]
                    rank1 = (kind != "sin" and par == 0) or (kind == "sin" and par == 1)
                    for t in range(MT):
                        ti = (ji % PC) * MT + t
                        bh, bl = st.tile(st.hi, c, ti), st.tile(st.lo, c, ti)
                        pe.matmul(pk[job % 2][:], bh, opnd_h[:, t, x, :], start=(t == 0), stop=False)
                        pe.matmul(pk[job % 2][:], bh, opnd_l[:, t, x, :], start=False, stop=False)
                        mm = pe.matmul(pk[job % 2][:], bl, opnd_h[:, t, x, :], start=False,
                                       stop=(t == MT - 1 and not rank1))
                    if ji % PC == PC - 1 or ji == NJ - 1:
                        mm.then_inc(st.used, 1)
                    if rank1:
                        mm = pe.matmul(pk[job % 2][:], sgn[:], mid[:, 0 if kind != "sin" else 1, :], start=False, stop=True)
                        mm.then_inc(s_k, 1)
                    elif ji % PC == PC - 1 or ji == NJ - 1:
                        pe.matmul(pm[0:1, 0:2], sgn[:, 0:1], sgn[:, 0:2], start=True, stop=True).then_inc(s_k, 1)
                    else:
                        mm.then_inc(s_k, 1)
                    job += 1

        @block.scalar
        def _(act):
            for layer in range(2):
                act.wait_ge(s_y, layer + 1)
                act.activation(hid[:], y[:], ACT.Sin).then_inc(s_sin, 1)
            for o in range(2):
                for c in range(2):
                    if c < NCK:
                        st.split_hi(act, 0, 0, o * NCK + c)
                for t in range(MT):
                    n = o * MT + t
                    act.wait_ge(s_pool, 8 * n + 8)
                    if o and t == 0:
                        act.wait_ge(s_k, NJ)
                    for x in range(4):
                        act.activation(opnd_h[:, t, x, :], ABm[:, x, :], ACT.Copy).then_inc(s_oh, 1)
                for c in range(2, NCK):
                    st.split_hi(act, 0, 0, o * NCK + c)

        @block.gpsimd
        def _(pool):
            sub, add = ALU.subtract, ALU.add
            for o in range(2):
                for t in range(MT):
                    n = o * MT + t
                    pool.wait_ge(s_F, n + 1)
                    if n:
                        pool.wait_ge(s_ol, n)
                    for m in range(2):
                        pool.tensor_tensor(AB[:, m, :], F[:, 2 * m, :], F[:, 2 * m + 1, :], add).then_inc(s_pool, 1)
                        pool.tensor_tensor(AB[:, 2 + m, :], F[:, 2 * m + 1, :], F[:, 2 * m, :], sub).then_inc(s_pool, 1)
                    pool.wait_ge(s_pool, 8 * n + 4)
                    for x, (q, op) in enumerate(((0, add), (0, sub), (2, sub), (2, add))):
                        pool.tensor_tensor(ABm[:, x, :], AB[:, q, :], AB[:, q + 1, :], op).then_inc(s_pool, 1)

        @block.vector
        def _(dve):
            st.start_dve(dve)
            chain = Chain(dve, s_dve)
            dve.wait_ge(s_in, 16 * 10)
            for layer in range(2):
                for b, (c0, w) in enumerate(TB):
                    dve.wait_ge(s_h, layer * NB + b + 1)
                    ins = dve.tensor_scalar(y[:, c0:c0 + w], pf[b][0:64, 0:w], fb[:, layer:layer + 1], fb[:, 2:3],
                                            ALU.add, ALU.mult)
                chain(ins)
                chain(dve.tensor_scalar(kk[:], y[:], 1.0 / (2 * np.pi), MAGIC, ALU.mult, ALU.add))
                chain(dve.tensor_scalar(kk[:], kk[:], MAGIC, None, ALU.subtract))
                for part in (TWO_PI_HI, TWO_PI_MID, TWO_PI_LO):
                    chain(dve.scalar_tensor_tensor(y[:], kk[:], -part, y[:], ALU.mult, ALU.add))
                dve.tensor_scalar(y[:], y[:], 3.1415925, -3.1415925, ALU.min, ALU.max).then_inc(s_y, 1)
            for o in range(2):
                dve.memset(absacc[:], 0.0).then_inc(s_dve, 1)
                chain.n += 1
                dve.wait_ge(s_dve, chain.n)
                if o:
                    dve.wait_ge(s_n, 1)
                for t in range(MT):
                    n = o * MT + t
                    dve.wait_ge(s_f, n + 1)
                    dve.wait_ge(s_win[n % 2], 16 * (n // 2 + 1))
                    if n:
                        dve.wait_ge(s_pool, 8 * n)
                    for x in range(4):
                        ins = dve.tensor_tensor(F[:, x, :], pf[x][:], win[:, n % 2, x // 2, :], ALU.mult)
                    if t == 0:
                        chain(ins)
                        chain(dve.memset(F[0:1, 1, :], 0.0))
                    else:
                        chain(ins)
                    for x in range(4):
                        chain(dve.scalar_tensor_tensor(AA[:], F[:, x, :], -1.0, F[:, x, :], ALU.mult, ALU.max))
                        ins = dve.tensor_tensor(absacc[:], absacc[:], AA[:], ALU.add)
                        if x < 3:
                            chain(ins)
                    ins.then_inc(s_F, 1)
                    dve.wait_ge(s_F, n + 1)
                    for x in range(4):
                        dve.wait_ge(s_oh, 4 * n + x + 1)
                        ins = dve.tensor_tensor(opnd_l[:, t, x, :], ABm[:, x, :], opnd_h[:, t, x, :].bitcast(F32), ALU.subtract)
                    ins.then_inc(s_ol, 1)
                for d in range(2):
                    dve.wait_ge(s_midv, 2 * o + d + 1)
                    dve.tensor_tensor(mid[:, 2 + d, :], pm[0:1, :], wmid[:], ALU.mult).then_inc(s_mid, 1)
                dve.wait_ge(s_mid, 2 * o + 2)
                dve.tensor_tensor(mid[:, 0, :], mid[:, 2, :], mid[:, 3, :], ALU.add)
                dve.tensor_tensor(mid[:, 1, :], mid[:, 3, :], mid[:, 2, :], ALU.subtract)
                for d in range(2):
                    chain(dve.scalar_tensor_tensor(AA[0:1, :], mid[:, 2 + d, :], -1.0, mid[:, 2 + d, :], ALU.mult, ALU.max))
                    ins = dve.tensor_tensor(absacc[0:1, :], absacc[0:1, :], AA[0:1, :], ALU.add)
                    if d == 0:
                        chain(ins)
                ins.then_inc(s_ab, 1)
                for c in range(min(2, NCK)):
                    st.split_lo(dve, 0, o * NCK + c)
                dve.wait_ge(s_n, o + 1)
                chain(dve.reciprocal(rn[:], pn[:]))
                for ji in range(NJ):
                    job = o * NJ + ji
                    c = ji // PC + 2
                    if ji % PC == 0 and c < NCK:
                        st.split_lo(dve, 0, o * NCK + c)
                    dve.wait_ge(s_k, job + 1)
                    if job >= 2:
                        dve.wait_ge(s_st[job % 2], 16 * (job // 2))
                    col = 0 if JOBS[ji][1:] == (0, 0) else 1
                    ins = dve.scalar_tensor_tensor(spec[:, job % 2, :], pk[job % 2][:], rowf[:, col:col + 1], rn[:],
                                                   ALU.mult, ALU.mult)
                    if JOBS[ji][0] != "sin":
                        chain(ins)
                        ins = dve.scalar_tensor_tensor(spec[:, job % 2, :], skip[:, o, :], rowf[:, col:col + 1],
                                                       spec[:, job % 2, :], ALU.mult, ALU.add)
                    ins.then_inc(s_ev, 1)


def hyena(nc, a, g, s, L, tok0):
    M = L // 2
    MT = M // 128
    NJ = 2 * MT
    NC = 16 if MT == 4 else 1

    def fwd_tile(j, kind, t):
        return (j, kind * MT + t) if MT == 4 else (0, 2 * j + kind)

    def inv_tile(j, kind):
        return (8 + j, kind) if MT == 4 else (0, 4 + 2 * j + kind)

    with Phase(nc, f"hy{s}") as ph:
        s_step = ph.sem("step_mm")
        st = Stream(ph, 3, 3, s_step, 2 * NJ // NC)
        S0 = 3 * st.per
        pad = ph.sb("pad", [128, 2, L + 2])
        cw = ph.sb("cw", [128, 12, 4])
        u = ph.sb("u", [128, 4, L])
        fold = ph.sb("fold", [128, 4, L])
        uh = ph.sb("uh", [128, 2, MT, DH], F32R)
        ul = ph.sb("ul", [128, 2, MT, DH], F32R)
        kt = ph.sb("kt", [128, 2, 3, DH])
        pr = ph.sb("pr", [128, 4, DH])
        Ph = ph.sb("Ph", [128, 2, NJ, DH], F32R)
        Pl = ph.sb("Pl", [128, 2, NJ, DH], F32R)
        pc = pr
        bank = [ph.ps(f"bank{b}", [128, 512]) for b in range(8)]
        s_cw = ph.sem("cw_landed")
        s_pad = [ph.sem(f"pad_landed{b}") for b in range(2)]
        s_zero, s_dve, s_conv, s_fold = ph.sem("edges"), ph.sem("dve_steps"), ph.sem("conv"), ph.sem("folded")
        s_tr, s_uh, s_ul = ph.sem("transposed"), ph.sem("u_hi"), ph.sem("u_lo")
        s_kt = [ph.sem(f"k_landed{b}") for b in range(2)]
        s_prod, s_pool = ph.sem("products"), ph.sem("pool_steps")
        s_Ph, s_Pl = ph.sem("P_hi"), ph.sem("P_lo")
        s_pc, s_z, s_out = ph.sem("half_copied"), ph.sem("gated"), ph.sem("out")
        block = ph.block()

        def load_pad(pool, n):
            if n >= 2:
                pool.wait_ge(s_conv, n - 1)
            pool.dma_start(pad[:, n % 2, 1:L + 1], g["QKH"][1024 + n * 128:1152 + n * 128, tok0:tok0 + L])\
                .then_inc(s_pad[n % 2], 16)

        def load_k(pool, o, j):
            n = o * NJ + j
            if n >= 2:
                pool.wait_ge(s_prod, n - 1)
            w = 3 if j == 0 else 2
            pool.dma_start(kt[:, n % 2, 0:w, :], g[f"K{s}"][o, j, 0:w].rearrange("a p f -> p a f")).then_inc(s_kt[n % 2], 16)

        @block.sync
        def _(sp):
            sp.dma_start(cw[:], a["conv"]).then_inc(s_cw, 16)
            for o in range(2):
                for c in range(NC):
                    st.load(sp, 0, 0, o * NC + c, a[f"basis_{s}"][c])
            for ct in range(4):
                sp.wait_ge(s_z, 4 + ct + 1)
                sp.dma_start(g["MIXT"][DA + ct * 128:DA + (ct + 1) * 128, tok0:tok0 + L], u[:, ct, :]).then_inc(s_out, 16)
            sp.wait_ge(s_out, 64)

        @block.gpsimd
        def _(pool):
            pool.wait_ge(s_zero, 1)
            for n in range(4):
                load_pad(pool, n)
            for o in range(2):
                load_k(pool, o, 0)
                load_k(pool, o, 1)
                for j in range(NJ):
                    n = o * NJ + j
                    pool.wait_ge(s_prod, n + 1)
                    pool.tensor_tensor(pr[:, 0, :], pr[:, 0, :], pr[:, 1, :], ALU.add).then_inc(s_pool, 1)
                    pool.tensor_tensor(pr[:, 2, :], pr[:, 2, :], pr[:, 3, :], ALU.subtract).then_inc(s_pool, 1)
                    if j + 2 < NJ:
                        load_k(pool, o, j + 2)
                for c in range(4):
                    load_pad(pool, 4 + 4 * o + c)

        @block.scalar
        def _(act):
            for o in range(2):
                for c in range(min(2, NC)):
                    st.split_hi(act, 0, 0, o * NC + c)
                for q in range(2 * MT):
                    act.wait_ge(s_tr, o * 2 * MT + q + 1)
                    act.activation(uh[:, q // MT, q % MT, :], bank[q][:], ACT.Copy).then_inc(s_uh, 1)
                for j in range(NJ):
                    n = o * NJ + j
                    if j + 2 < NC:
                        st.split_hi(act, 0, 0, o * NC + j + 2)
                    act.wait_ge(s_pool, 2 * n + 2)
                    if o and j == 0:
                        act.wait_ge(s_step, S0 + 2 * NJ)
                    for x in range(2):
                        act.activation(Ph[:, x, j, :], pr[:, 2 * x, :], ACT.Copy).then_inc(s_Ph, 1)
                for c in range(NJ + 2, NC):
                    st.split_hi(act, 0, 0, o * NC + c)
                act.wait_ge(s_step, S0 + (o + 1) * 2 * NJ)
                act.wait_ge(s_Pl, (o + 1) * 2 * NJ)
                for ct in range(4):
                    act.activation(pc[:, ct, 0:M], bank[4 + ct][:, 0:M], ACT.Copy).then_inc(s_pc, 1)

        @block.vector
        def _(dve):
            st.start_dve(dve)
            chain = Chain(dve, s_dve)
            dve.memset(pad[:, :, 0:1], 0.0)
            dve.memset(pad[:, :, L + 1:L + 2], 0.0).then_inc(s_zero, 1)
            dve.wait_ge(s_cw, 16)

            def conv(n, out):
                dve.wait_ge(s_pad[n % 2], 16 * (n // 2 + 1))
                p = pad[:, n % 2]
                chain(dve.tensor_scalar(out, p[:, 1:L + 1], cw[:, n, 1:2], cw[:, n, 3:4], ALU.mult, ALU.add))
                chain(dve.scalar_tensor_tensor(out, p[:, 0:L], cw[:, n, 0:1], out, ALU.mult, ALU.add))
                dve.scalar_tensor_tensor(out, p[:, 2:L + 2], cw[:, n, 2:3], out, ALU.mult, ALU.add).then_inc(s_conv, 1)

            for n in range(4):
                conv(n, u[:, n, :])
            dve.wait_ge(s_conv, 4)
            for o in range(2):
                if o:
                    dve.wait_ge(s_z, 4)
                dve.tensor_tensor(fold[:, :, 0:M], u[:, :, 0:M], u[:, :, L - 1:M - 1:-1], ALU.add)
                dve.tensor_tensor(fold[:, :, M:L], u[:, :, 0:M], u[:, :, L - 1:M - 1:-1], ALU.subtract).then_inc(s_fold, 1)
                for c in range(min(2, NC)):
                    st.split_lo(dve, 0, o * NC + c)
                for q in range(2 * MT):
                    dve.wait_ge(s_uh, o * 2 * MT + q + 1)
                    dve.tensor_tensor(ul[:, q // MT, q % MT, :], bank[q][:], uh[:, q // MT, q % MT, :].bitcast(F32),
                                      ALU.subtract).then_inc(s_ul, 1)
                for j in range(NJ):
                    n = o * NJ + j
                    if j + 2 < NC:
                        st.split_lo(dve, 0, o * NC + j + 2)
                    dve.wait_ge(s_kt[n % 2], 16 * (n // 2 + 1))
                    dve.wait_ge(s_step, S0 + o * 2 * NJ + j + 1)
                    ur, us = bank[(n % 2) * 2], bank[(n % 2) * 2 + 1]
                    k = kt[:, n % 2]
                    dve.tensor_tensor(pr[:, 0, :], ur[:], k[:, 0, :], ALU.mult)
                    dve.tensor_tensor(pr[:, 1, :], us[:], k[:, 1, :], ALU.mult)
                    dve.tensor_tensor(pr[:, 2, :], us[:], k[:, 2 if j == 0 else 0, :], ALU.mult)
                    dve.tensor_tensor(pr[:, 3, :], ur[:], k[:, 1, :], ALU.mult).then_inc(s_prod, 1)
                    for x in range(2):
                        dve.wait_ge(s_Ph, 2 * n + x + 1)
                        dve.tensor_tensor(Pl[:, x, j, :], pr[:, 2 * x, :], Ph[:, x, j, :].bitcast(F32),
                                          ALU.subtract).then_inc(s_Pl, 1)
                    dve.wait_ge(s_Pl, 2 * n + 2)
                for c in range(4):
                    if NJ + 2 + 2 * c < NC:
                        st.split_lo(dve, 0, o * NC + NJ + 2 + 2 * c)
                    conv(4 + 4 * o + c, fold[:, c, :])
                    if NJ + 3 + 2 * c < NC:
                        st.split_lo(dve, 0, o * NC + NJ + 3 + 2 * c)
                dve.wait_ge(s_conv, 8 + 4 * o)
                for ct in range(4):
                    dve.wait_ge(s_pc, 4 * o + ct + 1)
                    dve.wait_ge(s_step, S0 + (o + 1) * 2 * NJ)
                    chain(dve.tensor_tensor(u[:, ct, 0:M], pc[:, ct, 0:M], bank[ct][:, 0:M], ALU.add))
                    chain(dve.tensor_tensor(u[:, ct, L - 1:M - 1:-1], pc[:, ct, 0:M], bank[ct][:, 0:M], ALU.subtract))
                    dve.tensor_tensor(u[:, ct, :], u[:, ct, :], fold[:, ct, :], ALU.mult).then_inc(s_z, 1)

        @block.tensor
        def _(pe):
            st.start_pe(pe)
            for o in range(2):
                pe.wait_ge(s_fold, o + 1)
                if o:
                    pe.wait_ge(s_z, 4)
                for q in range(2 * MT):
                    par, t = divmod(q, MT)
                    for ct in range(4):
                        tr = pe.transpose(bank[q][:, ct * 128:(ct + 1) * 128],
                                          fold[:, ct, par * M + t * 128:par * M + (t + 1) * 128], g["ident"][:])
                    tr.then_inc(s_tr, 1)
                pe.wait_ge(s_ul, (o + 1) * 2 * MT)
                last = -1
                for j in range(NJ):
                    n = o * NJ + j
                    if n >= 2:
                        pe.wait_ge(s_prod, n - 1)
                    par = j // MT
                    for kind in range(2):
                        src = par if kind == 0 else 1 - par
                        out = bank[(n % 2) * 2 + kind]
                        for t in range(MT):
                            c, ti = fwd_tile(j, kind, t)
                            if c > last:
                                st.ready(pe, 0, o * NC + c)
                                last = c
                            bh, bl = st.tile(st.hi, o * NC + c, ti), st.tile(st.lo, o * NC + c, ti)
                            pe.matmul(out[:], bh, uh[:, src, t, :], start=(t == 0), stop=False)
                            pe.matmul(out[:], bh, ul[:, src, t, :], start=False, stop=False)
                            mm = pe.matmul(out[:], bl, uh[:, src, t, :], start=False, stop=(t == MT - 1))
                    mm.then_inc(s_step, 1)
                pe.wait_ge(s_prod, (o + 1) * NJ)
                for j in range(NJ):
                    n = o * NJ + j
                    pe.wait_ge(s_Pl, 2 * n + 2)
                    for kind in range(2):
                        c, ti = inv_tile(j, kind)
                        if c > last:
                            st.ready(pe, 0, o * NC + c)
                            last = c
                        w = M
                        bh, bl = st.tile(st.hi, o * NC + c, ti, w), st.tile(st.lo, o * NC + c, ti, w)
                        even = (kind == j // MT)
                        first = j == 0
                        final = j == NJ - 1
                        for ct in range(4):
                            out = bank[(4 if even else 0) + ct][:, 0:w]
                            xh, xl = Ph[:, kind, j, ct * 128:(ct + 1) * 128], Pl[:, kind, j, ct * 128:(ct + 1) * 128]
                            pe.matmul(out, xh, bh, start=first, stop=False)
                            pe.matmul(out, xh, bl, start=False, stop=False)
                            mm = pe.matmul(out, xl, bh, start=False, stop=final)
                    mm.then_inc(s_step, 1)


def mix_and_route(nc, a, g):
    BLK = [(0, 512), (512, 512), (1024, 256)]
    with Phase(nc, "mix") as ph:
        s_tile = ph.sem("mix_mm")
        st = Stream(ph, 2, 8, ph.sem("unused"), 1)
        mh = ph.sb("mh", [128, KT, T], F32R)
        ml = ph.sb("ml", [128, KT, T], F32R)
        raw = ph.sb("raw4", [128, 4, T])
        r = ph.sb("r", [128, T])
        work = ph.sb("work", [128, 6 * D])
        sq = work[:, 0:4 * T].rearrange("p (a b) -> p a b", a=4)
        sqr = work[:, 0:2 * T].rearrange("p (a b) -> p a b", a=2)
        h2 = work[:, 0:2 * D].rearrange("p (a b) -> p a b", a=2)
        h2T = work[:, 2 * D:3 * D].rearrange("p (a b) -> p a b", a=KT)
        rows = work[:, 3 * D:6 * D].rearrange("p (a b) -> p a b", a=3)
        wr = ph.sb("wr", [128, KT, NE])
        ss, rr, r2, root = (ph.sb(x, [128, NTT]) for x in ("ss", "rr", "r2", "root"))
        lm, lsum, linv = (ph.sb(x, [128, NTT]) for x in ("lm", "lsum", "linv"))
        aff = ph.sb("aff", [128, NTT, NE])
        bank = [ph.ps(f"bank{b}", [128, 512]) for b in range(8)]
        xb = [raw[:, b, 0:D] for b in range(2)]
        tb = [raw[:, 2 + b, 0:D] for b in range(2)]
        s_y, s_at = [ph.sem(f"y_landed{b}") for b in range(4)], [ph.sem(f"at_landed{b}") for b in range(4)]
        s_sq, s_sum, s_dve, s_root, s_yn = ph.sem("squares"), ph.sem("sum_mm"), ph.sem("dve_steps"), ph.sem("root"), ph.sem("y_normed")
        s_mh, s_ml = ph.sem("m_hi"), ph.sem("m_lo")
        s_row, s_x = ph.sem("rows_landed"), [ph.sem(f"x_landed{b}") for b in range(2)]
        s_wr = ph.sem("router_landed")
        s_t, s_x1, s_ss, s_rt, s_h = ph.sem("mixed"), ph.sem("x1"), ph.sem("x1_squares"), ph.sem("row_root"), ph.sem("h2_scaled")
        s_h2, s_x1st, s_h2st = ph.sem("h2"), [ph.sem(f"x1_stored{b}") for b in range(2)], [ph.sem(f"h2_stored{b}") for b in range(2)]
        s_tr, s_hT, s_lg, s_lm, s_ex = ph.sem("h2_transposed"), ph.sem("h2T"), ph.sem("logits"), ph.sem("logit_max"), ph.sem("exps")
        s_aff = ph.sem("affinity")
        s_swap = ph.sem("group_done")
        block = ph.block()
        junk = r[:, 0:D]

        def load_rows(sp, c):
            for n, (src, c0) in enumerate((("MODR", 2 * D), ("GMODR", D), ("MODR", 3 * D))):
                sp.dma_start(rows[:, n, :], g[src][c:c + 1, c0:c0 + D].to_broadcast([128, D])).then_inc(s_row, 16)

        def store(sp, t):
            sp.wait_ge(s_x1, t + 1)
            sp.dma_start(g["X"][t * 128:(t + 1) * 128, :], xb[t % 2]).then_inc(s_x1st[t % 2], 16)
            sp.wait_ge(s_h2, t + 1)
            sp.dma_start(g["H2"][t * 128:(t + 1) * 128, :], h2[:, t % 2, :]).then_inc(s_h2st[t % 2], 16)

        @block.sync
        def _(sp):
            for ct in range(4):
                sp.dma_start(raw[:, ct, :], g["MIXT"][DA + ct * 128:DA + (ct + 1) * 128, :]).then_inc(s_y[ct], 16)
            sp.dma_start(wr[:], a["w_router"]).then_inc(s_wr, 16)
            for c in range(2):
                st.load(sp, 0, 0, c, a["w_out"][c])
            sp.wait_ge(s_yn, 4)
            load_rows(sp, 1)
            for ct in range(4):
                sp.wait_ge(s_ml, ct + 1)
                sp.dma_start(raw[:, ct, :], g["MIXT"][ct * 128:(ct + 1) * 128, :]).then_inc(s_at[ct], 16)
            for c in range(2, 8):
                st.load(sp, 0, 0, c, a["w_out"][c])
            for t in range(NTT):
                if t < 2:
                    sp.wait_ge(s_ml, 8)
                else:
                    if t == 2:
                        sp.wait_ge(s_h2, 2)
                        load_rows(sp, 0)
                    sp.wait_ge(s_x1st[t % 2], 16 * (t // 2))
                    sp.wait_ge(s_h, t - 1)
                    sp.wait_ge(s_ss, t - 1)
                sp.dma_start(xb[t % 2], a["x"][t * 128:(t + 1) * 128, :]).then_inc(s_x[t % 2], 16)
                if t:
                    store(sp, t - 1)
            store(sp, NTT - 1)
            for b in range(2):
                sp.wait_ge(s_x1st[b], 16 * (NTT // 2))
                sp.wait_ge(s_h2st[b], 16 * (NTT // 2))

        @block.gpsimd
        def _(pool):
            for t in range(NTT):
                pool.wait_ge(s_t, t + 1)
                pool.wait_ge(s_x[t % 2], 16 * (t // 2 + 1))
                pool.tensor_tensor(xb[t % 2], xb[t % 2], tb[t % 2], ALU.add).then_inc(s_x1, 1)
                pool.wait_ge(s_h, t + 1)
                pool.tensor_tensor(h2[:, t % 2, :], h2[:, t % 2, :], rows[:, 2, :], ALU.add).then_inc(s_h2, 1)

        @block.scalar
        def _(act):
            act.sem_inc(st.used, 8)
            for ct in range(4):
                act.wait_ge(s_y[ct], 16)
                act.activation(sq[:, ct, :], raw[:, ct, :], ACT.Square).then_inc(s_sq, 1)
            rstd_scalar(act, s_root, sqr[:, 0, :], sqr[:, 1, :])
            for ct in range(4):
                act.wait_ge(s_yn, ct + 1)
                act.activation(mh[:, 4 + ct, :], raw[:, ct, :], ACT.Copy).then_inc(s_mh, 1)
            for c in range(8):
                if c < 4:
                    act.wait_ge(s_at[c], 16)
                    act.activation(mh[:, c, :], raw[:, c, :], ACT.Copy).then_inc(s_mh, 1)
                st.split_hi(act, 0, 0, c)
            for t in range(NTT + 1):
                if t < NTT:
                    act.wait_ge(s_x1, t + 1)
                    if t:
                        act.wait_ge(s_ss, t)
                    act.activation(junk, xb[t % 2], ACT.Square,
                                   accum_out=ss[:, t:t + 1]).then_inc(s_ss, 1)
                    act.wait_ge(s_rt, 2 * t + 1)
                    act.activation(root[:, t:t + 1], r2[:, t:t + 1], ACT.Sqrt).then_inc(s_rt, 1)
                if t:
                    q = t - 1
                    for b in range(2):
                        act.wait_ge(s_tr, 2 * q + b + 1)
                        act.activation(h2T[:, 4 * b:4 * b + 4, :].rearrange("p a b -> p (a b)"), bank[4 + b][:], ACT.Copy).then_inc(s_hT, 1)
                    act.wait_ge(s_lm, q + 1)
                    act.activation(aff[:, q, :], bank[6][:, 0:NE], ACT.Exp, bias=lm[:, q:q + 1],
                                   accum_out=lsum[:, q:q + 1]).then_inc(s_ex, 1)

        @block.vector
        def _(dve):
            st.start_dve(dve)
            chain = Chain(dve, s_dve)
            v = r[:]
            for b, (c0, w) in enumerate(BLK):
                dve.wait_ge(s_sum, b + 1)
                ins = dve.tensor_scalar(r[:, c0:c0 + w], bank[b][:, 0:w], 1.0 / DH, EPS, ALU.mult, ALU.add)
            chain(ins)
            x0, x1_ = sqr[:, 0, :], sqr[:, 1, :]
            dve.reciprocal(x1_, r[:]).then_inc(s_root, 1)
            dve.wait_ge(s_root, 2)
            chain(dve.tensor_tensor(x1_, x0, x0, ALU.mult))
            chain(dve.tensor_tensor(x1_, x1_, r[:], ALU.mult))
            chain(dve.tensor_scalar(x1_, x1_, -0.5, 1.5, ALU.mult, ALU.add))
            chain(dve.tensor_tensor(r[:], x0, x1_, ALU.mult))
            for ct in range(4):
                dve.scalar_tensor_tensor(raw[:, ct, :], raw[:, ct, :], g["gains"][:, 20 + ct:21 + ct], r[:],
                                         ALU.mult, ALU.mult).then_inc(s_yn, 1)
            for ct in range(4):
                dve.wait_ge(s_mh, ct + 1)
                dve.tensor_tensor(ml[:, 4 + ct, :], raw[:, ct, :], mh[:, 4 + ct, :].bitcast(F32), ALU.subtract).then_inc(s_ml, 1)
            for c in range(8):
                if c < 4:
                    dve.wait_ge(s_mh, 5 + c)
                    dve.tensor_tensor(ml[:, c, :], raw[:, c, :], mh[:, c, :].bitcast(F32), ALU.subtract).then_inc(s_ml, 1)
                st.split_lo(dve, 0, c)
            for t in range(NTT + 1):
                if t < NTT:
                    dve.wait_ge(s_row, 48 if t < 2 else 96)
                    dve.wait_ge(s_tile, t + 1)
                    if t >= 2:
                        dve.wait_ge(s_x1, t - 1)
                    if t < 2:
                        dve.wait_ge(s_ml, 8)
                    for b in range(2):
                        ins = dve.tensor_tensor(tb[t % 2][:, b * 512:b * 512 + 512], bank[(t % 2) * 2 + b][:],
                                                rows[:, 0, b * 512:b * 512 + 512], ALU.mult)
                    ins.then_inc(s_t, 1)
                    dve.wait_ge(s_ss, t + 1)
                    c1 = slice(t, t + 1)
                    chain(dve.tensor_scalar(rr[:, c1], ss[:, c1], 1.0 / D, EPS, ALU.mult, ALU.add))
                    dve.reciprocal(r2[:, c1], rr[:, c1]).then_inc(s_rt, 1)
                    dve.wait_ge(s_rt, 2 * t + 2)
                    chain(dve.tensor_tensor(r2[:, c1], root[:, c1], root[:, c1], ALU.mult))
                    chain(dve.tensor_tensor(r2[:, c1], r2[:, c1], rr[:, c1], ALU.mult))
                    chain(dve.tensor_scalar(r2[:, c1], r2[:, c1], -0.5, 1.5, ALU.mult, ALU.add))
                    chain(dve.tensor_tensor(rr[:, c1], root[:, c1], r2[:, c1], ALU.mult))
                    if t >= 2:
                        dve.wait_ge(s_h2st[t % 2], 16 * (t // 2))
                        dve.wait_ge(s_tr, 2 * (t - 1))
                    dve.scalar_tensor_tensor(h2[:, t % 2, :], xb[t % 2], rr[:, c1], rows[:, 1, :],
                                             ALU.mult, ALU.mult).then_inc(s_h, 1)
                if t:
                    q = slice(t - 1, t)
                    dve.wait_ge(s_lg, t)
                    dve.tensor_reduce(lm[:, q], bank[6][:, 0:NE], AX.X, ALU.max, negate=True).then_inc(s_lm, 1)
                    dve.wait_ge(s_ex, t)
                    chain(dve.reciprocal(linv[:, q], lsum[:, q]))
                    dve.tensor_scalar(g["aff"][:, t - 1, :], aff[:, t - 1, :], linv[:, q], None, ALU.mult).then_inc(s_aff, 1)

        @block.tensor
        def _(pe):
            for b, (c0, w) in enumerate(BLK):
                for ct in range(4):
                    if b == 0:
                        pe.wait_ge(s_sq, ct + 1)
                    mm = pe.matmul(bank[b][:, 0:w], g["ones"][:], sq[:, ct, c0:c0 + w], start=(ct == 0), stop=(ct == 3))
                mm.then_inc(s_sum, 1)
            pe.wait_ge(s_wr, 16)
            pe.wait_ge(s_yn, 1)

            def route(t):
                pe.wait_ge(s_h2, t + 1)
                for b in range(2):
                    if t:
                        pe.wait_ge(s_hT, 2 * (t - 1) + b + 1)
                    for k in range(4):
                        tr = pe.transpose(bank[4 + b][:, k * 128:(k + 1) * 128], h2[:, t % 2, (4 * b + k) * 128:(4 * b + k + 1) * 128],
                                          g["ident"][:])
                    tr.then_inc(s_tr, 1)
                pe.wait_ge(s_hT, 2 * t + 2)
                if t:
                    pe.wait_ge(s_ex, t)
                for k in range(KT):
                    mm = pe.matmul(bank[6][:, 0:NE], h2T[:, k, :], wr[:, k, :], start=(k == 0), stop=(k == KT - 1))
                mm.then_inc(s_lg, 1)

            for t in range(NTT):
                if t == 0:
                    pe.wait_ge(s_ml, 8)
                    st.ready(pe, 0, 7)
                if t >= 2:
                    pe.wait_ge(s_t, t - 1)
                for b in range(2):
                    out = bank[(t % 2) * 2 + b][:]
                    for k in range(KT):
                        xh, xl = mh[:, k, t * 128:(t + 1) * 128], ml[:, k, t * 128:(t + 1) * 128]
                        wh, wl = st.tile(st.hi, k, b, 512), st.tile(st.lo, k, b, 512)
                        pe.matmul(out, xh, wh, start=(k == 0), stop=False)
                        pe.matmul(out, xh, wl, start=False, stop=False)
                        mm = pe.matmul(out, xl, wh, start=False, stop=(k == KT - 1))
                mm.then_inc(s_tile, 1)
                if t:
                    route(t - 1)
            route(NTT - 1)


def choose_tokens(nc, a, g):
    with Phase(nc, "top") as ph:
        affT = ph.sb("affT", [NE, T])
        val = ph.sb("val", [NE, CAP])
        idx = ph.sb("idx", [NE, CAP], U32)
        idf = ph.sb("idf", [NE, CAP])
        pa = [ph.ps(f"pa{b}", [NE, 512]) for b in range(3)]
        pt = ph.ps("pt", [128, 2, NE])
        ptp = ph.ps("ptp", [CAP_P, 2, NE])
        s_tr, s_dve, s_tab = ph.sem("tr"), ph.sem("dve_steps"), ph.sem("tables")
        block = ph.block()

        @block.tensor
        def _(pe):
            for t in range(NTT):
                tr = pe.transpose(pa[t // 4][:, (t % 4) * 128:(t % 4) * 128 + 128], g["aff"][:, t, :], g["ident"][:])
                tr.then_inc(s_tr, 1)
            pe.wait_ge(s_tab, 1)
            for n, src in enumerate((idf, val)):
                pe.transpose(pt[:, n, :], src[:, 0:CAP_S], g["ident"][0:NE, 0:NE])
                tr = pe.transpose(ptp[:, n, :], src[:, CAP_S:CAP], g["ident"][0:NE, 0:NE])
            tr.then_inc(s_tr, 1)

        @block.vector
        def _(dve):
            chain = Chain(dve, s_dve)
            dve.memset(g["rows_s"][:], 0)
            dve.memset(g["rows_p"][:], 0)
            for b in range(3):
                w = min(512, T - 512 * b)
                dve.wait_ge(s_tr, min(4 * b + 4, NTT))
                ins = dve.tensor_copy(affT[:, 512 * b:512 * b + w], pa[b][:, 0:w])
            chain(ins)
            for c0, n, s0 in ((TP, TS, 0), (0, TP, CAP_S)):
                work = affT[:, c0:c0 + n]
                cap = CAP_S if n == TS else CAP_P
                for r in range(cap // 8):
                    v, x = val[:, s0 + 8 * r:s0 + 8 * r + 8], idx[:, s0 + 8 * r:s0 + 8 * r + 8]
                    chain(dve.max(v, work))
                    chain(dve.max_index(x, v, work))
                    if r + 1 < cap // 8:
                        chain(dve.match_replace(work, v, work, -1.0))
            dve.tensor_copy(idf[:, CAP_S:CAP], idx[:, CAP_S:CAP])
            dve.tensor_scalar(idf[:, 0:CAP_S], idx[:, 0:CAP_S], float(TP), None, ALU.add).then_inc(s_tab, 1)
            dve.wait_ge(s_tr, NTT + 1)
            dve.tensor_copy(g["rows_s"][:, 0:NE], pt[:, 0, :])
            dve.tensor_copy(g["gate_s"][:, 0:NE], pt[:, 1, :])
            dve.tensor_copy(g["rows_p"][:, 0:NE], ptp[:, 0, :])
            dve.tensor_copy(g["gate_p"][:, 0:NE], ptp[:, 1, :]).then_inc(s_tab, 1)
            dve.wait_ge(s_tab, 2)


def experts(nc, a, g):
    CW, C2 = 2 * FT, FT * D // CH
    NC = CW + C2
    GD = D // 128
    XB = [(0, 3), (3, 3), (6, 2)]
    AHEAD_HI, AHEAD_LO = 4, 3
    end = [CW + (FT * d + FT - 1) // 8 for d in range(GD)]
    shared = [d for d in range(GD) if (FT * d + FT) % 8 == 0]
    alone = [d for d in range(GD) if d not in shared]
    with Phase(nc, "exp") as ph:
        st = Stream(ph, 11, 6, ph.sem("chunk_used"), 1)
        xg = ph.sb("xg", [128, D])
        xp = ph.sb("xp", [CAP_P, D])
        xt = ph.sb("xt", [128, KT, 2 * CAP], F32R)
        hid = ph.sb("hid", [128, FT, 2 * CAP], F32R)
        cpy = ph.sb("cpy", [128, 2, 2, CAP])
        s13 = ph.sb("s13", [128, 2, 2, CAP])
        sl = ph.sb("sl", [128, 2, CAP])
        hd = ph.sb("hd", [128, 2, CAP])
        cy = ph.sb("cy", [128, 2, CAP])
        ye = ph.sb("ye", [128, 2, CAP])
        ys = ph.sb("ys", [128, D])
        yp = ph.sb("yp", [CAP_P, D])
        cur_s, next_s = ph.sb("cur_s", [128, 1], U32), ph.sb("next_s", [128, 1], U32)
        cur_p, next_p = ph.sb("cur_p", [CAP_P, 1], U32), ph.sb("next_p", [CAP_P, 1], U32)
        gate_s, gate_p = ph.sb("gate_s", [128, 1]), ph.sb("gate_p", [CAP_P, 1])
        step, one = ph.sb("step", [1, 1]), g["ident"][0:1, 0:1]
        ps = ph.ps("ps", [128, 4, 512])
        py = [ph.ps(f"py{b}", [128, 512]) for b in range(2)]
        pr = ph.ps("pr", [128, 512])
        pp = ph.ps("pp", [CAP_P, 512])
        s_ix, s_xg, s_xtr = ph.sem("index_ready"), ph.sem("x_gathered"), ph.sem("x_transposed")
        s_xhi, s_xlo = ph.sem("x_hi"), ph.sem("x_lo")
        s_cp, s_add, s_sl, s_hd = ph.sem("low_copied"), ph.sem("pair_summed"), ph.sem("silu"), ph.sem("hidden")
        s_hh, s_hid = ph.sem("hidden_hi"), ph.sem("hidden_lo")
        s_g, s_cy, s_ye, s_yt = ph.sem("group_done"), ph.sem("y_low_copied"), ph.sem("y_gated"), ph.sem("y_transposed")
        s_row, s_sc = ph.sem("rows_ready"), ph.sem("scattered")
        block = ph.block()

        def xbank(b, n):
            return ps[:, b, 0:n * CAP].rearrange("p (k t) -> p k t", k=n)

        def group_done(eng, e, d):
            if d in shared:
                eng.wait_ge(st.used, e * NC + end[d] + 1 + st.ns)
            else:
                eng.wait_ge(s_g, e * len(alone) + alone.index(d) + 1)

        @block.sync
        def _(sp):
            with sp.Fori(0, NE) as e:
                for c in range(CW):
                    st.load(sp, 0, e * NC, c, a["w13"][bass.ds(e * CW + c, 1)].rearrange("a p f -> p (a f)"))
                for c in range(CW, NC):
                    st.load(sp, 0, e * NC, c, a["w2"][bass.ds(e * C2 + (c - CW), 1)].rearrange("a p f -> p (a f)"))
            for c in range(AHEAD_HI):
                st.load(sp, 0, NE * NC, c, a["w13"][c])

        @block.gpsimd
        def _(pool):
            pool.tensor_copy(next_s[:], g["rows_s"][:, 0:1])
            pool.tensor_copy(next_p[:], g["rows_p"][:, 0:1]).then_inc(s_ix, 1)

            def gather(n):
                pool.wait_ge(s_ix, n)
                pool.tensor_tensor(step[:], one, one, ALU.mult)
                pool.indirect_dma_start(xg[:], None, g["H2"], bass.IndirectOffsetOnAxis(ap=next_s[:, 0:1], axis=0)).then_inc(s_xg, 16)
                pool.indirect_dma_start(xp[:], None, g["H2"], bass.IndirectOffsetOnAxis(ap=next_p[:, 0:1], axis=0)).then_inc(s_xg, 16)

            gather(1)
            with pool.Fori(0, NE) as e:
                pool.wait_ge(s_xg, e * 32 + 32)
                pool.wait_ge(s_xtr, e * 3 + 3)
                pool.tensor_copy(cur_s[:], g["rows_s"][:, bass.ds(e, 1)])
                pool.tensor_copy(cur_p[:], g["rows_p"][:, bass.ds(e, 1)])
                pool.tensor_copy(gate_s[:], g["gate_s"][:, bass.ds(e, 1)])
                pool.tensor_copy(gate_p[:], g["gate_p"][:, bass.ds(e, 1)])
                pool.tensor_copy(next_s[:], g["rows_s"][:, bass.ds(e + 1, 1)])
                pool.tensor_copy(next_p[:], g["rows_p"][:, bass.ds(e + 1, 1)]).then_inc(s_ix, 1)
                gather(e + 2)
                for j in range(FT):
                    b = j % 2
                    pool.wait_ge(s_sl, e * FT + j + 1)
                    pool.tensor_tensor(hd[:, b], sl[:, b], s13[:, b, 1], ALU.mult).then_inc(s_hd, 1)
                    pool.wait_ge(s_hh, e * FT + j + 1)
                    pool.tensor_tensor(hid[:, j, CAP:2 * CAP], hd[:, b], hid[:, j, 0:CAP].bitcast(F32), ALU.subtract).then_inc(s_hid, 1)
                pool.wait_ge(s_row, e * 2 + 3)
                pool.tensor_tensor(step[:], one, one, ALU.mult)
                pool.indirect_dma_start(g["X"], bass.IndirectOffsetOnAxis(ap=cur_s[:, 0:1], axis=0), ys[:], None,
                                        compute_op=ALU.add).then_inc(s_sc, 16)
                pool.indirect_dma_start(g["X"], bass.IndirectOffsetOnAxis(ap=cur_p[:, 0:1], axis=0), yp[:], None,
                                        compute_op=ALU.add).then_inc(s_sc, 16)
                pool.wait_ge(s_sc, e * 32 + 32)
            pool.wait_ge(s_xg, NE * 32 + 32)

        @block.scalar
        def _(act):
            act.sem_inc(s_row, 1)

            def x_hi(n):
                for b, (k0, m) in enumerate(XB):
                    act.wait_ge(s_xtr, n * 3 + b + 1)
                    act.activation(xt[:, k0:k0 + m, 0:CAP], xbank(b, m), ACT.Copy).then_inc(s_xhi, 1)

            def y_low(e, d):
                group_done(act, e, d)
                act.wait_ge(s_ye, e * GD + d + 1)
                act.activation(cy[:, d % 2, 0:CAP_S], py[d % 2][:, CAP:CAP + CAP_S], ACT.Identity,
                               scale=g["mod"][:, 40 + d, 0:1])
                act.activation(cy[:, d % 2, CAP_S:CAP], py[d % 2][:, CAP + CAP_S:2 * CAP], ACT.Identity,
                               scale=g["mod"][:, 40 + d, 1:2]).then_inc(s_cy, 1)

            def rows_out(e, h):
                act.wait_ge(s_ix, e + 2)
                act.wait_ge(s_yt, e * GD + 4 * h + 6)
                act.activation(ys[:, h * 512:h * 512 + 512], pr[:], ACT.Identity, scale=gate_s[:])
                act.activation(yp[:, h * 512:h * 512 + 512], pp[:], ACT.Identity, scale=gate_p[:]).then_inc(s_row, 1)

            for c in range(AHEAD_HI):
                st.split_hi(act, 0, 0, c)
            x_hi(0)
            with act.Fori(0, NE) as e:
                for c in range(NC):
                    st.split_hi(act, e * (NC // st.nr), e * NC, c + AHEAD_HI)
                    j = (c - 4) // 2
                    if c % 2 == 0 and 0 <= j < FT:
                        act.wait_ge(s_hd, e * FT + j + 1)
                        act.activation(hid[:, j, 0:CAP], hd[:, j % 2], ACT.Copy).then_inc(s_hh, 1)
                    j = (c - 3) // 2
                    if c % 2 == 1 and 0 <= j < FT:
                        act.wait_ge(s_add, e * FT + j + 3)
                        act.activation(sl[:, j % 2], s13[:, j % 2, 0], ACT.Silu).then_inc(s_sl, 1)
                    j = (c - 2) // 2
                    if c % 2 == 0 and 0 <= j < FT:
                        act.wait_ge(st.used, e * NC + 2 * j + 2 + st.ns)
                        act.wait_ge(s_add, e * FT + j + 1)
                        act.activation(cpy[:, j % 2], ps[:, 2 * (j % 2):2 * (j % 2) + 2, CAP:2 * CAP], ACT.Copy).then_inc(s_cp, 1)
                    for d in range(GD):
                        if c == end[d] + 1:
                            y_low(e, d)
                    if c == end[4] + 2:
                        rows_out(e, 0)
                    if c == end[6] + 1:
                        x_hi(e + 1)
                y_low(e, GD - 1)
                rows_out(e, 1)

        @block.vector
        def _(dve):
            st.start_dve(dve)
            dve.sem_inc(s_add, 2)
            dve.sem_inc(s_ye, 2)

            def x_lo(n):
                for b, (k0, m) in enumerate(XB):
                    dve.wait_ge(s_xhi, n * 3 + b + 1)
                    dve.tensor_tensor(xt[:, k0:k0 + m, CAP:2 * CAP], xbank(b, m), xt[:, k0:k0 + m, 0:CAP].bitcast(F32),
                                      ALU.subtract).then_inc(s_xlo, 1)

            def y_gate(e, d):
                dve.wait_ge(s_cy, e * GD + d + 1)
                dve.wait_ge(s_yt, e * GD + d + 1)
                dve.scalar_tensor_tensor(ye[:, d % 2, 0:CAP_S], py[d % 2][:, 0:CAP_S], g["mod"][:, 40 + d, 0:1],
                                         cy[:, d % 2, 0:CAP_S], ALU.mult, ALU.add)
                dve.scalar_tensor_tensor(ye[:, d % 2, CAP_S:CAP], py[d % 2][:, CAP_S:CAP], g["mod"][:, 40 + d, 1:2],
                                         cy[:, d % 2, CAP_S:CAP], ALU.mult, ALU.add).then_inc(s_ye, 1)

            for c in range(AHEAD_LO):
                st.split_lo(dve, 0, c)
            x_lo(0)
            with dve.Fori(0, NE) as e:
                for c in range(NC):
                    st.split_lo(dve, e * NC, c + AHEAD_LO)
                    j = (c - 2) // 2
                    if c % 2 == 0 and 0 <= j < FT:
                        dve.wait_ge(s_cp, e * FT + j + 1)
                        if j >= 2:
                            dve.wait_ge(s_hd, e * FT + j - 1)
                        dve.tensor_tensor(s13[:, j % 2], ps[:, 2 * (j % 2):2 * (j % 2) + 2, 0:CAP], cpy[:, j % 2],
                                          ALU.add).then_inc(s_add, 1)
                    for d in range(GD):
                        if c == end[d] + 1:
                            y_gate(e, d)
                    if c == end[6] + 1:
                        x_lo(e + 1)
                y_gate(e, GD - 1)

        @block.tensor
        def _(pe):
            st.start_pe(pe)
            pe.sem_inc(s_yt, 2)

            def x_transposes(n):
                pe.wait_ge(s_xg, n * 32 + 32)
                for b, (k0, m) in enumerate(XB):
                    for k in range(m):
                        cols = slice((k0 + k) * 128, (k0 + k + 1) * 128)
                        pe.transpose(ps[:, b, k * CAP:k * CAP + CAP_S], xg[:, cols], g["ident"][:])
                        tr = pe.transpose(ps[:, b, k * CAP + CAP_S:(k + 1) * CAP], xp[:, cols], g["ident"][0:CAP_P, 0:CAP_P])
                    tr.then_inc(s_xtr, 1)

            def y_transposes(e, d):
                pe.wait_ge(s_ye, e * GD + d + 3)
                if d % 4 == 0:
                    pe.wait_ge(s_row, e * 2 + d // 4 + 1)
                cols = slice((d % 4) * 128, (d % 4) * 128 + 128)
                pe.transpose(pr[:, cols], ye[:, d % 2, 0:CAP_S], g["ident"][:])
                pe.transpose(pp[:, cols], ye[:, d % 2, CAP_S:CAP], g["ident"][:]).then_inc(s_yt, 1)

            def product(out, c, t, rhs, first, last):
                wh, wl = st.tile(st.hi, c, t), st.tile(st.lo, c, t)
                if last:
                    pe.matmul(out[:, 0:CAP], wl, rhs[:, 0:CAP], start=False, stop=False)
                mm = pe.matmul(out[:, 0:2 * CAP], wh, rhs, start=first, stop=last)
                if not last:
                    mm = pe.matmul(out[:, 0:CAP], wl, rhs[:, 0:CAP], start=False, stop=False)
                return mm

            x_transposes(0)
            with pe.Fori(0, NE) as e:
                pe.wait_ge(s_xlo, e * 3 + 3)
                for c in range(CW):
                    j = c // 2
                    st.ready(pe, e * NC, c)
                    if c % 2 == 0:
                        pe.wait_ge(s_add, e * FT + j + 1)
                    for k in range(KT):
                        mm = product(ps[:, 2 * (j % 2) + c % 2, :], c, k, xt[:, k, :], k == 0, k == KT - 1)
                    mm.then_inc(st.used, 1)
                for n in range(GD * FT):
                    c, t, d, f = CW + n // 8, n % 8, n // FT, n % FT
                    if t == 0:
                        st.ready(pe, e * NC, c)
                    if f == 0:
                        pe.wait_ge(s_ye, e * GD + d + 1)
                    if d == 0:
                        pe.wait_ge(s_hid, e * FT + f + 1)
                    mm = product(py[d % 2], c, t, hid[:, f, :], f == 0, f == FT - 1)
                    if t == 7:
                        mm.then_inc(st.used, 1)
                    elif f == FT - 1:
                        mm.then_inc(s_g, 1)
                    if f == FT - 1:
                        if d:
                            y_transposes(e, d - 1)
                        if d == 6:
                            x_transposes(e + 1)
                y_transposes(e, GD - 1)


def final_norm(nc, a, g):
    NB = 5
    with Phase(nc, "fin") as ph:
        x = ph.sb("x", [128, NTT, D])
        gain = ph.sb("gain", [128, D])
        junk = ph.sb("junk", [128, D])
        ss, rr, r2, root = (ph.sb(n, [128, NTT]) for n in ("ss", "rr", "r2", "root"))
        s_g, s_x = ph.sem("gain_landed"), [ph.sem(f"x_landed{t}") for t in range(NTT)]
        s_ss, s_root, s_dve, s_y, s_out = ph.sem("squares"), ph.sem("root"), ph.sem("dve_steps"), ph.sem("y"), ph.sem("stored")
        block = ph.block()

        @block.sync
        def _(sp):
            for t in range(NTT):
                sp.dma_start(x[:, t, :], g["X"][t * 128:(t + 1) * 128, :]).then_inc(s_x[t], 16)
            sp.dma_start(gain[:], a["final_g"].to_broadcast([128, D])).then_inc(s_g, 16)
            for t in range(NTT):
                sp.wait_ge(s_y, t + 1)
                sp.dma_start(a["y"][t * 128:(t + 1) * 128, :], x[:, t, :]).then_inc(s_out, 16)
            sp.wait_ge(s_out, 16 * NTT)

        @block.scalar
        def _(act):
            for t in range(NTT):
                act.wait_ge(s_x[t], 16)
                if t:
                    act.wait_ge(s_ss, t)
                act.activation(junk[:], x[:, t, :], ACT.Square, accum_out=ss[:, t:t + 1]).then_inc(s_ss, 1)
                if (t + 1) % NB == 0:
                    q = t // NB
                    act.wait_ge(s_root, 2 * q + 1)
                    act.activation(root[:, q * NB:(q + 1) * NB], r2[:, q * NB:(q + 1) * NB], ACT.Sqrt).then_inc(s_root, 1)

        @block.vector
        def _(dve):
            chain = Chain(dve, s_dve)
            dve.wait_ge(s_g, 16)
            for q in range(NTT // NB):
                c = slice(q * NB, (q + 1) * NB)
                dve.wait_ge(s_ss, (q + 1) * NB)
                chain(dve.tensor_scalar(rr[:, c], ss[:, c], 1.0 / D, EPS, ALU.mult, ALU.add))
                dve.reciprocal(r2[:, c], rr[:, c]).then_inc(s_root, 1)
                dve.wait_ge(s_root, 2 * q + 2)
                chain(dve.tensor_tensor(r2[:, c], root[:, c], root[:, c], ALU.mult))
                chain(dve.tensor_tensor(r2[:, c], r2[:, c], rr[:, c], ALU.mult))
                chain(dve.tensor_scalar(r2[:, c], r2[:, c], -0.5, 1.5, ALU.mult, ALU.add))
                chain(dve.tensor_tensor(rr[:, c], root[:, c], r2[:, c], ALU.mult))
                for t in range(q * NB, (q + 1) * NB):
                    dve.scalar_tensor_tensor(x[:, t, :], x[:, t, :], rr[:, t:t + 1], gain[:], ALU.mult, ALU.mult).then_inc(s_y, 1)


def arrange(i):
    c = np.ascontiguousarray

    def cols(v):
        return v.reshape(-1, 128).T

    o = {}
    o["x"] = c(np.concatenate([i["x_prompt"][0], i["x_sample"][0]], 0))
    o["cond"] = c(np.stack([i["c"][0], i["c_ctx"]], 0).reshape(2, KT, 128).transpose(2, 1, 0))
    o["bada"] = c(cols(i["b_ada"][0]))
    o["gains"] = c(np.concatenate([cols(i["norm1_g"][0]), cols(i["norm2_g"][0]), cols(i["out_g_attn"][0]),
                                   cols(i["out_g_hyena"][0]), np.zeros((128, 8), np.float32)], 1))
    o["ident"] = np.eye(128, dtype=np.float32)
    o["w_ada"] = c(i["w_ada"][0].reshape(KT, 128, 6 * D).transpose(1, 0, 2))
    w = i["w_in"][0]
    wf = np.concatenate([w[:, 0:2 * DA], w[:, 3 * DA:]], 1)
    wf = wf.reshape(KT, 128, NF, 128).transpose(2, 1, 0, 3).reshape(NF, 128, CH)
    wv = w[:, 2 * DA:3 * DA].reshape(4, 2, 128, 512).transpose(0, 2, 1, 3).reshape(4, 128, CH)
    o["w_in"] = np.concatenate([wf, wv], 0)
    o["cache_kT"] = c(i["cache_k"][0, 0].transpose(0, 2, 1).reshape(DA, NCTX))
    o["cache_v"] = c(i["cache_v"][0, 0].reshape(NH, 2, 128, HD).transpose(2, 1, 0, 3).reshape(128, 2, DA))
    o["bias"] = relative_bias(i["rpb"][0])
    o["w_out"] = c(i["w_out"][0].reshape(KT, 128, D))
    o["w_router"] = c(i["w_router"][0].reshape(KT, 128, NE).transpose(1, 0, 2))
    o["w13"] = np.stack([i[n][0].reshape(NE, KT, 128, FT, 128).transpose(0, 3, 2, 1, 4).reshape(NE, FT, 128, CH)
                         for n in ("w1", "w3")], 2).reshape(NE * 2 * FT, 128, CH)
    o["w2"] = c(i["w2"][0].reshape(NE, FT, 128, KT, 128).transpose(0, 3, 1, 2, 4).reshape(NE, FT, 8, 128, 128)
                .transpose(0, 1, 3, 2, 4).reshape(NE * FT, 128, CH))
    o["final_g"] = c(i["final_g"][None])
    for s, L in (("p", TP), ("s", TS)):
        o |= filter_constants(s, L)
        o |= convolution_constants(s, L)
    f0 = lambda n: i[n][0]
    o["filt_w1"], o["filt_w2"], o["filt_w3"] = c(f0("filt_w1")), c(f0("filt_w2")), c(f0("filt_w3"))
    o["filt_b"] = c(np.stack([f0("filt_b1"), f0("filt_b2"), f0("filt_freq")], 1))
    o["hyena_bias"] = c(f0("hyena_bias"))
    o["conv"] = c(np.stack([cols(f0("conv_w")[x]) for x in range(3)] + [cols(f0("conv_b"))], 2))
    o["sgn"] = np.where(np.arange(128) % 2, -1.0, 1.0).astype(np.float32)[None]
    return o


def filter_constants(s, L):
    M, MT, bands = L // 2, L // 256, 16
    f32 = np.float32
    pos = np.concatenate([np.arange(M), L - np.arange(M), [M, M]]) % L
    t = np.linspace(0.0, 1.0, L, dtype=f32)[pos]
    w = (f32(2.0 * np.pi / L) * np.arange(L, dtype=f32))[pos]
    b = np.linspace(1e-4, bands - 1, bands, dtype=f32)
    ph = b[None, :] * w[:, None]
    z = np.concatenate([t[:, None], np.cos(ph), -np.sin(ph)], 1).T
    deltas = np.abs(np.linspace(np.log(1e-2) / 1.5, np.log(1e-2) / 0.3, DH, dtype=f32))
    win = np.exp(-t[:, None] * deltas) + f32(0.05)
    win[M] = 0.0
    wd = np.stack([win[:M].reshape(MT, 128, DH), win[M:2 * M].reshape(MT, 128, DH)], 2)
    x = np.arange(M)[:, None].astype(np.float64)
    tiles = []
    for kind, par, f in filter_jobs(MT):
        fr = 2.0 * (f * 128 + np.arange(128)) + par
        if kind == "cosx":
            fr[0] = L
        th = np.pi * fr[None, :] * x / L
        v = (np.sin(th) if kind == "sin" else np.cos(th)).reshape(MT, 128, 128)
        tiles += list(v)
    n = -(-len(tiles) // 8)
    tiles += [np.zeros((128, 128))] * (n * 8 - len(tiles))
    kb = np.stack(tiles).reshape(n, 8, 128, 128).transpose(0, 2, 1, 3).reshape(n, 128, CH)
    rowf = np.full((128, 3), 1.0 / L)
    rowf[0, 0] = 0.5 / L
    c = lambda v: np.ascontiguousarray(v, dtype=f32)
    return {f"z_{s}": c(z), f"win_{s}": c(wd), f"wmid_{s}": c(win[2 * M:2 * M + 1]), f"kbasis_{s}": c(kb), f"rowf_{s}": c(rowf)}


def convolution_constants(s, L):
    M, MT = L // 2, L // 256
    x = np.arange(M)[:, None] + 0.5
    fwd, inv = [], []
    for j in range(2 * MT):
        par, f = divmod(j, MT)
        fr = 2.0 * (f * 128 + np.arange(128)) + par
        for kind in range(2):
            fk = fr.copy()
            if kind == 1 and j == 0:
                fk[0] = L
            th = np.pi * fk[None, :] * x / L
            v = np.sin(th) if kind else np.cos(th)
            fwd += list(v.reshape(MT, 128, 128))
            inv.append(v.T)
    if MT == 4:
        f = np.stack(fwd).reshape(8, 8, 128, 128).transpose(0, 2, 1, 3).reshape(8, 128, CH)
        v = np.stack(inv).reshape(8, 2, 128, M).transpose(0, 2, 1, 3).reshape(8, 128, CH)
        b = np.concatenate([f, v])
    else:
        b = np.stack(fwd + inv).transpose(1, 0, 2).reshape(1, 128, CH)
    return {f"basis_{s}": np.ascontiguousarray(b, dtype=np.float32)}


def relative_bias(rpb):
    qi = np.arange(128)
    ki = np.arange(NWIN)
    out = np.full((NH, 128, 8, NWIN), NEG, np.float32)
    for half in range(2):
        for j in range(4):
            r, col = half * 8 + qi // QC, j * QC + qi % QC
            kr, kc = half * 4 + ki // KC, BLK_START[j] + ki % KC
            rs = np.clip(r - WR // 2, 0, TS // GW - WR)[:, None]
            ws = np.clip(col - WC // 2, 0, GW - WC)[:, None]
            ok = (kr[None] >= rs) & (kr[None] < rs + WR) & (kc[None] >= ws) & (kc[None] < ws + WC)
            dr = np.clip(kr[None] - r[:, None] + WR - 1, 0, 2 * WR - 2)
            dc = np.clip(kc[None] - col[:, None] + WC - 1, 0, 2 * WC - 2)
            t = out[:, :, half * 4 + j, :]
            t[:, ok] = rpb[:, dr[ok], dc[ok]]
    return out.reshape(NH * 128, 8 * NWIN)


def build(nc, a):
    def dram(name, shape):
        return nc.dram_tensor(name, shape, F32, kind="Internal").ap()

    g = {
        "MODR": dram("modulation_rows", [2, 6 * D]), "GMODR": dram("gain_rows", [2, 2 * D]),
        "QKH": dram("features", [NF * 128, T]), "V": dram("values", [T, DA]),
        "Kp": dram("spectrum_p", [2, 2, 3, 128, DH]), "Ks": dram("spectrum_s", [2, 8, 3, 128, DH]),
        "MIXT": dram("mixed", [D, T]), "X": dram("residual", [T, D]), "H2": dram("hidden_rows", [T, D]),
    }
    with ExitStack() as keep:
        for name, shape, dt in (("mod", [128, 48, 2], F32), ("gmod", [128, 2, 16], F32), ("gains", [128, 32], F32),
                                ("ident", [128, 128], F32), ("ones", [128, 128], F32), ("aff", [128, NTT, NE], F32),
                                ("gate_s", [128, NE], F32), ("gate_p", [CAP_P, NE], F32),
                                ("rows_s", [128, NE + 1], U32), ("rows_p", [CAP_P, NE + 1], U32)):
            g[name] = keep.enter_context(nc.sbuf_tensor(f"g_{name}", shape, dt))
        modulation(nc, a, g)
        projection(nc, a, g)
        attention(nc, a, g)
        for s, L, tok0 in (("p", TP, 0), ("s", TS, TP)):
            filters(nc, a, g, s, L)
            hyena(nc, a, g, s, L, tok0)
        mix_and_route(nc, a, g)
        choose_tokens(nc, a, g)
        experts(nc, a, g)
        final_norm(nc, a, g)


def kernel(**inputs):
    import concourse.bacc as bacc
    from concourse.bass_utils import run_bass_kernel_spmd

    arrays = {f"in_{n}": v for n, v in arrange({n: np.asarray(v) for n, v in inputs.items()}).items()}
    outputs = {"y": (T, D), "state_kT": (DA, TP), "state_v": (TP, DA)}
    nc = bacc.Bacc("TRN2", target_bir_lowering=False, num_devices=1)
    a = {n[3:]: nc.dram_tensor(n, v.shape, F32, kind="ExternalInput").ap() for n, v in arrays.items()}
    for n, shape in outputs.items():
        a[n] = nc.dram_tensor(f"out_{n}", shape, F32, kind="ExternalOutput").ap()
    build(nc, a)
    res = run_bass_kernel_spmd(nc, [arrays], core_ids=[0]).results[0]
    y = res["out_y"]
    state_k = res["out_state_kT"].reshape(1, 1, NH, HD, TP).transpose(0, 1, 2, 4, 3)
    state_v = res["out_state_v"].reshape(1, 1, TP, NH, HD).transpose(0, 1, 3, 2, 4)
    return y[None, :TP], y[None, TP:], np.ascontiguousarray(state_k), np.ascontiguousarray(state_v)
```

```python
from contextlib import ExitStack

import numpy as np
import concourse.bass as bass
from concourse import mybir

F32 = mybir.dt.float32
F32R = mybir.dt.float32r
U32 = mybir.dt.uint32
ALU = mybir.AluOpType
ACT = mybir.ActivationFunctionType
AX = mybir.AxisListType

D = 1024
KT = D // 128
TP, TS = 256, 1024
T = TP + TS
NTT = T // 128
DA = DH = 512
NH, HD = 8, 64
GW, WR, WC = 64, 8, 16
QC, KC = 16, 32
KR = 12
NWIN = KR * KC
NCTX = 256
NE, FF = 16, 2816
FT = FF // 128
CAP_S, CAP_P = 2 * TS // NE, 2 * TP // NE
CAP = CAP_S + CAP_P
EPS = 1e-6
NEG = -1e30
CH = 1024
NF = 20


class Phase:

    def __init__(self, nc, name):
        self.nc, self.name, self.stack, self.sems = nc, name, ExitStack(), []

    def __enter__(self):
        return self

    def __exit__(self, *exc):
        self.stack.__exit__(*exc)
        self.nc.clear_and_free_semaphores(self.sems)
        self.nc.all_engine_barrier()

    def sb(self, name, shape, dt=F32):
        return self.stack.enter_context(self.nc.sbuf_tensor(f"{self.name}_{name}", shape, dt))

    def ps(self, name, shape, dt=F32):
        return self.stack.enter_context(self.nc.psum_tensor(f"{self.name}_{name}", shape, dt))

    def sem(self, name):
        self.sems.append(self.nc.alloc_semaphore(f"{self.name}_{name}"))
        return self.sems[-1]

    def block(self):
        return self.stack.enter_context(self.nc.Block())


class Chain:

    def __init__(self, eng, sem, base=0):
        self.eng, self.sem, self.n, self.base = eng, sem, 0, base

    def __call__(self, ins):
        ins.then_inc(self.sem, 1)
        self.n += 1
        self.eng.wait_ge(self.sem, self.base + self.n)


class Stream:

    def __init__(self, ph, nr, ns, used, per=1):
        self.nr, self.ns, self.used, self.per = nr, ns, used, per
        self.raw = ph.sb("raw", [128, nr, CH])
        self.hi = ph.sb("hi", [128, ns, CH], F32R)
        self.lo = ph.sb("lo", [128, ns, CH], F32R)
        self.landed = [ph.sem(f"raw_landed{i}") for i in range(nr)]
        self.hi_done = ph.sem("hi_done")
        self.lo_done = ph.sem("lo_done")

    def start_pe(self, pe):
        pe.sem_inc(self.used, self.ns * self.per)

    def start_dve(self, dve):
        dve.sem_inc(self.lo_done, self.nr)

    def load(self, sp, base, c, src):
        sp.wait_ge(self.lo_done, base + c + 1)
        sp.dma_start(self.raw[:, c % self.nr, :], src).then_inc(self.landed[c % self.nr], 16)

    def split_hi(self, act, laps, base, c):
        act.wait_ge(self.landed[c % self.nr], (laps + c // self.nr) * 16 + 16)
        act.wait_ge(self.used, (base + c + 1) * self.per)
        act.activation(self.hi[:, c % self.ns, :], self.raw[:, c % self.nr, :], ACT.Copy).then_inc(self.hi_done, 1)

    def split_lo(self, dve, base, c):
        dve.wait_ge(self.hi_done, base + c + 1)
        dve.tensor_tensor(self.lo[:, c % self.ns, :], self.raw[:, c % self.nr, :],
                          self.hi[:, c % self.ns, :].bitcast(F32), ALU.subtract).then_inc(self.lo_done, 1)

    def ready(self, pe, base, c):
        pe.wait_ge(self.lo_done, base + c + 1 + self.nr)

    def tile(self, part, c, j, n=128):
        return part[:, c % self.ns, j * n:(j + 1) * n]


def projection(nc, a, g):
    NS = 5
    GRP = [(0, 2), (2, 4), (6, 4)]
    BLK = [(0, 512), (512, 512), (1024, 256)]
    with Phase(nc, "proj") as ph:
        s_mm = ph.sem("mm")
        st = Stream(ph, NS, NS, s_mm, 3)
        M0 = 3 * NS
        xr = ph.sb("xr", [128, NTT, D])
        hh = ph.sb("hh", [128, KT, T], F32R)
        hl = ph.sb("hl", [128, KT, T], F32R)
        junk = ph.sb("junk", [128, D])
        ss = ph.sb("ss", [128, NTT])
        rr = ph.sb("rr", [128, NTT])
        r2 = ph.sb("r2", [128, NTT])
        root = ph.sb("root", [128, NTT])
        bank = [ph.ps(f"bank{i}", [128, 512]) for i in range(8)]
        s_x = [ph.sem(f"x_landed{i}") for i in range(NTT)]
        s_ss, s_sq, s_r, s_xs = ph.sem("ss"), ph.sem("sqrt"), ph.sem("rstd"), ph.sem("xs")
        s_tr, s_h, s_hh, s_hl = ph.sem("tr"), ph.sem("h"), ph.sem("hh"), ph.sem("hl")
        s_evd, s_eva = ph.sem("ev_dve"), ph.sem("ev_act")
        s_st = [ph.sem(f"stored{i}") for i in range(2)]
        s_vmm, s_vev = ph.sem("vmm"), ph.sem("vev")
        s_vst = [ph.sem(f"vstored{i}") for i in range(2)]
        s_fin = ph.sem("fin")
        block = ph.block()
        tmp = [junk[:, 0:512], junk[:, 512:1024]]
        stage = [xr[:, 2:4, :].rearrange("p a b -> p (a b)")[:, 0:T], xr[:, 4:6, :].rearrange("p a b -> p (a b)")[:, 0:T]]
        vstage = [xr[:, 6, 0:512], xr[:, 7, 0:512]]
        NIT = 2
        CPI = NF // NIT

        @block.sync
        def _(sp):
            for t in range(NTT):
                sp.dma_start(xr[:, t, :], a["x"][t * 128:(t + 1) * 128, :]).then_inc(s_x[t], 16)
            for s in s_st:
                sp.sem_inc(s, 16)
            for c in range(4):
                st.load(sp, 0, c, a["w_in"][c])
            with sp.Fori(0, NIT) as i:
                for c in range(CPI):
                    n = i * CPI + c
                    st.load(sp, i * CPI, c + 4, a["w_in"][bass.ds(n + 4, 1)].rearrange("a p f -> p (a f)"))
                    sp.wait_ge(s_evd, n + 3)
                    sp.wait_ge(s_eva, n * 2 + 6)
                    sp.dma_start(g["QKH"][bass.ds(n * 128, 128), :], stage[c % 2]).then_inc(s_st[c % 2], 16)
            for b in range(2):
                sp.wait_ge(s_st[b], 16 * (NF // 2 + 1))

        @block.gpsimd
        def _(pool):
            for t in range(NTT):
                pool.wait_ge(s_vev, t + 1)
                pool.dma_start(g["V"][t * 128:(t + 1) * 128, :], vstage[t % 2]).then_inc(s_vst[t % 2], 16)
            for b in range(2):
                pool.wait_ge(s_st[b], 16 * (NF // 2 + 1))
                pool.wait_ge(s_vst[b], 16 * (NTT // 2))
            pool.dma_start(a["state_kT"], g["QKH"][512:1024, 0:TP]).then_inc(s_fin, 16)
            pool.dma_start(a["state_v"], g["V"][0:TP, :]).then_inc(s_fin, 16)
            pool.wait_ge(s_fin, 32)

        @block.scalar
        def _(act):
            for t in range(NTT):
                act.wait_ge(s_x[t], 16)
                if t:
                    act.wait_ge(s_ss, t)
                act.activation(junk[:], xr[:, t, :], ACT.Square, accum_out=ss[:, t:t + 1]).then_inc(s_ss, 1)
            act.wait_ge(s_r, 1)
            act.activation(root[:], r2[:], ACT.Sqrt).then_inc(s_sq, 1)
            for q, (t0, nt) in enumerate(GRP):
                c = 1 if q == 0 else 0
                for k in range(KT):
                    n = q * KT + k
                    act.wait_ge(s_tr, n + 1)
                    if n >= 2:
                        act.wait_ge(s_hl, n - 1)
                    act.activation(tmp[n % 2][:, 0:nt * 128], bank[n % 8][:, 0:nt * 128], ACT.Identity,
                                   bias=g["mod"][:, k, c:c + 1], scale=g["gmod"][:, c, k:k + 1]).then_inc(s_h, 1)
                    act.wait_ge(s_h, n + 1)
                    act.activation(hh[:, k, t0 * 128:(t0 + nt) * 128], tmp[n % 2][:, 0:nt * 128], ACT.Copy).then_inc(s_hh, 1)
            act.sem_inc(s_eva, 4)
            for c in range(2):
                st.split_hi(act, 0, 0, c)
            with act.Fori(0, NIT) as i:
                for c in range(CPI):
                    n = i * CPI + c
                    st.split_hi(act, i * (CPI // NS), i * CPI, c + 2)
                    act.wait_ge(s_st[c % 2], (i * (CPI // 2) + c // 2 + 1) * 16)
                    for b in (1, 2):
                        c0, w = BLK[b]
                        act.wait_ge(s_mm, n * 3 + b + 1 + M0)
                        act.activation(stage[c % 2][:, c0:c0 + w], bank[(c % 2) * 3 + b][:, 0:w], ACT.Copy).then_inc(s_eva, 1)
            for c in range(2, 4):
                st.split_hi(act, NF // NS, NF, c)

        @block.vector
        def _(dve):
            st.start_dve(dve)
            dve.wait_ge(s_ss, NTT)
            dve.tensor_scalar(rr[:], ss[:], 1.0 / D, EPS, ALU.mult, ALU.add).then_inc(s_xs, 1)
            dve.wait_ge(s_xs, 1)
            dve.reciprocal(r2[:], rr[:]).then_inc(s_r, 1)
            dve.wait_ge(s_sq, 1)
            dve.tensor_tensor(r2[:], root[:], root[:], ALU.mult).then_inc(s_xs, 1)
            dve.wait_ge(s_xs, 2)
            dve.tensor_tensor(r2[:], r2[:], rr[:], ALU.mult).then_inc(s_xs, 1)
            dve.wait_ge(s_xs, 3)
            dve.tensor_scalar(r2[:], r2[:], -0.5, 1.5, ALU.mult, ALU.add).then_inc(s_xs, 1)
            dve.wait_ge(s_xs, 4)
            dve.tensor_tensor(rr[:], root[:], r2[:], ALU.mult).then_inc(s_xs, 1)
            dve.wait_ge(s_xs, 5)
            for t in range(NTT):
                dve.tensor_scalar(xr[:, t, :], xr[:, t, :], rr[:, t:t + 1], None, ALU.mult).then_inc(s_xs, 1)
            for q, (t0, nt) in enumerate(GRP):
                for k in range(KT):
                    n = q * KT + k
                    dve.wait_ge(s_hh, n + 1)
                    dve.tensor_tensor(hl[:, k, t0 * 128:(t0 + nt) * 128], tmp[n % 2][:, 0:nt * 128],
                                      hh[:, k, t0 * 128:(t0 + nt) * 128].bitcast(F32), ALU.subtract).then_inc(s_hl, 1)
            dve.sem_inc(s_evd, 2)
            for c in range(2):
                st.split_lo(dve, 0, c)
            with dve.Fori(0, NIT) as i:
                for c in range(CPI):
                    n = i * CPI + c
                    st.split_lo(dve, i * CPI, c + 2)
                    dve.wait_ge(s_st[c % 2], (i * (CPI // 2) + c // 2 + 1) * 16)
                    dve.wait_ge(s_mm, n * 3 + 1 + M0)
                    dve.tensor_copy(stage[c % 2][:, 0:512], bank[(c % 2) * 3][:, :]).then_inc(s_evd, 1)
            for c in range(2, 4):
                st.split_lo(dve, NF, c)
            for t in range(NTT):
                if t >= 2:
                    dve.wait_ge(s_vst[t % 2], 16 * (t // 2))
                dve.wait_ge(s_vmm, t + 1)
                dve.tensor_copy(vstage[t % 2], bank[6 + t % 2][:, :]).then_inc(s_vev, 1)

        @block.tensor
        def _(pe):
            st.start_pe(pe)
            for q, (t0, nt) in enumerate(GRP):
                for k in range(KT):
                    n = q * KT + k
                    if k == 0:
                        pe.wait_ge(s_xs, 5 + t0 + nt)
                    if n >= 8:
                        pe.wait_ge(s_h, n - 7)
                    for j in range(nt):
                        tr = pe.transpose(bank[n % 8][:, j * 128:(j + 1) * 128], xr[:, t0 + j, k * 128:(k + 1) * 128],
                                          g["ident"][:])
                    tr.then_inc(s_tr, 1)
            pe.wait_ge(s_hl, 3 * KT)
            pe.wait_ge(s_h, 3 * KT)
            with pe.Fori(0, NIT) as i:
                for c in range(CPI):
                    n = i * CPI + c
                    st.ready(pe, i * CPI, c)
                    for b, (c0, w) in enumerate(BLK):
                        pe.wait_ge(s_evd if b == 0 else s_eva, n + 1 if b == 0 else n * 2 + b)
                        out = bank[(c % 2) * 3 + b][:, 0:w]
                        for k in range(KT):
                            whi, wlo = st.tile(st.hi, c, k), st.tile(st.lo, c, k)
                            pe.matmul(out, whi, hh[:, k, c0:c0 + w], start=(k == 0), stop=False)
                            pe.matmul(out, whi, hl[:, k, c0:c0 + w], start=False, stop=False)
                            mm = pe.matmul(out, wlo, hh[:, k, c0:c0 + w], start=False, stop=(k == KT - 1))
                        mm.then_inc(s_mm, 1)
            st.ready(pe, NF, 3)
            for t in range(NTT):
                if t >= 2:
                    pe.wait_ge(s_vev, t - 1)
                out = bank[6 + t % 2][:, :]
                for k in range(KT):
                    xh, xl = hh[:, k, t * 128:(t + 1) * 128], hl[:, k, t * 128:(t + 1) * 128]
                    whi, wlo = st.tile(st.hi, k // 2, k % 2, 512), st.tile(st.lo, k // 2, k % 2, 512)
                    pe.matmul(out, xh, whi, start=(k == 0), stop=False)
                    pe.matmul(out, xh, wlo, start=False, stop=False)
                    mm = pe.matmul(out, xl, whi, start=False, stop=(k == KT - 1))
                mm.then_inc(s_vmm, 1)




def rstd_vector(dve, chain, s_root, root, ss, out, tmp, n):
    chain(dve.tensor_scalar(out, ss, 1.0 / n, EPS, ALU.mult, ALU.add))
    dve.reciprocal(tmp, out).then_inc(s_root, 1)
    dve.wait_ge(s_root, 2)
    chain(dve.tensor_tensor(tmp, root, root, ALU.mult))
    chain(dve.tensor_tensor(tmp, tmp, out, ALU.mult))
    chain(dve.tensor_scalar(tmp, tmp, -0.5, 1.5, ALU.mult, ALU.add))
    chain(dve.tensor_tensor(out, root, tmp, ALU.mult))


def rstd_scalar(act, s_root, root, tmp):
    act.wait_ge(s_root, 1)
    act.activation(root, tmp, ACT.Sqrt).then_inc(s_root, 1)


BLK_START = [min(max(j * QC - WC // 2, 0), GW - KC) for j in range(GW // QC)]


def attention(nc, a, g):
    NT = 2 * NTT
    with Phase(nc, "attn") as ph:
        q, k = ph.sb("q", [128, 2, T]), ph.sb("k", [128, 2, T])
        ck = ph.sb("ck", [128, 2, NCTX])
        qsc = ph.sb("qsc", [128, T])
        qs = ph.sb("qs", [128, 2, T], F32R)
        kh, kl = (ph.sb(n, [128, 2, T], F32R) for n in ("kh", "kl"))
        ckh, ckl = (ph.sb(n, [128, 2, NCTX], F32R) for n in ("ckh", "ckl"))
        bias = ph.sb("bias", [128, 2, 8, NWIN])
        vw = ph.sb("vw", [128, 4, 4, DA])
        vc = ph.sb("vc", [128, 2, DA])
        vp = ph.sb("vp", [128, 2, DA])
        sw = ph.sb("sw", [128, 2, NWIN])
        p = ph.sb("p", [128, 2, NWIN + NCTX])
        pt = ph.sb("pt", [128, 2, NWIN + NCTX])
        mx = ph.sb("mx", [128, 2, 2])
        nm = ph.sb("nm", [128, 2])
        neg1 = ph.sb("neg1", [128, 1])
        l = ph.sb("l", [128, 4, 2])
        ls = ph.sb("ls", [128, 1])
        li = ph.sb("li", [128, 1])
        ar = ph.sb("ar", [128, NTT, DA])
        at = ph.sb("at", [128, 4, T])
        ss, rr, r2, root = (ph.sb(x, [128, NTT]) for x in ("ss", "rr", "r2", "root"))
        psw = [ph.ps(f"psw{b}", [128, 512]) for b in range(2)]
        psc = [ph.ps(f"psc{b}", [128, 512]) for b in range(2)]
        ptw = ph.ps("ptw", [128, 512])
        ptc = ph.ps("ptc", [128, 512])
        po = [ph.ps(f"po{b}", [128, 512]) for b in range(2)]
        s_v = ph.sem("v_landed")
        s_head = [ph.sem(f"head_landed{u}") for u in range(2)]
        s_q, s_s, s_am, s_exp = ph.sem("q_scaled"), ph.sem("scores"), ph.sem("max"), ph.sem("exp")
        s_t, s_ptw, s_ptc = ph.sem("transposed"), ph.sem("win_copied"), ph.sem("ctx_copied")
        s_pv, s_norm, s_dve = ph.sem("pv"), ph.sem("normed"), ph.sem("dve_steps")
        s_ss, s_root, s_rows = ph.sem("ss"), ph.sem("root"), ph.sem("rows")
        s_tr, s_atd, s_ata, s_out = ph.sem("tr"), ph.sem("at_dve"), ph.sem("at_act"), ph.sem("out")
        s_neg = ph.sem("neg1")
        s_hi, s_lo = ph.sem("head_hi"), ph.sem("head_lo")
        block = ph.block()

        def tiles():
            return [(u * NTT + t, u, t) for u in range(2) for t in range(NTT)]

        def keys(t):
            if t < 2:
                return [(NWIN + 128 * c, ("p", c)) for c in range(2)]
            half, j = divmod(t - 2, 4)
            return [(128 * c, ("w", half + c, j)) for c in range(3)] + [(NWIN + 128 * c, ("c", c)) for c in range(2)]

        @block.sync
        def _(sp):
            with sp.Fori(0, NH // 2) as i:
                for u in range(2):
                    sp.wait_ge(s_pv, i * NT + u * NTT + NTT)
                    row = i * 128 + u * 64
                    for half in (slice(0, 64), slice(64, 128)):
                        sp.dma_start(q[half, u, :], g["QKH"][bass.ds(row, 64), :]).then_inc(s_head[u], 16)
                        sp.dma_start(k[half, u, :], g["QKH"][bass.ds(row + DA, 64), :]).then_inc(s_head[u], 16)
                        sp.dma_start(ck[half, u, :], a["cache_kT"][bass.ds(row, 64), :]).then_inc(s_head[u], 16)
                    sp.dma_start(bias[:, u, :, :].rearrange("p a b -> p (a b)"),
                                 a["bias"][bass.ds(i * 256 + u * 128, 128), :]).then_inc(s_head[u], 16)
            sp.wait_ge(s_atd, 2 * NTT)
            sp.wait_ge(s_ata, 2 * NTT)
            for f in range(4):
                sp.dma_start(g["MIXT"][f * 128:(f + 1) * 128, :], at[:, f, :]).then_inc(s_out, 16)
            sp.wait_ge(s_out, 64)

        @block.gpsimd
        def _(pool):
            vs = g["V"][TP:T, :].rearrange("(rg r c) f -> r c rg f", r=4, c=GW)
            pool.dma_start(vp[:], g["V"][0:TP, :].rearrange("(c p) f -> p c f", p=128)).then_inc(s_v, 16)
            pool.dma_start(vc[:], a["cache_v"]).then_inc(s_v, 16)
            for r in range(4):
                for j in range(4):
                    pool.dma_start(vw[32 * r:32 * r + 32, :, j, :], vs[r, BLK_START[j]:BLK_START[j] + KC]).then_inc(s_v, 16)
            pool.wait_ge(s_v, 16 * 18)

        @block.tensor
        def _(pe):
            pe.sem_inc(s_pv, NT)

            def scores(i, n, u, t):
                if t == 0:
                    pe.wait_ge(s_lo, i * 2 + u + 1)
                qv = qs[:, u, t * 128:(t + 1) * 128]
                if t < 2:
                    for x, kx in enumerate((kh, kl)):
                        mm = pe.matmul(psc[n % 2][:, 0:NCTX], qv, kx[:, u, 0:TP], start=(x == 0), stop=(x == 1))
                    mm.then_inc(s_s, 1)
                    return
                half, j = divmod(t - 2, 4)
                for x, kx in enumerate((kh, kl)):
                    kv = kx[:, u, TP:T].rearrange("d (r c) -> d r c", c=GW)[:, half * 4:half * 4 + KR,
                                                                           BLK_START[j]:BLK_START[j] + KC]
                    pe.matmul(psw[n % 2][:, 0:NWIN], qv, kv, start=(x == 0), stop=(x == 1))
                for x, kx in enumerate((ckh, ckl)):
                    mm = pe.matmul(psc[n % 2][:, 0:NCTX], qv, kx[:, u, :], start=(x == 0), stop=(x == 1))
                mm.then_inc(s_s, 1)

            def transposes(i, n, t):
                pe.wait_ge(s_exp, i * NT + n + 1)
                for col, _ in keys(t):
                    out = ptw[:, col:col + 128] if col < NWIN else ptc[:, col - NWIN:col - NWIN + 128]
                    tr = pe.transpose(out, p[:, n % 2, col:col + 128], g["ident"][:])
                tr.then_inc(s_t, 1)

            def values(i, n, u, t):
                if t >= 2:
                    pe.wait_ge(s_ptw, i * 16 + u * 8 + t - 1)
                pe.wait_ge(s_ptc, i * NT + n + 1)
                pe.wait_ge(s_norm, i * NT + n + 1)
                ks = keys(t)
                if n == 0:
                    pe.wait_ge(s_v, 16 * 18)
                for x, (col, v) in enumerate(ks):
                    vt = {"p": vp[:, v[1], :], "c": vc[:, v[1], :]}[v[0]] if v[0] != "w" else vw[:, v[1], v[2], :]
                    mm = pe.matmul(po[n % 2][:, 0:HD], pt[:, n % 2, col:col + 128],
                                   vt[:, bass.ds(i * 128 + u * 64, HD)], start=(x == 0), stop=(x == len(ks) - 1))
                mm.then_inc(s_pv, 1)

            with pe.Fori(0, NH // 2) as i:
                ts = tiles()
                scores(i, *ts[0])
                for n, u, t in ts:
                    if n + 1 < NT:
                        scores(i, *ts[n + 1])
                    if n:
                        values(i, *ts[n - 1])
                    transposes(i, n, t)
                values(i, *ts[-1])
            for t in range(NTT):
                pe.wait_ge(s_rows, t + 1)
                if t >= 2:
                    pe.wait_ge(s_atd, 2 * (t - 1))
                    pe.wait_ge(s_ata, 2 * (t - 1))
                for f in range(4):
                    out = (psw if f < 2 else psc)[t % 2][:, f % 2 * 128:f % 2 * 128 + 128]
                    tr = pe.transpose(out, ar[:, t, f * 128:(f + 1) * 128], g["ident"][:])
                tr.then_inc(s_tr, 1)

        def at_out(f, t):
            if t < 2:
                return at[:, f, t * 128:(t + 1) * 128]
            half, j = divmod(t - 2, 4)
            return at[:, f, TP:T].rearrange("p (r c) -> p r c", c=GW)[:, half * 8:half * 8 + 8, j * QC:(j + 1) * QC]

        def at_in(f, t):
            x = (psw if f < 2 else psc)[t % 2][:, f % 2 * 128:f % 2 * 128 + 128]
            return x if t < 2 else x.rearrange("p (r c) -> p r c", c=QC)

        @block.vector
        def _(dve):
            dve.sem_inc(s_norm, 2)
            dve.memset(neg1[:], -1.0).then_inc(s_neg, 1)
            dve.wait_ge(s_neg, 1)
            with dve.Fori(0, NH // 2) as i:
                PER = 2 * (2 * 2 + 8 * 3)
                chain = Chain(dve, s_dve, i * PER)

                def prepare(u):
                    dve.wait_ge(s_head[u], i * 112 + 112)
                    dve.tensor_scalar(qsc[:, 0:TP], q[:, u, 0:TP], HD ** -0.5, None, ALU.mult)
                    for h in range(2):
                        c0 = TP + h * 512
                        ins = dve.tensor_scalar(qsc[:, c0:c0 + 512].rearrange("d (j r c) -> d j r c", r=8, c=QC),
                                                q[:, u, c0:c0 + 512].rearrange("d (r j c) -> d j r c", r=8, c=QC),
                                                HD ** -0.5, None, ALU.mult)
                    ins.then_inc(s_q, 1)
                    dve.wait_ge(s_hi, i * 4 + u * 2 + 1)
                    dve.tensor_tensor(kl[:, u, :], k[:, u, :], kh[:, u, :].bitcast(F32), ALU.subtract)
                    dve.tensor_tensor(ckl[:, u, :], ck[:, u, :], ckh[:, u, :].bitcast(F32), ALU.subtract)
                    dve.wait_ge(s_hi, i * 4 + u * 2 + 2)
                    dve.tensor_tensor(qs[64:128, u, :], qsc[64:128, :], qs[64:128, u, :].bitcast(F32),
                                      ALU.subtract).then_inc(s_lo, 1)

                def add_max(n, u, t):
                    dve.wait_ge(s_s, i * NT + n + 1)
                    if t < 2:
                        chain(dve.tensor_reduce(mx[:, n % 2, 0:1], psc[n % 2][:, 0:NCTX], AX.X, ALU.max))
                        dve.tensor_scalar(nm[:, n % 2:n % 2 + 1], mx[:, n % 2, 0:1], -1.0, None, ALU.mult).then_inc(s_am, 1)
                        return
                    dve.tensor_reduce(mx[:, n % 2, 1:2], psc[n % 2][:, 0:NCTX], AX.X, ALU.max)
                    chain(dve.tensor_tensor_reduce(sw[:, n % 2, :], psw[n % 2][:, 0:NWIN], bias[:, u, t - 2, :], 1.0,
                                                   3 * NEG, ALU.add, ALU.max, mx[:, n % 2, 0:1]))
                    dve.scalar_tensor_tensor(nm[:, n % 2:n % 2 + 1], mx[:, n % 2, 0:1], mx[:, n % 2, 1:2], neg1[:],
                                             ALU.max, ALU.mult).then_inc(s_am, 1)

                def copy_win(n, u, t):
                    if t >= 2:
                        dve.wait_ge(s_t, i * NT + n + 1)
                        dve.tensor_copy(pt[:, n % 2, 0:NWIN], ptw[:, 0:NWIN]).then_inc(s_ptw, 1)

                def norm(n, u, t):
                    dve.wait_ge(s_pv, i * NT + n + 1 + NT)
                    if t < 2:
                        chain(dve.reciprocal(li[:], l[:, n % 4, 1:2]))
                    else:
                        chain(dve.tensor_tensor(ls[:], l[:, n % 4, 0:1], l[:, n % 4, 1:2], ALU.add))
                        chain(dve.reciprocal(li[:], ls[:]))
                    dve.tensor_scalar(ar[:, t, bass.ds(i * 128 + u * 64, HD)], po[n % 2][:, 0:HD], li[:], None,
                                      ALU.mult).then_inc(s_norm, 1)

                ts = tiles()
                prepare(0)
                add_max(*ts[0])
                for n, u, t in ts:
                    if n + 1 < NT:
                        add_max(*ts[n + 1])
                    if n == 6:
                        prepare(1)
                    copy_win(n, u, t)
                    if n:
                        norm(*ts[n - 1])
                norm(*ts[-1])
                assert chain.n == PER
            dve.wait_ge(s_ss, NTT)
            rchain = Chain(dve, s_neg, 1)
            rstd_vector(dve, rchain, s_root, root[:], ss[:], rr[:], r2[:], DA)
            for t in range(NTT):
                dve.tensor_scalar(ar[:, t, :], ar[:, t, :], rr[:, t:t + 1], None, ALU.mult).then_inc(s_rows, 1)
            for t in range(NTT):
                dve.wait_ge(s_tr, t + 1)
                for f in range(2):
                    dve.tensor_scalar(at_out(f, t), at_in(f, t), g["gains"][:, 16 + f:17 + f], None, ALU.mult).then_inc(s_atd, 1)

        @block.scalar
        def _(act):
            with act.Fori(0, NH // 2) as i:
                def exps(n, u, t):
                    act.wait_ge(s_am, i * NT + n + 1)
                    nb = nm[:, n % 2:n % 2 + 1]
                    if t >= 2:
                        act.activation(p[:, n % 2, 0:NWIN], sw[:, n % 2, :], ACT.Exp, bias=nb, accum_out=l[:, n % 4, 0:1])
                    act.activation(p[:, n % 2, NWIN:], psc[n % 2][:, 0:NCTX], ACT.Exp, bias=nb,
                                   accum_out=l[:, n % 4, 1:2]).then_inc(s_exp, 1)

                def copy_ctx(n, u, t):
                    act.wait_ge(s_t, i * NT + n + 1)
                    act.activation(pt[:, n % 2, NWIN:], ptc[:, 0:NCTX], ACT.Copy).then_inc(s_ptc, 1)

                def prepare(u):
                    act.wait_ge(s_head[u], i * 112 + 112)
                    act.activation(kh[:, u, :], k[:, u, :], ACT.Copy)
                    act.activation(ckh[:, u, :], ck[:, u, :], ACT.Copy).then_inc(s_hi, 1)
                    act.wait_ge(s_q, i * 2 + u + 1)
                    act.activation(qs[:, u, :], qsc[:], ACT.Copy).then_inc(s_hi, 1)

                ts = tiles()
                prepare(0)
                exps(*ts[0])
                for n, u, t in ts:
                    if n + 1 < NT:
                        exps(*ts[n + 1])
                    if n == 6:
                        prepare(1)
                    copy_ctx(n, u, t)
            act.wait_ge(s_norm, NH * NTT + 2)
            for t in range(NTT):
                if t:
                    act.wait_ge(s_ss, t)
                act.activation(p[:, 0, 0:DA], ar[:, t, :], ACT.Square, accum_out=ss[:, t:t + 1]).then_inc(s_ss, 1)
            rstd_scalar(act, s_root, root[:], r2[:])
            for t in range(NTT):
                act.wait_ge(s_tr, t + 1)
                for f in range(2, 4):
                    act.activation(at_out(f, t), at_in(f, t), ACT.Copy, scale=g["gains"][:, 16 + f:17 + f]).then_inc(s_ata, 1)


TWO_PI_HI = 6.28125
TWO_PI_MID = 0.0019353071693331003
TWO_PI_LO = 1.0253131677018246e-11
MAGIC = 12582912.0


def filter_jobs(MT):
    jobs = []
    for par in range(2):
        for f in range(MT):
            jobs += [("cos", par, f), ("sin", par, f)]
    return jobs + [("cosx", 0, 0)]


def filters(nc, a, g, s, L, ada):
    M = L // 2
    MT = M // 128
    NZ = 2 * M + 2
    JOBS = filter_jobs(MT)
    NCK = (len(JOBS) * MT * 128 + CH - 1) // CH
    PC = 8 // MT if MT > 1 else 8
    TB = [(c, min(512, NZ - c)) for c in range(0, NZ, 512)]
    NB = len(TB)
    with Phase(nc, f"filt{s}") as ph:
        st = Stream(ph, 3, 3, ph.sem("chunk_used"))
        w1 = ph.sb("w1", [33, 64])
        w2 = ph.sb("w2", [64, 64])
        w3 = ph.sb("w3", [64, 4 * DH])
        fb = ph.sb("fb", [64, 3])
        hid = ph.sb("hid", [64, NZ])
        win = ph.sb("win", [128, 2, 2, DH])
        wmid = ph.sb("wmid", [1, DH])
        sgn = ph.sb("sgn", [1, 128])
        rowf = ph.sb("rowf", [128, 3])
        F = ph.sb("F", [128, 2, 4, DH])
        AB = ph.sb("AB", [128, 4, DH])
        ABm = ph.sb("ABm", [128, 4, DH])
        AA = ph.sb("AA", [128, 4, DH])
        y, kk, z = (t[0:n].rearrange("p a b -> p (a b)")[:, 0:NZ] for t, n in ((AB, 64), (ABm, 64), (AA, 33)))
        opnd_h = ph.sb("opnd_h", [128, MT, 4, DH], F32R)
        opnd_l = ph.sb("opnd_l", [128, MT, 4, DH], F32R)
        mid = ph.sb("mid", [1, 4, DH])
        rn = ph.sb("rn", [128, DH])
        skip = ph.sb("skip", [128, DH])
        spec = ph.sb("spec", [128, 2, DH])
        pf = [ph.ps(f"pf{b}", [128, 512]) for b in range(4)]
        pk = [ph.ps(f"pk{b}", [128, 512]) for b in range(2)]
        pn = ph.ps("pn", [128, 512])
        pm = ph.ps("pm", [128, 512])
        s_in, s_h, s_dve, s_sin = ph.sem("in_landed"), ph.sem("hidden_mm"), ph.sem("dve_steps"), ph.sem("sin")
        s_y = ph.sem("y_ready")
        s_win = [ph.sem(f"win_landed{b}") for b in range(2)]
        s_f, s_F, s_AB, s_pool, s_ab = ph.sem("filt_mm"), ph.sem("windowed"), ph.sem("ab_ready"), ph.sem("mixed"), ph.sem("mid_abs")
        s_abs, s_sum = ph.sem("abs_ready"), ph.sem("abs_summed")
        s_oh, s_ol, s_n, s_rn = ph.sem("opnd_hi"), ph.sem("opnd_lo"), ph.sem("norm_mm"), ph.sem("rnorm")
        s_mid, s_midv = ph.sem("mid_mm"), ph.sem("mid_ready")
        s_k = ph.sem("spec_mm")
        s_ev, s_skip = ph.sem("spec_ready"), ph.sem("skip_landed")
        s_st = [ph.sem(f"stored{b}") for b in range(2)]
        NA, RA = (24, 3) if ada else (0, 0)
        HIDDEN = 3 if ada else 0
        BUILD = 1 if ada else 0
        JOB = (NA - 2 * HIDDEN - 2 * MT * BUILD) // 2
        if ada:
            wa = ph.sb("wa", [128, RA, KT * 256])
            cond, sc, bada = ph.sb("cond", [128, KT, 2]), ph.sb("sc", [128, KT, 2]), ph.sb("bada", [128, 48])
            rows2 = ph.sb("rows2", [2, 256])
            rows48, rows16 = (AA[0:n, x, 0:256].rearrange("p (c n) -> p c n", c=2) for x, n in enumerate((48, 16)))
            s_wa = [ph.sem(f"wada_landed{b}") for b in range(RA)]
            s_silu, s_adm, s_ade, s_mod = ph.sem("silu"), ph.sem("ada_mm"), ph.sem("ada_out"), ph.sem("mod_steps")
            s_tr, s_rows, s_out = ph.sem("rows_transposed"), ph.sem("rows_ready"), ph.sem("rows_stored")

        def ada_bank(n):
            o, x = divmod(n - 2 * HIDDEN, MT * BUILD + JOB)
            if n == NA:
                return pf[n % 4]
            return pk[n % 2] if n < 2 * HIDDEN or x < MT * BUILD else pf[n % 4]

        class Ada:

            def __init__(self, step):
                self.n, self.step = 0, step

            def __call__(self, count):
                for _ in range(count):
                    self.step(self.n)
                    self.n += 1

        def ada_load(sp, n):
            if n < NA:
                if n >= RA:
                    sp.wait_ge(s_adm, n - RA + 1)
                sp.dma_start(wa[:, n % RA, :], a["w_ada"][n]).then_inc(s_wa[n % RA], 16)

        def ada_products(pe, n):
            if n:
                pe.wait_ge(s_ade, n)
                for f in range(2):
                    tr = pe.transpose(ada_bank(n)[:, 256 + 2 * f:258 + 2 * f], rows2[:, f * 128:(f + 1) * 128],
                                      g["ident"][0:2, 0:2])
                if n == NA:
                    tr.then_inc(s_adm, 1)
                    return
            else:
                pe.wait_ge(s_silu, 1)
            pe.wait_ge(s_wa[n % RA], 16 * (n // RA + 1))
            for k in range(KT):
                mm = pe.matmul(ada_bank(n)[0:2, 0:256], sc[:, k, :], wa[:, n % RA, k * 256:(k + 1) * 256],
                               start=(k == 0), stop=(k == KT - 1))
            mm.then_inc(s_adm, 1)

        def ada_out(dve, n):
            dve.wait_ge(s_adm, n + 1)
            if n:
                for c in range(2):
                    ins = dve.tensor_tensor(g["mod"][:, 2 * n - 2:2 * n, c], ada_bank(n)[:, 256 + c:260:2],
                                            bada[:, 2 * n - 2:2 * n], ALU.add)
            if n < NA:
                ins = dve.tensor_copy(rows2[:], ada_bank(n)[0:2, 0:256])
            ins.then_inc(s_ade, 1)

        NIN = 16 * (12 if ada else 8)
        block = ph.block()
        NJ = len(JOBS)

        @block.sync
        def _(sp):
            sp.dma_start(z, a[f"z_{s}"]).then_inc(s_in, 16)
            for dst, name in ((w1, "filt_w1"), (w2, "filt_w2"), (w3, "filt_w3"), (fb, "filt_b"), (wmid, f"wmid_{s}"),
                              (sgn, "sgn"), (rowf, f"rowf_{s}")):
                sp.dma_start(dst[:], a[name]).then_inc(s_in, 16)
            if ada:
                for dst, src in ((cond, "cond"), (bada, "bada"), (g["gains"], "gains"), (g["ident"], "ident")):
                    sp.dma_start(dst[:], a[src]).then_inc(s_in, 16)
            for n in range(RA):
                ada_load(sp, n)
            ada_next = Ada(lambda n: ada_load(sp, n + RA))
            for o in range(2):
                sp.dma_start(skip[:], a["hyena_bias"][o:o + 1, :].to_broadcast([128, DH])).then_inc(s_skip, 16)
                for c in range(min(3, NCK)):
                    st.load(sp, 0, o * NCK + c, a[f"kbasis_{s}"][c])
                if o == 0:
                    ada_next(2 * HIDDEN)
                for t in range(MT):
                    n = o * MT + t
                    if n >= 2:
                        sp.wait_ge(s_F, (n - 1))
                    sp.dma_start(win[:, n % 2], a[f"win_{s}"][t]).then_inc(s_win[n % 2], 16)
                    if t:
                        ada_next(BUILD)
                ada_next(BUILD)
                for ji, (kind, par, f) in enumerate(JOBS):
                    if ji % PC == 0 and ji // PC + 3 < NCK:
                        st.load(sp, 0, o * NCK + ji // PC + 3, a[f"kbasis_{s}"][ji // PC + 3])
                    job = o * NJ + ji
                    sp.wait_ge(s_ev, job + 1)
                    slot = {"cos": 0, "sin": 1, "cosx": 2}[kind]
                    sp.dma_start(g[f"K{s}"][o, par * MT + f, slot], spec[:, job % 2, :]).then_inc(s_st[job % 2], 16)
                    ada_next(ji < JOB)
            for b in range(2):
                sp.wait_ge(s_st[b], 16 * NJ)
            if ada:
                sp.wait_ge(s_rows, 1)
                for c in range(2):
                    sp.dma_start(g["MODR"][c].rearrange("(f p) -> f p", p=128), rows48[:, c, :]).then_inc(s_out, 16)
                    sp.dma_start(g["GMODR"][c].rearrange("(f p) -> f p", p=128), rows16[:, c, :]).then_inc(s_out, 16)
                sp.wait_ge(s_out, 64)

        @block.tensor
        def _(pe):
            st.start_pe(pe)
            pe.wait_ge(s_in, NIN)
            ada_next = Ada(lambda n: ada_products(pe, n))
            for layer in range(2):
                for b, (c0, w) in enumerate(TB):
                    if layer:
                        pe.wait_ge(s_sin, 1)
                    pe.matmul(pf[b][0:64, 0:w], (w2 if layer else w1)[:], (hid if layer else z)[:, c0:c0 + w],
                              start=True, stop=True).then_inc(s_h, 1)
                ada_next(HIDDEN)
            pe.wait_ge(s_sin, 2)
            job = 0

            def sum_abs(o, t):
                pe.wait_ge(s_abs, o * MT + t + 1)
                if o and t == 0:
                    pe.wait_ge(s_rn, 1)
                for x in range(4):
                    mm = pe.matmul(pn[:], g["ones"][:], AA[:, x, :], start=(t == 0 and x == 0), stop=False)
                mm.then_inc(s_sum, 1)

            for o in range(2):
                if ada and o:
                    pe.wait_ge(s_ade, ada_next.n)
                for t in range(MT):
                    n = o * MT + t
                    if n:
                        pe.wait_ge(s_F, n)
                    for x in range(4):
                        d, m = x % 2, x // 2
                        mm = pe.matmul(pf[x][:], hid[:, m * M + t * 128:m * M + t * 128 + 128],
                                       w3[:, (d * 2 + o) * DH:(d * 2 + o + 1) * DH], start=True, stop=True)
                    mm.then_inc(s_f, 1)
                    if t:
                        sum_abs(o, t - 1)
                        ada_next(BUILD)
                for d in range(2):
                    if d or o:
                        pe.wait_ge(s_mid, 2 * o + d)
                    pe.matmul(pm[0:1, :], hid[:, 2 * M:2 * M + 1], w3[:, (d * 2 + o) * DH:(d * 2 + o + 1) * DH],
                              start=True, stop=True).then_inc(s_midv, 1)
                sum_abs(o, MT - 1)
                ada_next(BUILD)
                pe.wait_ge(s_ab, o + 1)
                for d in range(2):
                    mm = pe.matmul(pn[:], g["ones"][0:1, :], mid[:, 2 + d, :], start=False, stop=(d == 1))
                mm.then_inc(s_n, 1)
                if ada:
                    pe.wait_ge(s_ade, ada_next.n)
                pe.wait_ge(s_ol, (o + 1) * MT)
                for ji, (kind, par, f) in enumerate(JOBS):
                    c = o * NCK + ji // PC
                    if ji % PC == 0:
                        st.ready(pe, 0, c)
                    if job >= 2:
                        pe.wait_ge(s_ev, job - 1)
                    x = {"cos": par, "cosx": 0, "sin": 2 + par}[kind]
                    rank1 = (kind != "sin" and par == 0) or (kind == "sin" and par == 1)
                    for t in range(MT):
                        ti = (ji % PC) * MT + t
                        bh, bl = st.tile(st.hi, c, ti), st.tile(st.lo, c, ti)
                        pe.matmul(pk[job % 2][:], bh, opnd_h[:, t, x, :], start=(t == 0), stop=False)
                        pe.matmul(pk[job % 2][:], bh, opnd_l[:, t, x, :], start=False, stop=False)
                        mm = pe.matmul(pk[job % 2][:], bl, opnd_h[:, t, x, :], start=False,
                                       stop=(t == MT - 1 and not rank1))
                    if ji % PC == PC - 1 or ji == NJ - 1:
                        mm.then_inc(st.used, 1)
                    if rank1:
                        mm = pe.matmul(pk[job % 2][:], sgn[:], mid[:, 0 if kind != "sin" else 1, :], start=False, stop=True)
                        mm.then_inc(s_k, 1)
                    elif ji % PC == PC - 1 or ji == NJ - 1:
                        pe.matmul(pm[0:1, 0:2], sgn[:, 0:1], sgn[:, 0:2], start=True, stop=True).then_inc(s_k, 1)
                    else:
                        mm.then_inc(s_k, 1)
                    job += 1
                    ada_next(ji < JOB)
            if ada:
                ada_next(1)
                pe.wait_ge(s_mod, 1)
                for c in range(2):
                    pe.transpose(pf[0][0:48, c * 128:(c + 1) * 128], g["mod"][:, :, c], g["ident"][:])
                    tr = pe.transpose(pf[1][0:16, c * 128:(c + 1) * 128], g["gmod"][:, c, :], g["ident"][:])
                tr.then_inc(s_tr, 1)

        @block.scalar
        def _(act):
            if ada:
                act.wait_ge(s_in, NIN)
                act.activation(sc[:], cond[:], ACT.Silu).then_inc(s_silu, 1)
            for layer in range(2):
                act.wait_ge(s_y, layer + 1)
                act.activation(hid[:], y, ACT.Sin).then_inc(s_sin, 1)
            for o in range(2):
                for c in range(2):
                    if c < NCK:
                        st.split_hi(act, 0, 0, o * NCK + c)
                for t in range(MT):
                    n = o * MT + t
                    act.wait_ge(s_F, n + 1)
                    if n:
                        act.wait_ge(s_sum, n)
                    act.activation(AA[:], F[:, n % 2], ACT.Abs).then_inc(s_abs, 1)
                    act.wait_ge(s_pool, n + 1)
                    if o and t == 0:
                        act.wait_ge(s_k, NJ)
                    act.activation(opnd_h[:, t], ABm[:], ACT.Copy).then_inc(s_oh, 1)
                for c in range(2, NCK):
                    st.split_hi(act, 0, 0, o * NCK + c)

        @block.gpsimd
        def _(pool):
            for n in range(2 * MT):
                pool.wait_ge(s_AB, n + 1)
                if n:
                    pool.wait_ge(s_ol, n)
                for x, (q, op) in enumerate(((0, ALU.add), (0, ALU.subtract), (2, ALU.subtract), (2, ALU.add))):
                    ins = pool.tensor_tensor(ABm[:, x, :], AB[:, q, :], AB[:, q + 1, :], op)
                ins.then_inc(s_pool, 1)

        @block.vector
        def _(dve):
            st.start_dve(dve)
            chain = Chain(dve, s_dve)
            if not ada:
                dve.memset(g["ones"][:], 1.0)
            ada_next = Ada(lambda n: ada_out(dve, n))
            dve.wait_ge(s_in, NIN)
            for layer in range(2):
                for b, (c0, w) in enumerate(TB):
                    dve.wait_ge(s_h, layer * NB + b + 1)
                    ins = dve.tensor_scalar(y[:, c0:c0 + w], pf[b][0:64, 0:w], fb[:, layer:layer + 1], fb[:, 2:3],
                                            ALU.add, ALU.mult)
                chain(ins)
                chain(dve.tensor_scalar(kk, y, 1.0 / (2 * np.pi), MAGIC, ALU.mult, ALU.add))
                chain(dve.tensor_scalar(kk, kk, MAGIC, None, ALU.subtract))
                for part in (TWO_PI_HI, TWO_PI_MID, TWO_PI_LO):
                    chain(dve.scalar_tensor_tensor(y, kk, -part, y, ALU.mult, ALU.add))
                dve.tensor_scalar(y, y[:], 3.1415925, -3.1415925, ALU.min, ALU.max).then_inc(s_y, 1)
                ada_next(HIDDEN)
            for o in range(2):
                def low(t):
                    dve.wait_ge(s_oh, o * MT + t + 1)
                    dve.tensor_tensor(opnd_l[:, t], ABm[:], opnd_h[:, t].bitcast(F32), ALU.subtract).then_inc(s_ol, 1)

                for t in range(MT):
                    n = o * MT + t
                    dve.wait_ge(s_f, n + 1)
                    dve.wait_ge(s_win[n % 2], 16 * (n // 2 + 1))
                    if n >= 2:
                        dve.wait_ge(s_abs, n - 1)
                    for x in range(4):
                        ins = dve.tensor_tensor(F[:, n % 2, x, :], pf[x][:], win[:, n % 2, x // 2, :], ALU.mult)
                    if t == 0:
                        chain(ins)
                        ins = dve.memset(F[0:1, n % 2, 1, :], 0.0)
                    ins.then_inc(s_F, 1)
                    dve.wait_ge(s_F, n + 1)
                    if n:
                        dve.wait_ge(s_pool, n)
                    dve.tensor_tensor(AB[:, 0:2, :], F[:, n % 2, 0:4:2, :], F[:, n % 2, 1:4:2, :], ALU.add)
                    dve.tensor_tensor(AB[:, 2:4, :], F[:, n % 2, 1:4:2, :], F[:, n % 2, 0:4:2, :], ALU.subtract).then_inc(s_AB, 1)
                    if t:
                        low(t - 1)
                        ada_next(BUILD)
                for d in range(2):
                    dve.wait_ge(s_midv, 2 * o + d + 1)
                    if o and d == 0:
                        dve.wait_ge(s_k, NJ)
                    dve.tensor_tensor(mid[:, 2 + d, :], pm[0:1, :], wmid[:], ALU.mult).then_inc(s_mid, 1)
                dve.wait_ge(s_mid, 2 * o + 2)
                dve.tensor_tensor(mid[:, 0, :], mid[:, 2, :], mid[:, 3, :], ALU.add)
                chain(dve.tensor_tensor(mid[:, 1, :], mid[:, 3, :], mid[:, 2, :], ALU.subtract))
                for d in range(2):
                    ins = dve.scalar_tensor_tensor(mid[:, 2 + d, :], mid[:, 2 + d, :], -1.0, mid[:, 2 + d, :], ALU.mult, ALU.max)
                ins.then_inc(s_ab, 1)
                low(MT - 1)
                ada_next(BUILD)
                for c in range(min(2, NCK)):
                    st.split_lo(dve, 0, o * NCK + c)
                dve.wait_ge(s_n, o + 1)
                dve.wait_ge(s_skip, 16 * (o + 1))
                dve.reciprocal(rn[:], pn[:]).then_inc(s_rn, 1)
                dve.wait_ge(s_rn, o + 1)
                for ji in range(NJ):
                    job = o * NJ + ji
                    c = ji // PC + 2
                    if ji % PC == 0 and c < NCK:
                        st.split_lo(dve, 0, o * NCK + c)
                    dve.wait_ge(s_k, job + 1)
                    if job >= 2:
                        dve.wait_ge(s_st[job % 2], 16 * (job // 2))
                    col = 0 if JOBS[ji][1:] == (0, 0) else 1
                    ins = dve.scalar_tensor_tensor(spec[:, job % 2, :], pk[job % 2][:], rowf[:, col:col + 1], rn[:],
                                                   ALU.mult, ALU.mult)
                    if JOBS[ji][0] != "sin":
                        chain(ins)
                        ins = dve.scalar_tensor_tensor(spec[:, job % 2, :], skip[:], rowf[:, col:col + 1],
                                                       spec[:, job % 2, :], ALU.mult, ALU.add)
                    ins.then_inc(s_ev, 1)
                    ada_next(ji < JOB)
            if ada:
                ada_next(1)
                dve.wait_ge(s_ade, NA + 1)
                for c in range(2):
                    for j, (sc0, gn) in enumerate(((8, 0), (32, 8))):
                        ins = dve.scalar_tensor_tensor(g["gmod"][:, c, j * 8:(j + 1) * 8], g["mod"][:, sc0:sc0 + 8, c], 1.0,
                                                       g["gains"][:, gn:gn + 8], ALU.add, ALU.mult)
                ins.then_inc(s_mod, 1)
                dve.wait_ge(s_tr, 1)
                dve.tensor_copy(rows48, pf[0][0:48, 0:256].rearrange("p (c n) -> p c n", c=2))
                dve.tensor_copy(rows16, pf[1][0:16, 0:256].rearrange("p (c n) -> p c n", c=2)).then_inc(s_rows, 1)


def hyena(nc, a, g, s, L, tok0):
    M = L // 2
    MT = M // 128
    NJ = 2 * MT
    NC = 16 if MT == 4 else 1

    def fwd_tile(j, kind, t):
        return (j, kind * MT + t) if MT == 4 else (0, 2 * j + kind)

    def inv_tile(j, kind):
        return (8 + j, kind) if MT == 4 else (0, 4 + 2 * j + kind)

    with Phase(nc, f"hy{s}") as ph:
        s_step = ph.sem("step_mm")
        st = Stream(ph, 3, 3, s_step, 2 * NJ // NC)
        S0 = 3 * st.per
        pad = ph.sb("pad", [128, 2, L + 2])
        cw = ph.sb("cw", [128, 12, 4])
        u = ph.sb("u", [128, 4, L])
        fold = ph.sb("fold", [128, 4, L])
        uh = ph.sb("uh", [128, 2, MT, DH], F32R)
        ul = ph.sb("ul", [128, 2, MT, DH], F32R)
        kt = ph.sb("kt", [128, 2, 3, DH])
        pr = ph.sb("pr", [128, 2, 4, DH])
        Ph = ph.sb("Ph", [128, 2, NJ, DH], F32R)
        Pl = ph.sb("Pl", [128, 2, NJ, DH], F32R)
        pc = pr[:, 0]
        bank = [ph.ps(f"bank{b}", [128, 512]) for b in range(8)]
        s_cw = ph.sem("cw_landed")
        s_pad = [ph.sem(f"pad_landed{b}") for b in range(2)]
        s_zero, s_dve, s_conv, s_fold = ph.sem("edges"), ph.sem("dve_steps"), ph.sem("conv"), ph.sem("folded")
        s_tr, s_uh, s_ul = ph.sem("transposed"), ph.sem("u_hi"), ph.sem("u_lo")
        s_kt = [ph.sem(f"k_landed{b}") for b in range(2)]
        s_prod, s_pool = ph.sem("products"), ph.sem("pool_steps")
        s_Ph, s_Pl = ph.sem("P_hi"), ph.sem("P_lo")
        s_pc, s_z, s_out = ph.sem("half_copied"), ph.sem("gated"), ph.sem("out")
        block = ph.block()

        def load_pad(pool, n):
            if n >= 2:
                pool.wait_ge(s_conv, n - 1)
            pool.dma_start(pad[:, n % 2, 1:L + 1], g["QKH"][1024 + n * 128:1152 + n * 128, tok0:tok0 + L])\
                .then_inc(s_pad[n % 2], 16)

        def load_k(pool, o, j):
            n = o * NJ + j
            if n >= 2:
                pool.wait_ge(s_prod, n - 1)
            w = 3 if j == 0 else 2
            pool.dma_start(kt[:, n % 2, 0:w, :], g[f"K{s}"][o, j, 0:w].rearrange("a p f -> p a f")).then_inc(s_kt[n % 2], 16)

        @block.sync
        def _(sp):
            sp.dma_start(cw[:], a["conv"]).then_inc(s_cw, 16)
            for o in range(2):
                for c in range(NC):
                    st.load(sp, 0, o * NC + c, a[f"basis_{s}"][c])
            for ct in range(4):
                sp.wait_ge(s_z, 4 + ct + 1)
                sp.dma_start(g["MIXT"][DA + ct * 128:DA + (ct + 1) * 128, tok0:tok0 + L], u[:, ct, :]).then_inc(s_out, 16)
            sp.wait_ge(s_out, 64)

        @block.gpsimd
        def _(pool):
            pool.wait_ge(s_zero, 1)
            for n in range(4):
                load_pad(pool, n)
            for o in range(2):
                load_k(pool, o, 0)
                load_k(pool, o, 1)
                for j in range(NJ):
                    n = o * NJ + j
                    pool.wait_ge(s_prod, n + 1)
                    pool.tensor_tensor(pr[:, n % 2, 0, :], pr[:, n % 2, 0, :], pr[:, n % 2, 1, :], ALU.add).then_inc(s_pool, 1)
                    pool.tensor_tensor(pr[:, n % 2, 2, :], pr[:, n % 2, 2, :], pr[:, n % 2, 3, :], ALU.subtract).then_inc(s_pool, 1)
                    if j + 2 < NJ:
                        load_k(pool, o, j + 2)
                for c in range(4):
                    load_pad(pool, 4 + 4 * o + c)

        @block.scalar
        def _(act):
            for o in range(2):
                for c in range(min(2, NC)):
                    st.split_hi(act, 0, 0, o * NC + c)
                for q in range(2 * MT):
                    act.wait_ge(s_tr, o * 2 * MT + q + 1)
                    act.activation(uh[:, q // MT, q % MT, :], bank[q][:], ACT.Copy).then_inc(s_uh, 1)
                for j in range(NJ + 1):
                    if j < NJ and j + 2 < NC:
                        st.split_hi(act, 0, 0, o * NC + j + 2)
                    if j == 0:
                        continue
                    j -= 1
                    n = o * NJ + j
                    act.wait_ge(s_pool, 2 * n + 2)
                    if o and j == 0:
                        act.wait_ge(s_step, S0 + 2 * NJ)
                    for x in range(2):
                        act.activation(Ph[:, x, j, :], pr[:, n % 2, 2 * x, :], ACT.Copy).then_inc(s_Ph, 1)
                for c in range(NJ + 2, NC):
                    st.split_hi(act, 0, 0, o * NC + c)
                act.wait_ge(s_step, S0 + (o + 1) * 2 * NJ)
                act.wait_ge(s_Pl, (o + 1) * 2 * NJ)
                for ct in range(4):
                    act.activation(pc[:, ct, 0:M], bank[4 + ct][:, 0:M], ACT.Copy).then_inc(s_pc, 1)

        @block.vector
        def _(dve):
            st.start_dve(dve)
            chain = Chain(dve, s_dve)
            dve.memset(pad[:, :, 0:1], 0.0)
            dve.memset(pad[:, :, L + 1:L + 2], 0.0).then_inc(s_zero, 1)
            dve.wait_ge(s_cw, 16)

            def conv(n, out):
                dve.wait_ge(s_pad[n % 2], 16 * (n // 2 + 1))
                p = pad[:, n % 2]
                chain(dve.tensor_scalar(out, p[:, 1:L + 1], cw[:, n, 1:2], cw[:, n, 3:4], ALU.mult, ALU.add))
                chain(dve.scalar_tensor_tensor(out, p[:, 0:L], cw[:, n, 0:1], out, ALU.mult, ALU.add))
                dve.scalar_tensor_tensor(out, p[:, 2:L + 2], cw[:, n, 2:3], out, ALU.mult, ALU.add).then_inc(s_conv, 1)

            for n in range(4):
                conv(n, u[:, n, :])
            dve.wait_ge(s_conv, 4)
            for o in range(2):
                if o:
                    dve.wait_ge(s_z, 4)
                dve.tensor_tensor(fold[:, :, 0:M], u[:, :, 0:M], u[:, :, L - 1:M - 1:-1], ALU.add)
                dve.tensor_tensor(fold[:, :, M:L], u[:, :, 0:M], u[:, :, L - 1:M - 1:-1], ALU.subtract).then_inc(s_fold, 1)
                for c in range(min(2, NC)):
                    st.split_lo(dve, 0, o * NC + c)
                for q in range(2 * MT):
                    dve.wait_ge(s_uh, o * 2 * MT + q + 1)
                    dve.tensor_tensor(ul[:, q // MT, q % MT, :], bank[q][:], uh[:, q // MT, q % MT, :].bitcast(F32),
                                      ALU.subtract).then_inc(s_ul, 1)
                def low(j):
                    n = o * NJ + j
                    for x in range(2):
                        dve.wait_ge(s_Ph, 2 * n + x + 1)
                        dve.tensor_tensor(Pl[:, x, j, :], pr[:, n % 2, 2 * x, :], Ph[:, x, j, :].bitcast(F32),
                                          ALU.subtract).then_inc(s_Pl, 1)

                for j in range(NJ):
                    n = o * NJ + j
                    if j + 2 < NC:
                        st.split_lo(dve, 0, o * NC + j + 2)
                    dve.wait_ge(s_kt[n % 2], 16 * (n // 2 + 1))
                    dve.wait_ge(s_step, S0 + o * 2 * NJ + j + 1)
                    if n >= 2:
                        dve.wait_ge(s_Pl, 2 * (n - 1))
                    ur, us = bank[(n % 2) * 2], bank[(n % 2) * 2 + 1]
                    k, q = kt[:, n % 2], pr[:, n % 2]
                    dve.tensor_tensor(q[:, 0, :], ur[:], k[:, 0, :], ALU.mult)
                    dve.tensor_tensor(q[:, 1, :], us[:], k[:, 1, :], ALU.mult)
                    dve.tensor_tensor(q[:, 2, :], us[:], k[:, 2 if j == 0 else 0, :], ALU.mult)
                    dve.tensor_tensor(q[:, 3, :], ur[:], k[:, 1, :], ALU.mult).then_inc(s_prod, 1)
                    if j:
                        low(j - 1)
                low(NJ - 1)
                for c in range(4):
                    if NJ + 2 + 2 * c < NC:
                        st.split_lo(dve, 0, o * NC + NJ + 2 + 2 * c)
                    conv(4 + 4 * o + c, fold[:, c, :])
                    if NJ + 3 + 2 * c < NC:
                        st.split_lo(dve, 0, o * NC + NJ + 3 + 2 * c)
                dve.wait_ge(s_conv, 8 + 4 * o)
                for ct in range(4):
                    dve.wait_ge(s_pc, 4 * o + ct + 1)
                    dve.wait_ge(s_step, S0 + (o + 1) * 2 * NJ)
                    chain(dve.tensor_tensor(u[:, ct, 0:M], pc[:, ct, 0:M], bank[ct][:, 0:M], ALU.add))
                    chain(dve.tensor_tensor(u[:, ct, L - 1:M - 1:-1], pc[:, ct, 0:M], bank[ct][:, 0:M], ALU.subtract))
                    dve.tensor_tensor(u[:, ct, :], u[:, ct, :], fold[:, ct, :], ALU.mult).then_inc(s_z, 1)

        @block.tensor
        def _(pe):
            st.start_pe(pe)
            for o in range(2):
                pe.wait_ge(s_fold, o + 1)
                if o:
                    pe.wait_ge(s_z, 4)
                for q in range(2 * MT):
                    par, t = divmod(q, MT)
                    for ct in range(4):
                        tr = pe.transpose(bank[q][:, ct * 128:(ct + 1) * 128],
                                          fold[:, ct, par * M + t * 128:par * M + (t + 1) * 128], g["ident"][:])
                    tr.then_inc(s_tr, 1)
                pe.wait_ge(s_ul, (o + 1) * 2 * MT)
                last = -1
                for j in range(NJ):
                    n = o * NJ + j
                    if n >= 2:
                        pe.wait_ge(s_prod, n - 1)
                    par = j // MT
                    for kind in range(2):
                        src = par if kind == 0 else 1 - par
                        out = bank[(n % 2) * 2 + kind]
                        for t in range(MT):
                            c, ti = fwd_tile(j, kind, t)
                            if c > last:
                                st.ready(pe, 0, o * NC + c)
                                last = c
                            bh, bl = st.tile(st.hi, o * NC + c, ti), st.tile(st.lo, o * NC + c, ti)
                            pe.matmul(out[:], bh, uh[:, src, t, :], start=(t == 0), stop=False)
                            pe.matmul(out[:], bh, ul[:, src, t, :], start=False, stop=False)
                            mm = pe.matmul(out[:], bl, uh[:, src, t, :], start=False, stop=(t == MT - 1))
                    mm.then_inc(s_step, 1)
                pe.wait_ge(s_prod, (o + 1) * NJ)
                for j in range(NJ):
                    n = o * NJ + j
                    pe.wait_ge(s_Pl, 2 * n + 2)
                    for kind in range(2):
                        c, ti = inv_tile(j, kind)
                        if c > last:
                            st.ready(pe, 0, o * NC + c)
                            last = c
                        w = M
                        bh, bl = st.tile(st.hi, o * NC + c, ti, w), st.tile(st.lo, o * NC + c, ti, w)
                        even = (kind == j // MT)
                        first = j == 0
                        final = j == NJ - 1
                        for ct in range(4):
                            out = bank[(4 if even else 0) + ct][:, 0:w]
                            xh, xl = Ph[:, kind, j, ct * 128:(ct + 1) * 128], Pl[:, kind, j, ct * 128:(ct + 1) * 128]
                            pe.matmul(out, xh, bh, start=first, stop=False)
                            pe.matmul(out, xh, bl, start=False, stop=False)
                            mm = pe.matmul(out, xl, bh, start=False, stop=final)
                    mm.then_inc(s_step, 1)


def mix_and_route(nc, a, g):
    BLK = [(0, 512), (512, 512), (1024, 256)]
    with Phase(nc, "mix") as ph:
        s_tile = ph.sem("mix_mm")
        st = Stream(ph, 2, 8, ph.sem("unused"), 1)
        mh = ph.sb("mh", [128, KT, T], F32R)
        ml = ph.sb("ml", [128, KT, T], F32R)
        raw = ph.sb("raw4", [128, 4, T])
        r = ph.sb("r", [128, T])
        work = ph.sb("work", [128, 6 * D])
        yh = work[:, 0:4 * T].rearrange("p (a b) -> p a b", a=4)
        h2 = [work[:, 0:D], work[:, D:2 * D], st.raw[:, 0, :], st.raw[:, 1, :]]
        h2T = work[:, 2 * D:3 * D].rearrange("p (a b) -> p a b", a=KT)
        rows = work[:, 3 * D:6 * D].rearrange("p (a b) -> p a b", a=3)
        wr = ph.sb("wr", [128, KT, NE])
        ss, rr, r2, root = (ph.sb(x, [128, NTT]) for x in ("ss", "rr", "r2", "root"))
        lm, lsum, linv = (ph.sb(x, [128, NTT]) for x in ("lm", "lsum", "linv"))
        lg = ph.sb("lg", [128, NTT, NE])
        aff = ph.sb("aff", [128, NTT, NE])
        bank = [ph.ps(f"bank{b}", [128, 512]) for b in range(8)]
        xb = [raw[:, b, 0:D] for b in range(2)]
        tb = [raw[:, 2 + b, 0:D] for b in range(2)]
        s_y, s_at = [ph.sem(f"y_landed{b}") for b in range(4)], [ph.sem(f"at_landed{b}") for b in range(4)]
        s_sq, s_sum, s_dve, s_root, s_yn = ph.sem("squares"), ph.sem("sum_mm"), ph.sem("dve_steps"), ph.sem("root"), ph.sem("y_normed")
        s_mh, s_ml = ph.sem("m_hi"), ph.sem("m_lo")
        s_row, s_x = ph.sem("rows_landed"), [ph.sem(f"x_landed{b}") for b in range(2)]
        s_wr = ph.sem("router_landed")
        s_t, s_x1, s_ss, s_rt, s_h = ph.sem("mixed"), ph.sem("x1"), ph.sem("x1_squares"), ph.sem("row_root"), ph.sem("h2_scaled")
        s_h2, s_x1st, s_h2st = ph.sem("h2"), [ph.sem(f"x1_stored{b}") for b in range(2)], [ph.sem(f"h2_stored{b}") for b in range(4)]
        s_tr, s_hT, s_lg, s_lm, s_ex = ph.sem("h2_transposed"), ph.sem("h2T"), ph.sem("logits"), ph.sem("logit_max"), ph.sem("exps")
        s_lgc = ph.sem("logits_copied")
        LAG = 3
        block = ph.block()
        junk = r[:, 0:D]
        ORDER = [2, 3, 4, 5, 6, 7, 0, 1]

        def mixed(n):
            return raw[:, n, :] if n < 4 else yh[:, n - 4, :]

        def load_rows(sp, c):
            for n, (src, c0) in enumerate((("MODR", 2 * D), ("GMODR", D), ("MODR", 3 * D))):
                sp.dma_start(rows[:, n, :], g[src][c:c + 1, c0:c0 + D].to_broadcast([128, D])).then_inc(s_row, 16)

        def store(sp, t):
            sp.wait_ge(s_x1, t + 1)
            sp.dma_start(g["X"][t * 128:(t + 1) * 128, :], xb[t % 2]).then_inc(s_x1st[t % 2], 16)
            sp.wait_ge(s_h2, t + 1)
            sp.dma_start(g["H2"][t * 128:(t + 1) * 128, :], h2[t % 4]).then_inc(s_h2st[t % 4], 16)

        @block.sync
        def _(sp):
            for ct in range(4):
                sp.dma_start(yh[:, ct, :], g["MIXT"][DA + ct * 128:DA + (ct + 1) * 128, :]).then_inc(s_y[ct], 16)
            sp.dma_start(wr[:], a["w_router"]).then_inc(s_wr, 16)
            for c in range(8):
                st.load(sp, 0, c, a["w_out"][c])
            for ct in (2, 3, 0, 1):
                if ct == 2:
                    sp.wait_ge(s_sum, 3)
                if ct == 0:
                    sp.wait_ge(s_yn, 1)
                sp.dma_start(raw[:, ct, :], g["MIXT"][ct * 128:(ct + 1) * 128, :]).then_inc(s_at[ct], 16)
            sp.wait_ge(s_ml, 8)
            load_rows(sp, 1)
            for t in range(NTT):
                if t < 2:
                    sp.wait_ge(s_ml, 8)
                else:
                    if t == 2:
                        sp.wait_ge(s_h2, 2)
                        load_rows(sp, 0)
                    sp.wait_ge(s_x1st[t % 2], 16 * (t // 2))
                    sp.wait_ge(s_h, t - 1)
                    sp.wait_ge(s_ss, t - 1)
                sp.dma_start(xb[t % 2], a["x"][t * 128:(t + 1) * 128, :]).then_inc(s_x[t % 2], 16)
                if t:
                    store(sp, t - 1)
            store(sp, NTT - 1)
            for b in range(2):
                sp.wait_ge(s_x1st[b], 16 * (NTT // 2))
            for b in range(4):
                sp.wait_ge(s_h2st[b], 16 * ((NTT + 3 - b) // 4))

        @block.gpsimd
        def _(pool):
            for t in range(NTT):
                pool.wait_ge(s_t, t + 1)
                pool.wait_ge(s_x[t % 2], 16 * (t // 2 + 1))
                pool.tensor_tensor(xb[t % 2], xb[t % 2], tb[t % 2], ALU.add).then_inc(s_x1, 1)
                pool.wait_ge(s_h, t + 1)
                pool.tensor_tensor(h2[t % 4], h2[t % 4], rows[:, 2, :], ALU.add).then_inc(s_h2, 1)

        @block.scalar
        def _(act):
            act.sem_inc(st.used, 8)
            for c in range(2):
                st.split_hi(act, 0, 0, c)
            for ct in range(4):
                act.wait_ge(s_y[ct], 16)
                act.activation(raw[:, ct, :], yh[:, ct, :], ACT.Square).then_inc(s_sq, 1)
            for c in range(2, 8):
                st.split_hi(act, 0, 0, c)
            act.wait_ge(s_root, 1)
            act.activation(raw[:, 1, :], r[:], ACT.Ln).then_inc(s_root, 1)
            act.wait_ge(s_root, 2)
            act.activation(raw[:, 0, :], raw[:, 1, :], ACT.Exp, scale=-0.5).then_inc(s_root, 1)
            for n in ORDER:
                if n < 4:
                    act.wait_ge(s_at[n], 16)
                else:
                    act.wait_ge(s_yn, n - 3)
                act.activation(mh[:, n, :], mixed(n), ACT.Copy).then_inc(s_mh, 1)
            for t in range(NTT + LAG):
                q = t - LAG
                if q >= 0:
                    for b in range(2):
                        act.wait_ge(s_tr, 2 * q + b + 1)
                        if q:
                            act.wait_ge(s_lg, q)
                        act.activation(work[:, 2 * D + b * 512:2 * D + b * 512 + 512], bank[4 + b][:], ACT.Copy).then_inc(s_hT, 1)
                if t < NTT:
                    act.wait_ge(s_x1, t + 1)
                    if t:
                        act.wait_ge(s_ss, t)
                    act.activation(junk, xb[t % 2], ACT.Square, accum_out=ss[:, t:t + 1]).then_inc(s_ss, 1)
                    act.wait_ge(s_rt, 2 * t + 1)
                    act.activation(root[:, t:t + 1], r2[:, t:t + 1], ACT.Sqrt).then_inc(s_rt, 1)
            act.wait_ge(s_lm, 1)
            for q in range(NTT):
                ins = act.activation(aff[:, q, :], lg[:, q, :], ACT.Exp, bias=lm[:, q:q + 1], accum_out=lsum[:, q:q + 1])
            ins.then_inc(s_ex, 1)

        @block.vector
        def _(dve):
            st.start_dve(dve)
            chain = Chain(dve, s_dve)
            for c in range(8):
                st.split_lo(dve, 0, c)
            for b, (c0, w) in enumerate(BLK):
                dve.wait_ge(s_sum, b + 1)
                ins = dve.tensor_scalar(r[:, c0:c0 + w], bank[b][:, 0:w], 1.0 / DH, EPS, ALU.mult, ALU.add)
            ins.then_inc(s_root, 1)
            root_y, t_y = raw[:, 0, :], raw[:, 1, :]
            dve.wait_ge(s_root, 3)
            chain(dve.tensor_tensor(t_y, root_y, root_y, ALU.mult))
            chain(dve.tensor_tensor(t_y, t_y, r[:], ALU.mult))
            chain(dve.tensor_scalar(t_y, t_y, -0.5, 1.5, ALU.mult, ALU.add))
            chain(dve.tensor_tensor(r[:], root_y, t_y, ALU.mult))
            for ct in range(4):
                dve.scalar_tensor_tensor(yh[:, ct, :], yh[:, ct, :], g["gains"][:, 20 + ct:21 + ct], r[:],
                                         ALU.mult, ALU.mult).then_inc(s_yn, 1)
            for x, n in enumerate(ORDER):
                dve.wait_ge(s_mh, x + 1)
                dve.tensor_tensor(ml[:, n, :], mixed(n), mh[:, n, :].bitcast(F32), ALU.subtract).then_inc(s_ml, 1)
            for t in range(NTT + LAG):
                if t < NTT:
                    dve.wait_ge(s_row, 48 if t < 2 else 96)
                    dve.wait_ge(s_tile, t + 1)
                    if t >= 2:
                        dve.wait_ge(s_x1, t - 1)
                    if t < 2:
                        dve.wait_ge(s_ml, 8)
                    for b in range(2):
                        ins = dve.tensor_tensor(tb[t % 2][:, b * 512:b * 512 + 512], bank[(t % 2) * 2 + b][:],
                                                rows[:, 0, b * 512:b * 512 + 512], ALU.mult)
                    ins.then_inc(s_t, 1)
                    dve.wait_ge(s_ss, t + 1)
                    c1 = slice(t, t + 1)
                    chain(dve.tensor_scalar(rr[:, c1], ss[:, c1], 1.0 / D, EPS, ALU.mult, ALU.add))
                    dve.reciprocal(r2[:, c1], rr[:, c1]).then_inc(s_rt, 1)
                    dve.wait_ge(s_rt, 2 * t + 2)
                    chain(dve.tensor_tensor(r2[:, c1], root[:, c1], root[:, c1], ALU.mult))
                    chain(dve.tensor_tensor(r2[:, c1], r2[:, c1], rr[:, c1], ALU.mult))
                    chain(dve.tensor_scalar(r2[:, c1], r2[:, c1], -0.5, 1.5, ALU.mult, ALU.add))
                    chain(dve.tensor_tensor(rr[:, c1], root[:, c1], r2[:, c1], ALU.mult))
                    if t >= 4:
                        dve.wait_ge(s_h2st[t % 4], 16 * (t // 4))
                        dve.wait_ge(s_tr, 2 * (t - 3))
                    dve.scalar_tensor_tensor(h2[t % 4], xb[t % 2], rr[:, c1], rows[:, 1, :],
                                             ALU.mult, ALU.mult).then_inc(s_h, 1)
                if t >= LAG:
                    q = t - LAG
                    dve.wait_ge(s_lg, q + 1)
                    dve.tensor_copy(lg[:, q, :], bank[6 + q % 2][:, 0:NE]).then_inc(s_lgc, 1)
            dve.wait_ge(s_lgc, NTT)
            dve.tensor_reduce(lm[:], lg[:], AX.X, ALU.max, negate=True).then_inc(s_lm, 1)
            dve.wait_ge(s_ex, 1)
            chain(dve.reciprocal(linv[:], lsum[:]))
            for q in range(NTT):
                dve.tensor_scalar(g["aff"][:, q, :], aff[:, q, :], linv[:, q:q + 1], None, ALU.mult)

        @block.tensor
        def _(pe):
            for b, (c0, w) in enumerate(BLK):
                for ct in range(4):
                    if b == 0:
                        pe.wait_ge(s_sq, ct + 1)
                    mm = pe.matmul(bank[b][:, 0:w], g["ones"][:], raw[:, ct, c0:c0 + w], start=(ct == 0), stop=(ct == 3))
                mm.then_inc(s_sum, 1)
            pe.wait_ge(s_wr, 16)
            pe.wait_ge(s_yn, 1)

            def transposes(q):
                pe.wait_ge(s_h2, q + 1)
                for b in range(2):
                    if q:
                        pe.wait_ge(s_hT, 2 * (q - 1) + b + 1)
                    for k in range(4):
                        tr = pe.transpose(bank[4 + b][:, k * 128:(k + 1) * 128],
                                          h2[q % 4][:, (4 * b + k) * 128:(4 * b + k + 1) * 128], g["ident"][:])
                    tr.then_inc(s_tr, 1)

            def logits(q):
                pe.wait_ge(s_hT, 2 * q + 2)
                if q >= 2:
                    pe.wait_ge(s_lgc, q - 1)
                for k in range(KT):
                    mm = pe.matmul(bank[6 + q % 2][:, 0:NE], h2T[:, k, :], wr[:, k, :], start=(k == 0), stop=(k == KT - 1))
                mm.then_inc(s_lg, 1)

            pe.wait_ge(s_ml, 8)
            st.ready(pe, 0, 7)
            for t in range(NTT + LAG):
                if t >= LAG:
                    transposes(t - LAG)
                if t < NTT:
                    if t >= 2:
                        pe.wait_ge(s_t, t - 1)
                    for b in range(2):
                        out = bank[(t % 2) * 2 + b][:]
                        for k in range(KT):
                            xh, xl = mh[:, k, t * 128:(t + 1) * 128], ml[:, k, t * 128:(t + 1) * 128]
                            wh, wl = st.tile(st.hi, k, b, 512), st.tile(st.lo, k, b, 512)
                            pe.matmul(out, xh, wh, start=(k == 0), stop=False)
                            pe.matmul(out, xh, wl, start=False, stop=False)
                            mm = pe.matmul(out, xl, wh, start=False, stop=(k == KT - 1))
                    mm.then_inc(s_tile, 1)
                if t >= LAG:
                    logits(t - LAG)


class Choice:

    def __init__(self, nc, ph, g, pa, pt, ptp):
        self.g, self.pa, self.pt, self.ptp = g, pa, pt, ptp
        H = TS // 2
        self.affT = ph.sb("affT", [80, H])
        self.val, self.idx = ph.sb("val", [80, CAP_S]), ph.sb("idx", [80, CAP_S], U32)
        self.low, self.high, self.hv, self.first = (ph.sb(n, [NE, CAP_S]) for n in ("low", "high", "hv", "first"))
        self.ip, self.vp = ph.sb("ip", [NE, CAP_P]), ph.sb("vp", [NE, CAP_P])
        self.s_tr, self.s_dve, self.s_tab = ph.sem("aff_transposed"), ph.sem("choice_steps"), ph.sem("tables")

    def on_tensor(self, pe):
        g = self.g
        for t in range(NTT):
            bank, c = (2, t) if t < 2 else divmod(t - 2, 4)
            pe.transpose(self.pa[bank][:, c * 128:(c + 1) * 128], g["aff"][:, t, :], g["ident"][:]).then_inc(self.s_tr, 1)
        pe.wait_ge(self.s_tab, 1)
        for n, (s, p) in enumerate(((self.low, self.ip), (self.hv, self.vp))):
            pe.transpose(self.pt[:, n * NE:(n + 1) * NE], s[:], g["ident"][0:NE, 0:NE])
            tr = pe.transpose(self.ptp[:, n * NE:(n + 1) * NE], p[:], g["ident"][0:NE, 0:NE])
        tr.then_inc(self.s_tr, 1)

    def on_vector(self, dve):
        g, affT, val, idx = self.g, self.affT, self.val, self.idx
        chain = Chain(dve, self.s_dve)
        dve.memset(g["rows_s"][:], 0)
        dve.memset(g["rows_p"][:], 0)
        chain(dve.memset(affT[:], -2.0))
        dve.wait_ge(self.s_tr, NTT)
        for p0, bank, w in ((0, 0, TS // 2), (32, 1, TS // 2), (64, 2, TP)):
            ins = dve.tensor_copy(affT[p0:p0 + NE, 0:w], self.pa[bank][:, 0:w])
        chain(ins)
        for r in range(CAP_S // 8):
            v, x = val[:, 8 * r:8 * r + 8], idx[:, 8 * r:8 * r + 8]
            chain(dve.max(v, affT[:]))
            chain(dve.max_index(x, v, affT[:]))
            if r + 1 < CAP_S // 8:
                chain(dve.match_replace(affT[:], v, affT[:], -1.0))
        dve.tensor_copy(self.ip[:], idx[64:64 + NE, 0:CAP_P])
        dve.tensor_copy(self.vp[:], val[64:64 + NE, 0:CAP_P])
        dve.tensor_scalar(self.low[:], idx[0:NE, :], float(TP), None, ALU.add)
        dve.tensor_scalar(self.high[:], idx[32:32 + NE, ::-1], float(TP + TS // 2), None, ALU.add)
        chain(dve.tensor_copy(self.hv[:], val[32:32 + NE, ::-1]))
        dve.tensor_tensor(self.first[:], val[0:NE, :], self.hv[:], ALU.is_ge)
        chain(dve.tensor_tensor(self.low[:], self.low[:], self.high[:], ALU.subtract))
        chain(dve.tensor_tensor(self.low[:], self.low[:], self.first[:], ALU.mult))
        dve.tensor_tensor(self.hv[:], val[0:NE, :], self.hv[:], ALU.max)
        dve.tensor_tensor(self.low[:], self.low[:], self.high[:], ALU.add).then_inc(self.s_tab, 1)
        dve.wait_ge(self.s_tr, NTT + 1)
        dve.tensor_copy(g["rows_s"][:, 0:NE], self.pt[:, 0:NE])
        dve.tensor_copy(g["gate_s"][:], self.pt[:, NE:2 * NE])
        dve.tensor_copy(g["rows_p"][:, 0:NE], self.ptp[:, 0:NE])
        dve.tensor_copy(g["gate_p"][:], self.ptp[:, NE:2 * NE]).then_inc(self.s_tab, 1)


def experts(nc, a, g):
    CW, C2 = 2 * FT, FT * D // CH
    NC = CW + C2
    GD = D // 128
    XB = [(0, 3), (3, 3), (6, 2)]
    AHEAD_HI, AHEAD_LO = 4, 3
    end = [CW + (FT * d + FT - 1) // 8 for d in range(GD)]
    shared = [d for d in range(GD) if (FT * d + FT) % 8 == 0]
    alone = [d for d in range(GD) if d not in shared]
    with Phase(nc, "exp") as ph:
        st = Stream(ph, 11, 6, ph.sem("chunk_used"), 1)
        xg = ph.sb("xg", [128, D])
        xp = ph.sb("xp", [CAP_P, D])
        xt = ph.sb("xt", [128, KT, 2 * CAP], F32R)
        hid = ph.sb("hid", [128, FT, 2 * CAP], F32R)
        cpy = ph.sb("cpy", [128, 2, 2, CAP])
        s13 = ph.sb("s13", [128, 2, 2, CAP])
        sl = ph.sb("sl", [128, 2, CAP])
        hd = ph.sb("hd", [128, 2, CAP])
        cy = ph.sb("cy", [128, 2, CAP])
        ye = ph.sb("ye", [128, 2, CAP])
        ys = ph.sb("ys", [128, D])
        yp = ph.sb("yp", [CAP_P, D])
        cur_s, next_s = ph.sb("cur_s", [128, 1], U32), ph.sb("next_s", [128, 1], U32)
        cur_p, next_p = ph.sb("cur_p", [CAP_P, 1], U32), ph.sb("next_p", [CAP_P, 1], U32)
        gate_s, gate_p = ph.sb("gate_s", [128, 1]), ph.sb("gate_p", [CAP_P, 1])
        step, one = ph.sb("step", [1, 1]), g["ident"][0:1, 0:1]
        ps = ph.ps("ps", [128, 4, 512])
        py = [ph.ps(f"py{b}", [128, 512]) for b in range(2)]
        pr = ph.ps("pr", [128, 512])
        pp = ph.ps("pp", [CAP_P, 512])
        choice = Choice(nc, ph, g, [ps[0:NE, b, :] for b in range(3)], py[0], py[1][0:CAP_P, :])
        s_ix, s_xg, s_xtr = ph.sem("index_ready"), ph.sem("x_gathered"), ph.sem("x_transposed")
        s_xhi, s_xlo = ph.sem("x_hi"), ph.sem("x_lo")
        s_cp, s_add, s_sl, s_hd = ph.sem("low_copied"), ph.sem("pair_summed"), ph.sem("silu"), ph.sem("hidden")
        s_hh, s_hid = ph.sem("hidden_hi"), ph.sem("hidden_lo")
        s_g, s_cy, s_ye, s_yt = ph.sem("group_done"), ph.sem("y_low_copied"), ph.sem("y_gated"), ph.sem("y_transposed")
        s_row, s_sc = ph.sem("rows_ready"), ph.sem("scattered")
        block = ph.block()

        def xbank(b, n):
            return ps[:, b, 0:n * CAP].rearrange("p (k t) -> p k t", k=n)

        def group_done(eng, e, d):
            if d in shared:
                eng.wait_ge(st.used, e * NC + end[d] + 1 + st.ns)
            else:
                eng.wait_ge(s_g, e * len(alone) + alone.index(d) + 1)

        @block.sync
        def _(sp):
            with sp.Fori(0, NE) as e:
                for c in range(CW):
                    st.load(sp, e * NC, c, a["w13"][bass.ds(e * CW + c, 1)].rearrange("a p f -> p (a f)"))
                for c in range(CW, NC):
                    st.load(sp, e * NC, c, a["w2"][bass.ds(e * C2 + (c - CW), 1)].rearrange("a p f -> p (a f)"))
            for c in range(AHEAD_HI):
                st.load(sp, NE * NC, c, a["w13"][c])

        @block.gpsimd
        def _(pool):
            pool.wait_ge(choice.s_tab, 2)
            pool.tensor_copy(next_s[:], g["rows_s"][:, 0:1])
            pool.tensor_copy(next_p[:], g["rows_p"][:, 0:1]).then_inc(s_ix, 1)

            def gather(n):
                pool.wait_ge(s_ix, n)
                pool.tensor_tensor(step[:], one, one, ALU.mult)
                pool.indirect_dma_start(xg[:], None, g["H2"], bass.IndirectOffsetOnAxis(ap=next_s[:, 0:1], axis=0)).then_inc(s_xg, 16)
                pool.indirect_dma_start(xp[:], None, g["H2"], bass.IndirectOffsetOnAxis(ap=next_p[:, 0:1], axis=0)).then_inc(s_xg, 16)

            gather(1)
            with pool.Fori(0, NE) as e:
                pool.wait_ge(s_xg, e * 32 + 32)
                pool.wait_ge(s_xtr, e * 3 + 3)
                pool.tensor_copy(cur_s[:], g["rows_s"][:, bass.ds(e, 1)])
                pool.tensor_copy(cur_p[:], g["rows_p"][:, bass.ds(e, 1)])
                pool.tensor_copy(gate_s[:], g["gate_s"][:, bass.ds(e, 1)])
                pool.tensor_copy(gate_p[:], g["gate_p"][:, bass.ds(e, 1)])
                pool.tensor_copy(next_s[:], g["rows_s"][:, bass.ds(e + 1, 1)])
                pool.tensor_copy(next_p[:], g["rows_p"][:, bass.ds(e + 1, 1)]).then_inc(s_ix, 1)
                gather(e + 2)
                for j in range(FT):
                    b = j % 2
                    pool.wait_ge(s_sl, e * FT + j + 1)
                    pool.tensor_tensor(hd[:, b], sl[:, b], s13[:, b, 1], ALU.mult).then_inc(s_hd, 1)
                    pool.wait_ge(s_hh, e * FT + j + 1)
                    pool.tensor_tensor(hid[:, j, CAP:2 * CAP], hd[:, b], hid[:, j, 0:CAP].bitcast(F32), ALU.subtract).then_inc(s_hid, 1)
                pool.wait_ge(s_row, e * 2 + 3)
                pool.tensor_tensor(step[:], one, one, ALU.mult)
                pool.indirect_dma_start(g["X"], bass.IndirectOffsetOnAxis(ap=cur_s[:, 0:1], axis=0), ys[:], None,
                                        compute_op=ALU.add).then_inc(s_sc, 16)
                pool.indirect_dma_start(g["X"], bass.IndirectOffsetOnAxis(ap=cur_p[:, 0:1], axis=0), yp[:], None,
                                        compute_op=ALU.add).then_inc(s_sc, 16)
                pool.wait_ge(s_sc, e * 32 + 32)
            pool.wait_ge(s_xg, NE * 32 + 32)

        @block.scalar
        def _(act):
            act.sem_inc(s_row, 1)

            def x_hi(n):
                for b, (k0, m) in enumerate(XB):
                    act.wait_ge(s_xtr, n * 3 + b + 1)
                    act.activation(xt[:, k0:k0 + m, 0:CAP], xbank(b, m), ACT.Copy).then_inc(s_xhi, 1)

            def y_low(e, d):
                group_done(act, e, d)
                act.wait_ge(s_ye, e * GD + d + 1)
                act.activation(cy[:, d % 2, 0:CAP_S], py[d % 2][:, CAP:CAP + CAP_S], ACT.Identity,
                               scale=g["mod"][:, 40 + d, 0:1])
                act.activation(cy[:, d % 2, CAP_S:CAP], py[d % 2][:, CAP + CAP_S:2 * CAP], ACT.Identity,
                               scale=g["mod"][:, 40 + d, 1:2]).then_inc(s_cy, 1)

            def rows_out(e, h):
                act.wait_ge(s_ix, e + 2)
                act.wait_ge(s_yt, e * GD + 4 * h + 6)
                act.activation(ys[:, h * 512:h * 512 + 512], pr[:], ACT.Identity, scale=gate_s[:])
                act.activation(yp[:, h * 512:h * 512 + 512], pp[:], ACT.Identity, scale=gate_p[:]).then_inc(s_row, 1)

            for c in range(AHEAD_HI):
                st.split_hi(act, 0, 0, c)
            x_hi(0)
            with act.Fori(0, NE) as e:
                for c in range(NC):
                    st.split_hi(act, e * (NC // st.nr), e * NC, c + AHEAD_HI)
                    j = (c - 4) // 2
                    if c % 2 == 0 and 0 <= j < FT:
                        act.wait_ge(s_hd, e * FT + j + 1)
                        act.activation(hid[:, j, 0:CAP], hd[:, j % 2], ACT.Copy).then_inc(s_hh, 1)
                    j = (c - 3) // 2
                    if c % 2 == 1 and 0 <= j < FT:
                        act.wait_ge(s_add, e * FT + j + 3)
                        act.activation(sl[:, j % 2], s13[:, j % 2, 0], ACT.Silu).then_inc(s_sl, 1)
                    j = (c - 2) // 2
                    if c % 2 == 0 and 0 <= j < FT:
                        act.wait_ge(st.used, e * NC + 2 * j + 2 + st.ns)
                        act.wait_ge(s_add, e * FT + j + 1)
                        act.activation(cpy[:, j % 2], ps[:, 2 * (j % 2):2 * (j % 2) + 2, CAP:2 * CAP], ACT.Copy).then_inc(s_cp, 1)
                    for d in range(GD):
                        if c == end[d] + 1:
                            y_low(e, d)
                    if c == end[4] + 2:
                        rows_out(e, 0)
                    if c == end[6] + 1:
                        x_hi(e + 1)
                y_low(e, GD - 1)
                rows_out(e, 1)

        @block.vector
        def _(dve):
            st.start_dve(dve)
            dve.sem_inc(s_add, 2)
            dve.sem_inc(s_ye, 2)

            def x_lo(n):
                for b, (k0, m) in enumerate(XB):
                    dve.wait_ge(s_xhi, n * 3 + b + 1)
                    dve.tensor_tensor(xt[:, k0:k0 + m, CAP:2 * CAP], xbank(b, m), xt[:, k0:k0 + m, 0:CAP].bitcast(F32),
                                      ALU.subtract).then_inc(s_xlo, 1)

            def y_gate(e, d):
                dve.wait_ge(s_cy, e * GD + d + 1)
                dve.wait_ge(s_yt, e * GD + d + 1)
                dve.scalar_tensor_tensor(ye[:, d % 2, 0:CAP_S], py[d % 2][:, 0:CAP_S], g["mod"][:, 40 + d, 0:1],
                                         cy[:, d % 2, 0:CAP_S], ALU.mult, ALU.add)
                dve.scalar_tensor_tensor(ye[:, d % 2, CAP_S:CAP], py[d % 2][:, CAP_S:CAP], g["mod"][:, 40 + d, 1:2],
                                         cy[:, d % 2, CAP_S:CAP], ALU.mult, ALU.add).then_inc(s_ye, 1)

            choice.on_vector(dve)
            for c in range(AHEAD_LO):
                st.split_lo(dve, 0, c)
            x_lo(0)
            with dve.Fori(0, NE) as e:
                for c in range(NC):
                    st.split_lo(dve, e * NC, c + AHEAD_LO)
                    j = (c - 2) // 2
                    if c % 2 == 0 and 0 <= j < FT:
                        dve.wait_ge(s_cp, e * FT + j + 1)
                        if j >= 2:
                            dve.wait_ge(s_hd, e * FT + j - 1)
                        dve.tensor_tensor(s13[:, j % 2], ps[:, 2 * (j % 2):2 * (j % 2) + 2, 0:CAP], cpy[:, j % 2],
                                          ALU.add).then_inc(s_add, 1)
                    for d in range(GD):
                        if c == end[d] + 1:
                            y_gate(e, d)
                    if c == end[6] + 1:
                        x_lo(e + 1)
                y_gate(e, GD - 1)

        @block.tensor
        def _(pe):
            st.start_pe(pe)
            pe.sem_inc(s_yt, 2)

            def x_transposes(n):
                pe.wait_ge(s_xg, n * 32 + 32)
                for b, (k0, m) in enumerate(XB):
                    for k in range(m):
                        cols = slice((k0 + k) * 128, (k0 + k + 1) * 128)
                        pe.transpose(ps[:, b, k * CAP:k * CAP + CAP_S], xg[:, cols], g["ident"][:])
                        tr = pe.transpose(ps[:, b, k * CAP + CAP_S:(k + 1) * CAP], xp[:, cols], g["ident"][0:CAP_P, 0:CAP_P])
                    tr.then_inc(s_xtr, 1)

            def y_transposes(e, d):
                pe.wait_ge(s_ye, e * GD + d + 3)
                if d % 4 == 0:
                    pe.wait_ge(s_row, e * 2 + d // 4 + 1)
                cols = slice((d % 4) * 128, (d % 4) * 128 + 128)
                pe.transpose(pr[:, cols], ye[:, d % 2, 0:CAP_S], g["ident"][:])
                pe.transpose(pp[:, cols], ye[:, d % 2, CAP_S:CAP], g["ident"][:]).then_inc(s_yt, 1)

            def product(out, c, t, rhs, first, last):
                wh, wl = st.tile(st.hi, c, t), st.tile(st.lo, c, t)
                if last:
                    pe.matmul(out[:, 0:CAP], wl, rhs[:, 0:CAP], start=False, stop=False)
                mm = pe.matmul(out[:, 0:2 * CAP], wh, rhs, start=first, stop=last)
                if not last:
                    mm = pe.matmul(out[:, 0:CAP], wl, rhs[:, 0:CAP], start=False, stop=False)
                return mm

            choice.on_tensor(pe)
            x_transposes(0)
            with pe.Fori(0, NE) as e:
                pe.wait_ge(s_xlo, e * 3 + 3)
                for c in range(CW):
                    j = c // 2
                    st.ready(pe, e * NC, c)
                    if c % 2 == 0:
                        pe.wait_ge(s_add, e * FT + j + 1)
                    for k in range(KT):
                        mm = product(ps[:, 2 * (j % 2) + c % 2, :], c, k, xt[:, k, :], k == 0, k == KT - 1)
                    mm.then_inc(st.used, 1)
                for n in range(GD * FT):
                    c, t, d, f = CW + n // 8, n % 8, n // FT, n % FT
                    if t == 0:
                        st.ready(pe, e * NC, c)
                    if f == 0:
                        pe.wait_ge(s_ye, e * GD + d + 1)
                    if d == 0:
                        pe.wait_ge(s_hid, e * FT + f + 1)
                    mm = product(py[d % 2], c, t, hid[:, f, :], f == 0, f == FT - 1)
                    if t == 7:
                        mm.then_inc(st.used, 1)
                    elif f == FT - 1:
                        mm.then_inc(s_g, 1)
                    if f == FT - 1:
                        if d:
                            y_transposes(e, d - 1)
                        if d == 6:
                            x_transposes(e + 1)
                y_transposes(e, GD - 1)


def final_norm(nc, a, g):
    NB = 5
    with Phase(nc, "fin") as ph:
        x = ph.sb("x", [128, NTT, D])
        gain = ph.sb("gain", [128, D])
        junk = ph.sb("junk", [128, D])
        ss, rr, r2, root = (ph.sb(n, [128, NTT]) for n in ("ss", "rr", "r2", "root"))
        s_g, s_x = ph.sem("gain_landed"), [ph.sem(f"x_landed{t}") for t in range(NTT)]
        s_ss, s_root, s_dve, s_y, s_out = ph.sem("squares"), ph.sem("root"), ph.sem("dve_steps"), ph.sem("y"), ph.sem("stored")
        block = ph.block()

        @block.sync
        def _(sp):
            for t in range(NTT):
                sp.dma_start(x[:, t, :], g["X"][t * 128:(t + 1) * 128, :]).then_inc(s_x[t], 16)
            sp.dma_start(gain[:], a["final_g"].to_broadcast([128, D])).then_inc(s_g, 16)
            for t in range(NTT):
                sp.wait_ge(s_y, t + 1)
                sp.dma_start(a["y"][t * 128:(t + 1) * 128, :], x[:, t, :]).then_inc(s_out, 16)
            sp.wait_ge(s_out, 16 * NTT)

        @block.scalar
        def _(act):
            for t in range(NTT):
                act.wait_ge(s_x[t], 16)
                if t:
                    act.wait_ge(s_ss, t)
                act.activation(junk[:], x[:, t, :], ACT.Square, accum_out=ss[:, t:t + 1]).then_inc(s_ss, 1)
                if (t + 1) % NB == 0:
                    q = t // NB
                    act.wait_ge(s_root, 2 * q + 1)
                    act.activation(root[:, q * NB:(q + 1) * NB], r2[:, q * NB:(q + 1) * NB], ACT.Sqrt).then_inc(s_root, 1)

        @block.vector
        def _(dve):
            chain = Chain(dve, s_dve)
            dve.wait_ge(s_g, 16)
            for q in range(NTT // NB):
                c = slice(q * NB, (q + 1) * NB)
                dve.wait_ge(s_ss, (q + 1) * NB)
                chain(dve.tensor_scalar(rr[:, c], ss[:, c], 1.0 / D, EPS, ALU.mult, ALU.add))
                dve.reciprocal(r2[:, c], rr[:, c]).then_inc(s_root, 1)
                dve.wait_ge(s_root, 2 * q + 2)
                chain(dve.tensor_tensor(r2[:, c], root[:, c], root[:, c], ALU.mult))
                chain(dve.tensor_tensor(r2[:, c], r2[:, c], rr[:, c], ALU.mult))
                chain(dve.tensor_scalar(r2[:, c], r2[:, c], -0.5, 1.5, ALU.mult, ALU.add))
                chain(dve.tensor_tensor(rr[:, c], root[:, c], r2[:, c], ALU.mult))
                for t in range(q * NB, (q + 1) * NB):
                    dve.scalar_tensor_tensor(x[:, t, :], x[:, t, :], rr[:, t:t + 1], gain[:], ALU.mult, ALU.mult).then_inc(s_y, 1)


def arrange(i):
    c = np.ascontiguousarray

    def cols(v):
        return v.reshape(-1, 128).T

    o = {}
    o["x"] = c(np.concatenate([i["x_prompt"][0], i["x_sample"][0]], 0))
    o["cond"] = c(np.stack([i["c"][0], i["c_ctx"]], 0).reshape(2, KT, 128).transpose(2, 1, 0))
    o["bada"] = c(cols(i["b_ada"][0]))
    o["gains"] = c(np.concatenate([cols(i["norm1_g"][0]), cols(i["norm2_g"][0]), cols(i["out_g_attn"][0]),
                                   cols(i["out_g_hyena"][0]), np.zeros((128, 8), np.float32)], 1))
    o["ident"] = np.eye(128, dtype=np.float32)
    o["w_ada"] = c(i["w_ada"][0].reshape(KT, 128, 24, 256).transpose(2, 1, 0, 3).reshape(24, 128, KT * 256))
    w = i["w_in"][0]
    wf = np.concatenate([w[:, 0:2 * DA], w[:, 3 * DA:]], 1)
    wf = wf.reshape(KT, 128, NF, 128).transpose(2, 1, 0, 3).reshape(NF, 128, CH)
    wv = w[:, 2 * DA:3 * DA].reshape(4, 2, 128, 512).transpose(0, 2, 1, 3).reshape(4, 128, CH)
    o["w_in"] = np.concatenate([wf, wv], 0)
    o["cache_kT"] = c(i["cache_k"][0, 0].transpose(0, 2, 1).reshape(DA, NCTX))
    o["cache_v"] = c(i["cache_v"][0, 0].reshape(NH, 2, 128, HD).transpose(2, 1, 0, 3).reshape(128, 2, DA))
    o["bias"] = relative_bias(i["rpb"][0])
    o["w_out"] = c(i["w_out"][0].reshape(KT, 128, D))
    o["w_router"] = c(i["w_router"][0].reshape(KT, 128, NE).transpose(1, 0, 2))
    o["w13"] = np.stack([i[n][0].reshape(NE, KT, 128, FT, 128).transpose(0, 3, 2, 1, 4).reshape(NE, FT, 128, CH)
                         for n in ("w1", "w3")], 2).reshape(NE * 2 * FT, 128, CH)
    o["w2"] = c(i["w2"][0].reshape(NE, FT, 128, KT, 128).transpose(0, 3, 1, 2, 4).reshape(NE, FT, 8, 128, 128)
                .transpose(0, 1, 3, 2, 4).reshape(NE * FT, 128, CH))
    o["final_g"] = c(i["final_g"][None])
    for s, L in (("p", TP), ("s", TS)):
        o |= filter_constants(s, L)
        o |= convolution_constants(s, L)
    f0 = lambda n: i[n][0]
    o["filt_w1"], o["filt_w2"], o["filt_w3"] = c(f0("filt_w1")), c(f0("filt_w2")), c(f0("filt_w3"))
    o["filt_b"] = c(np.stack([f0("filt_b1"), f0("filt_b2"), f0("filt_freq")], 1))
    o["hyena_bias"] = c(f0("hyena_bias"))
    o["conv"] = c(np.stack([cols(f0("conv_w")[x]) for x in range(3)] + [cols(f0("conv_b"))], 2))
    o["sgn"] = np.where(np.arange(128) % 2, -1.0, 1.0).astype(np.float32)[None]
    return o


def filter_constants(s, L):
    M, MT, bands = L // 2, L // 256, 16
    f32 = np.float32
    pos = np.concatenate([np.arange(M), L - np.arange(M), [M, M]]) % L
    t = np.linspace(0.0, 1.0, L, dtype=f32)[pos]
    w = (f32(2.0 * np.pi / L) * np.arange(L, dtype=f32))[pos]
    b = np.linspace(1e-4, bands - 1, bands, dtype=f32)
    ph = b[None, :] * w[:, None]
    z = np.concatenate([t[:, None], np.cos(ph), -np.sin(ph)], 1).T
    deltas = np.abs(np.linspace(np.log(1e-2) / 1.5, np.log(1e-2) / 0.3, DH, dtype=f32))
    win = np.exp(-t[:, None] * deltas) + f32(0.05)
    win[M] = 0.0
    wd = np.stack([win[:M].reshape(MT, 128, DH), win[M:2 * M].reshape(MT, 128, DH)], 2)
    x = np.arange(M)[:, None].astype(np.float64)
    tiles = []
    for kind, par, f in filter_jobs(MT):
        fr = 2.0 * (f * 128 + np.arange(128)) + par
        if kind == "cosx":
            fr[0] = L
        th = np.pi * fr[None, :] * x / L
        v = (np.sin(th) if kind == "sin" else np.cos(th)).reshape(MT, 128, 128)
        tiles += list(v)
    n = -(-len(tiles) // 8)
    tiles += [np.zeros((128, 128))] * (n * 8 - len(tiles))
    kb = np.stack(tiles).reshape(n, 8, 128, 128).transpose(0, 2, 1, 3).reshape(n, 128, CH)
    rowf = np.full((128, 3), 1.0 / L)
    rowf[0, 0] = 0.5 / L
    c = lambda v: np.ascontiguousarray(v, dtype=f32)
    return {f"z_{s}": c(z), f"win_{s}": c(wd), f"wmid_{s}": c(win[2 * M:2 * M + 1]), f"kbasis_{s}": c(kb), f"rowf_{s}": c(rowf)}


def convolution_constants(s, L):
    M, MT = L // 2, L // 256
    x = np.arange(M)[:, None] + 0.5
    fwd, inv = [], []
    for j in range(2 * MT):
        par, f = divmod(j, MT)
        fr = 2.0 * (f * 128 + np.arange(128)) + par
        for kind in range(2):
            fk = fr.copy()
            if kind == 1 and j == 0:
                fk[0] = L
            th = np.pi * fk[None, :] * x / L
            v = np.sin(th) if kind else np.cos(th)
            fwd += list(v.reshape(MT, 128, 128))
            inv.append(v.T)
    if MT == 4:
        f = np.stack(fwd).reshape(8, 8, 128, 128).transpose(0, 2, 1, 3).reshape(8, 128, CH)
        v = np.stack(inv).reshape(8, 2, 128, M).transpose(0, 2, 1, 3).reshape(8, 128, CH)
        b = np.concatenate([f, v])
    else:
        b = np.stack(fwd + inv).transpose(1, 0, 2).reshape(1, 128, CH)
    return {f"basis_{s}": np.ascontiguousarray(b, dtype=np.float32)}


def relative_bias(rpb):
    qi = np.arange(128)
    ki = np.arange(NWIN)
    out = np.full((NH, 128, 8, NWIN), NEG, np.float32)
    for half in range(2):
        for j in range(4):
            r, col = half * 8 + qi // QC, j * QC + qi % QC
            kr, kc = half * 4 + ki // KC, BLK_START[j] + ki % KC
            rs = np.clip(r - WR // 2, 0, TS // GW - WR)[:, None]
            ws = np.clip(col - WC // 2, 0, GW - WC)[:, None]
            ok = (kr[None] >= rs) & (kr[None] < rs + WR) & (kc[None] >= ws) & (kc[None] < ws + WC)
            dr = np.clip(kr[None] - r[:, None] + WR - 1, 0, 2 * WR - 2)
            dc = np.clip(kc[None] - col[:, None] + WC - 1, 0, 2 * WC - 2)
            t = out[:, :, half * 4 + j, :]
            t[:, ok] = rpb[:, dr[ok], dc[ok]]
    return out.reshape(NH * 128, 8 * NWIN)


def build(nc, a):
    def dram(name, shape):
        return nc.dram_tensor(name, shape, F32, kind="Internal").ap()

    g = {
        "MODR": dram("modulation_rows", [2, 6 * D]), "GMODR": dram("gain_rows", [2, 2 * D]),
        "QKH": dram("features", [NF * 128, T]), "V": dram("values", [T, DA]),
        "Kp": dram("spectrum_p", [2, 2, 3, 128, DH]), "Ks": dram("spectrum_s", [2, 8, 3, 128, DH]),
        "MIXT": dram("mixed", [D, T]), "X": dram("residual", [T, D]), "H2": dram("hidden_rows", [T, D]),
    }
    with ExitStack() as keep:
        for name, shape, dt in (("mod", [128, 48, 2], F32), ("gmod", [128, 2, 16], F32), ("gains", [128, 32], F32),
                                ("ident", [128, 128], F32), ("ones", [128, 128], F32), ("aff", [128, NTT, NE], F32),
                                ("gate_s", [128, NE], F32), ("gate_p", [CAP_P, NE], F32),
                                ("rows_s", [128, NE + 1], U32), ("rows_p", [CAP_P, NE + 1], U32)):
            g[name] = keep.enter_context(nc.sbuf_tensor(f"g_{name}", shape, dt))
        filters(nc, a, g, "p", TP, False)
        filters(nc, a, g, "s", TS, True)
        projection(nc, a, g)
        attention(nc, a, g)
        hyena(nc, a, g, "p", TP, 0)
        hyena(nc, a, g, "s", TS, TP)
        mix_and_route(nc, a, g)
        experts(nc, a, g)
        final_norm(nc, a, g)


def kernel(**inputs):
    import concourse.bacc as bacc
    from concourse.bass_utils import run_bass_kernel_spmd

    arrays = {f"in_{n}": v for n, v in arrange({n: np.asarray(v) for n, v in inputs.items()}).items()}
    outputs = {"y": (T, D), "state_kT": (DA, TP), "state_v": (TP, DA)}
    nc = bacc.Bacc("TRN2", target_bir_lowering=False, num_devices=1)
    a = {n[3:]: nc.dram_tensor(n, v.shape, F32, kind="ExternalInput").ap() for n, v in arrays.items()}
    for n, shape in outputs.items():
        a[n] = nc.dram_tensor(f"out_{n}", shape, F32, kind="ExternalOutput").ap()
    build(nc, a)
    res = run_bass_kernel_spmd(nc, [arrays], core_ids=[0]).results[0]
    y = res["out_y"]
    state_k = res["out_state_kT"].reshape(1, 1, NH, HD, TP).transpose(0, 1, 2, 4, 3)
    state_v = res["out_state_v"].reshape(1, 1, TP, NH, HD).transpose(0, 1, 3, 2, 4)
    return y[None, :TP], y[None, TP:], np.ascontiguousarray(state_k), np.ascontiguousarray(state_v)
```
